# Optimizing a Trainium2 kernel written in Bass

```python
import math
import jax, jax.numpy as jnp
from jax import lax
import numpy as np

D_MODEL = 1024
BATCH = 1
SEQ = 512
DEPTH = 1

N_Q_HEADS = 8
N_KV_HEADS = 2
GROUP = N_Q_HEADS // N_KV_HEADS
HEAD_DIM = 64
ROT_DIM = HEAD_DIM // 4
ROPE_THETA = 500000.0
WINDOW = 128
ATTN_BLOCK = 128
ATTN_WIDTH = N_Q_HEADS * HEAD_DIM
KV_WIDTH = N_KV_HEADS * HEAD_DIM

HGRN_HEADS = 4
HGRN_KEY_DIM = 128
HGRN_VAL_DIM = 128
HGRN_KEY_WIDTH = HGRN_HEADS * HGRN_KEY_DIM
HGRN_WIDTH = HGRN_HEADS * HGRN_VAL_DIM
HGRN_CHUNK = 64

IN_SIZES = (ATTN_WIDTH, KV_WIDTH, KV_WIDTH,
            HGRN_KEY_WIDTH, HGRN_KEY_WIDTH, HGRN_WIDTH, HGRN_WIDTH,
            D_MODEL, D_MODEL)
IN_WIDTH = sum(IN_SIZES)

N_GROUPS = 4
EXPERTS_PER_GROUP = 8
N_EXPERTS = N_GROUPS * EXPERTS_PER_GROUP
TOP_K = 2
EXPERT_FF = 512
MOE_BLOCK = 128

NORM_EPS = 1e-6


def rms_norm(x, w):
    xf = x.astype(jnp.float32)
    y = xf * lax.rsqrt(jnp.mean(xf * xf, axis=-1, keepdims=True) + NORM_EPS)
    return (y * w.astype(jnp.float32)).astype(x.dtype)

def rope_tables(positions):
    inv_freq = ROPE_THETA ** (-jnp.arange(0, ROT_DIM, 2, dtype=jnp.float32) / ROT_DIM)
    ang = positions.astype(jnp.float32)[..., None] * inv_freq
    return jnp.cos(ang)[:, :, None, :], jnp.sin(ang)[:, :, None, :]

def partial_rope(x, cos, sin):
    half = ROT_DIM // 2
    xf = x.astype(jnp.float32)
    x1, x2 = xf[..., :half], xf[..., half:ROT_DIM]
    out = jnp.concatenate([x1 * cos - x2 * sin, x2 * cos + x1 * sin, xf[..., ROT_DIM:]], axis=-1)
    return out.astype(x.dtype)

def sliding_window_gqa(q, k, v, sinks):
    B, S = q.shape[0], q.shape[1]
    nb = S // ATTN_BLOCK
    qb = q.reshape(B, nb, ATTN_BLOCK, N_KV_HEADS, GROUP, HEAD_DIM).astype(jnp.float32)
    kb = k.reshape(B, nb, ATTN_BLOCK, N_KV_HEADS, HEAD_DIM).astype(jnp.float32)
    vb = v.reshape(B, nb, ATTN_BLOCK, N_KV_HEADS, HEAD_DIM).astype(jnp.float32)
    pad = ((0, 0), (1, 0), (0, 0), (0, 0), (0, 0))
    kk = jnp.concatenate([jnp.pad(kb[:, :-1], pad), kb], axis=2)
    vv = jnp.concatenate([jnp.pad(vb[:, :-1], pad), vb], axis=2)
    s = jnp.einsum('bnqhgd,bnkhd->bnhgqk', qb, kk) * (HEAD_DIM ** -0.5)
    qi = jnp.arange(ATTN_BLOCK)[:, None] + ATTN_BLOCK
    kj = jnp.arange(2 * ATTN_BLOCK)[None, :]
    band = (kj <= qi) & (qi - kj < WINDOW)
    has_prev = (jnp.arange(nb)[:, None, None] > 0) | (kj[None] >= ATTN_BLOCK)
    valid = band[None] & has_prev
    s = jnp.where(valid[None, :, None, None], s, -jnp.inf)
    sink = sinks.astype(jnp.float32).reshape(N_KV_HEADS, GROUP)[None, None, :, :, None, None]
    m = jnp.maximum(jnp.max(s, axis=-1, keepdims=True), sink)
    p = jnp.exp(s - m)
    denom = jnp.sum(p, axis=-1, keepdims=True) + jnp.exp(sink - m)
    o = jnp.einsum('bnhgqk,bnkhd->bnqhgd', p / denom, vv)
    return o.reshape(B, S, ATTN_WIDTH).astype(q.dtype)

def hgrn2_chunkwise(q, k, v, log_f):
    B, S = q.shape[0], q.shape[1]
    nc = S // HGRN_CHUNK

    def to_chunks(t):
        return t.reshape(B, nc, HGRN_CHUNK, HGRN_HEADS, t.shape[-1]).transpose(1, 0, 3, 2, 4)

    causal = jnp.tril(jnp.ones((HGRN_CHUNK, HGRN_CHUNK), dtype=bool))

    def step(state, inp):
        qc, kc, vc, gc = inp
        b = jnp.cumsum(gc, axis=2)
        o_inter = jnp.einsum('bhtk,bhkv->bhtv', qc * jnp.exp(b), state)
        diff = b[:, :, :, None, :] - b[:, :, None, :, :]
        decay = jnp.exp(jnp.where(causal[:, :, None], diff, -jnp.inf))
        a = jnp.einsum('bhtk,bhsk,bhtsk->bhts', qc, kc, decay)
        o_intra = jnp.einsum('bhts,bhsv->bhtv', a, vc)
        b_last = b[:, :, -1:, :]
        state = jnp.exp(b_last[:, :, 0])[..., None] * state + jnp.einsum(
            'bhsk,bhsv->bhkv', kc * jnp.exp(b_last - b), vc)
        return state, o_inter + o_intra

    init = jnp.zeros((B, HGRN_HEADS, HGRN_KEY_DIM, HGRN_VAL_DIM), jnp.float32)
    _, o = lax.scan(step, init, (to_chunks(q), to_chunks(k), to_chunks(v), to_chunks(log_f)))
    return o.transpose(1, 0, 3, 2, 4).reshape(B, S, HGRN_HEADS, HGRN_VAL_DIM)

def hierarchical_moe(xn, w_rg, b_rg, w_re, b_re, w_gate, w_up, w_down):
    T, D = xn.shape
    lg = (xn @ w_rg).astype(jnp.float32) + b_rg.astype(jnp.float32)
    pg = jax.nn.softmax(lg, axis=-1)
    gsel = jnp.argmax(pg, axis=-1)
    pgsel = jnp.take_along_axis(pg, gsel[:, None], axis=1)[:, 0]
    le = ((xn @ w_re).astype(jnp.float32) + b_re.astype(jnp.float32)).reshape(T, N_GROUPS, EXPERTS_PER_GROUP)
    le_sel = jnp.take_along_axis(le, gsel[:, None, None], axis=1)[:, 0]
    pe = jax.nn.softmax(le_sel, axis=-1)
    topv, topi = lax.top_k(pe, TOP_K)
    gate_w = pgsel[:, None] * topv / jnp.sum(topv, axis=-1, keepdims=True)
    eid = gsel[:, None] * EXPERTS_PER_GROUP + topi

    TK = T * TOP_K
    flat_e = eid.reshape(-1).astype(jnp.int32)
    flat_tok = jnp.repeat(jnp.arange(T, dtype=jnp.int32), TOP_K)
    flat_w = gate_w.reshape(-1)
    order = jnp.argsort(flat_e)
    se = flat_e[order]
    counts = jnp.bincount(flat_e, length=N_EXPERTS)
    starts = jnp.cumsum(counts) - counts
    padded = ((counts + MOE_BLOCK - 1) // MOE_BLOCK) * MOE_BLOCK
    pends = jnp.cumsum(padded)
    pstarts = pends - padded
    dest = pstarts[se] + jnp.arange(TK, dtype=jnp.int32) - starts[se]
    P = TK + N_EXPERTS * MOE_BLOCK
    P = ((P + MOE_BLOCK - 1) // MOE_BLOCK) * MOE_BLOCK
    nblk = P // MOE_BLOCK
    row_tok = jnp.full((P,), T, jnp.int32).at[dest].set(flat_tok[order])
    row_w = jnp.zeros((P,), jnp.float32).at[dest].set(flat_w[order])
    blk_e = jnp.minimum(jnp.searchsorted(pends, jnp.arange(nblk, dtype=jnp.int32) * MOE_BLOCK, side='right'),
                        N_EXPERTS - 1)
    x_pad = jnp.concatenate([xn, jnp.zeros((1, D), xn.dtype)], axis=0)
    x_blocks = x_pad[row_tok].reshape(nblk, MOE_BLOCK, D)

    def expert_block(args):
        xb, e = args
        h = jax.nn.silu(xb @ w_gate[e]) * (xb @ w_up[e])
        return h @ w_down[e]

    y_blocks = lax.map(expert_block, (x_blocks, blk_e))
    y_rows = y_blocks.reshape(P, D) * row_w[:, None].astype(y_blocks.dtype)
    return jax.ops.segment_sum(y_rows, row_tok, num_segments=T + 1)[:T]

def first_inputs(seed: int = 0) -> dict:
    key = jax.random.key(seed)
    ks = jax.random.split(key, 24)
    f32 = jnp.float32
    nrm = lambda k, shape, scale: jax.random.normal(k, shape, f32) * scale
    x = jax.random.normal(ks[0], (BATCH, SEQ, D_MODEL), f32)
    offs = jax.random.randint(ks[1], (BATCH, 1), 0, 4096, dtype=jnp.int32)
    positions = offs + jnp.arange(SEQ, dtype=jnp.int32)[None, :]
    return {
        "x": x,
        "positions": positions,
        "norm1_w": 1.0 + nrm(ks[2], (DEPTH, D_MODEL), 0.02),
        "w_in": nrm(ks[3], (DEPTH, D_MODEL, IN_WIDTH), D_MODEL ** -0.5),
        "q_norm_w": 1.0 + nrm(ks[4], (DEPTH, HEAD_DIM), 0.02),
        "k_norm_w": 1.0 + nrm(ks[5], (DEPTH, HEAD_DIM), 0.02),
        "attn_sinks": nrm(ks[6], (DEPTH, N_Q_HEADS), 0.5),
        "hgrn_lower_bounds": nrm(ks[7], (DEPTH + 1, HGRN_KEY_WIDTH), 0.5),
        "hgrn_norm_w": 1.0 + nrm(ks[8], (DEPTH, HGRN_VAL_DIM), 0.02),
        "w_branch_attn": nrm(ks[9], (DEPTH, ATTN_WIDTH, D_MODEL), ATTN_WIDTH ** -0.5),
        "w_branch_hgrn": nrm(ks[10], (DEPTH, HGRN_WIDTH, D_MODEL), HGRN_WIDTH ** -0.5),
        "w_out": nrm(ks[11], (DEPTH, D_MODEL, D_MODEL), D_MODEL ** -0.5),
        "norm2_w": 1.0 + nrm(ks[12], (DEPTH, D_MODEL), 0.02),
        "w_router_group": nrm(ks[13], (DEPTH, D_MODEL, N_GROUPS), D_MODEL ** -0.5),
        "b_router_group": nrm(ks[14], (DEPTH, N_GROUPS), 0.01),
        "w_router_expert": nrm(ks[15], (DEPTH, D_MODEL, N_EXPERTS), D_MODEL ** -0.5),
        "b_router_expert": nrm(ks[16], (DEPTH, N_EXPERTS), 0.01),
        "w_gate_experts": nrm(ks[17], (DEPTH, N_EXPERTS, D_MODEL, EXPERT_FF), D_MODEL ** -0.5),
        "w_up_experts": nrm(ks[18], (DEPTH, N_EXPERTS, D_MODEL, EXPERT_FF), D_MODEL ** -0.5),
        "w_down_experts": nrm(ks[19], (DEPTH, N_EXPERTS, EXPERT_FF, D_MODEL), EXPERT_FF ** -0.5),
    }

def first_block(x, positions, norm1_w, w_in, q_norm_w, k_norm_w, attn_sinks, hgrn_lower_bounds,
              hgrn_norm_w, w_branch_attn, w_branch_hgrn, w_out, norm2_w, w_router_group,
              b_router_group, w_router_expert, b_router_expert, w_gate_experts, w_up_experts,
              w_down_experts):
    B, S, D = x.shape
    cos, sin = rope_tables(positions)
    split_points = [int(v) for v in np.cumsum(IN_SIZES)[:-1]]
    lower_bounds = jnp.cumsum(jax.nn.softmax(hgrn_lower_bounds.astype(jnp.float32), axis=0), axis=0)
    for l in range(DEPTH):
        xn = rms_norm(x, norm1_w[l])
        proj = xn @ w_in[l]
        q_a, k_a, v_a, q_h, f_h, i_h, g_h, z_a, z_b = jnp.split(proj, split_points, axis=-1)

        q_a = partial_rope(rms_norm(q_a.reshape(B, S, N_Q_HEADS, HEAD_DIM), q_norm_w[l]), cos, sin)
        k_a = partial_rope(rms_norm(k_a.reshape(B, S, N_KV_HEADS, HEAD_DIM), k_norm_w[l]), cos, sin)
        v_a = v_a.reshape(B, S, N_KV_HEADS, HEAD_DIM)
        attn = sliding_window_gqa(q_a, k_a, v_a, attn_sinks[l])

        lb = lower_bounds[l]
        fg = lb + (1.0 - lb) * jax.nn.sigmoid(f_h.astype(jnp.float32))
        hq = jax.nn.silu(q_h.astype(jnp.float32)).reshape(B, S, HGRN_HEADS, HGRN_KEY_DIM)
        hk = (1.0 - fg).reshape(B, S, HGRN_HEADS, HGRN_KEY_DIM)
        hlogf = jnp.log(fg).reshape(B, S, HGRN_HEADS, HGRN_KEY_DIM)
        hv = i_h.astype(jnp.float32).reshape(B, S, HGRN_HEADS, HGRN_VAL_DIM)
        ho = rms_norm(hgrn2_chunkwise(hq, hk, hv, hlogf), hgrn_norm_w[l]).reshape(B, S, HGRN_WIDTH)
        hgrn = (ho * jax.nn.silu(g_h.astype(jnp.float32))).astype(x.dtype)

        mixed = (jax.nn.sigmoid(z_a) * (attn @ w_branch_attn[l])
                 + jax.nn.sigmoid(z_b) * (hgrn @ w_branch_hgrn[l]))
        x = x + mixed @ w_out[l]

        hn = rms_norm(x, norm2_w[l]).reshape(B * S, D)
        moe = hierarchical_moe(hn, w_router_group[l], b_router_group[l], w_router_expert[l],
                               b_router_expert[l], w_gate_experts[l], w_up_experts[l], w_down_experts[l])
        x = x + moe.reshape(B, S, D).astype(x.dtype)
    return x


CHUNK = 64
N_LEFT_CHUNKS = 8
BAND = (N_LEFT_CHUNKS + 1) * CHUNK
D_MIX = D_MODEL
D_ATTN = D_MIX // 2
N_HEADS = D_ATTN // HEAD_DIM
D_POOL = D_MIX - D_ATTN
POOL_WINDOWS = (2, 4, 8, 16)
N_POOL_GROUPS = len(POOL_WINDOWS)
POOL_GROUP_DIM = D_POOL // N_POOL_GROUPS
REL_CLIP = 128
N_REL = 2 * REL_CLIP + 1
D_FF = 2816
D_IN = 3 * D_ATTN + D_POOL
EPS = 1e-6
NEG_INF = -1e30


def rmsnorm(x, g):
    xf = x.astype(jnp.float32)
    y = xf * lax.rsqrt(jnp.mean(xf * xf, axis=-1, keepdims=True) + EPS)
    return (y * g.astype(jnp.float32)).astype(x.dtype)

def swiglu_ffn(x, w_gate, w_up, w_down):
    return (jax.nn.silu(x @ w_gate) * (x @ w_up)) @ w_down

def multiscale_pool(u, pool_w, pool_scale):
    B, S, _ = u.shape
    uf = u.astype(jnp.float32)
    cs = jnp.cumsum(uf, axis=1)
    cs = jnp.concatenate([jnp.zeros_like(cs[:, :1]), cs], axis=1)
    t = jnp.arange(S)
    outs = []
    for g, w in enumerate(POOL_WINDOWS):
        lo, hi = g * POOL_GROUP_DIM, (g + 1) * POOL_GROUP_DIM
        c = cs[:, :, lo:hi]
        start = jnp.maximum(t + 1 - w, 0)
        win_sum = c[:, 1:] - c[:, start]
        count = (t + 1 - start).astype(jnp.float32)
        outs.append(win_sum / count[None, :, None] - uf[:, :, lo:hi])
    d = jnp.stack(outs, axis=2)
    y = jnp.einsum('bsgc,gcd->bsgd', d, pool_w.astype(jnp.float32)).reshape(B, S, D_POOL)
    return (y * pool_scale.astype(jnp.float32)).astype(u.dtype)

def chunked_attention(q, k, v, q_gain, k_gain, rel_bias):
    B, S, _ = q.shape
    nc = S // CHUNK
    q = rmsnorm(q.reshape(B, S, N_HEADS, HEAD_DIM), q_gain)
    k = rmsnorm(k.reshape(B, S, N_HEADS, HEAD_DIM), k_gain)
    v = v.reshape(B, S, N_HEADS, HEAD_DIM)
    pad = N_LEFT_CHUNKS * CHUNK
    kp = jnp.pad(k, ((0, 0), (pad, 0), (0, 0), (0, 0)))
    vp = jnp.pad(v, ((0, 0), (pad, 0), (0, 0), (0, 0)))
    qc = q.reshape(B, nc, CHUNK, N_HEADS, HEAD_DIM)
    qpos = jnp.arange(CHUNK)[:, None] + pad
    kpos = jnp.arange(BAND)[None, :]
    rel_idx = jnp.clip(qpos - kpos, -REL_CLIP, REL_CLIP) + REL_CLIP
    bias = rel_bias.astype(jnp.float32)[:, rel_idx]
    scale = HEAD_DIM ** -0.5

    def one_chunk(c):
        qb = lax.dynamic_index_in_dim(qc, c, axis=1, keepdims=False)
        kb = lax.dynamic_slice_in_dim(kp, c * CHUNK, BAND, axis=1)
        vb = lax.dynamic_slice_in_dim(vp, c * CHUNK, BAND, axis=1)
        s = jnp.einsum('bqhd,bkhd->bhqk', qb, kb).astype(jnp.float32) * scale + bias
        valid = (c * CHUNK + kpos - pad) >= 0
        s = jnp.where(valid[None, None], s, NEG_INF)
        p = jax.nn.softmax(s, axis=-1)
        return jnp.einsum('bhqk,bkhd->bqhd', p.astype(vb.dtype), vb)

    o = lax.map(one_chunk, jnp.arange(nc))
    return o.transpose(1, 0, 2, 3, 4).reshape(B, S, D_ATTN)

def hybrid_mixer(h, w_in, q_gain, k_gain, rel_bias, pool_w, pool_scale, w_out):
    proj = h @ w_in
    q = proj[..., :D_ATTN]
    k = proj[..., D_ATTN:2 * D_ATTN]
    v = proj[..., 2 * D_ATTN:3 * D_ATTN]
    u = proj[..., 3 * D_ATTN:]
    a = chunked_attention(q, k, v, q_gain, k_gain, rel_bias)
    p = multiscale_pool(u, pool_w, pool_scale)
    return jnp.concatenate([a, p], axis=-1) @ w_out

def second_inputs(seed: int = 0) -> dict:
    key = jax.random.key(seed)
    ks = jax.random.split(key, 20)
    f32 = jnp.float32
    L = DEPTH

    def nrm(k, shape, fan_in):
        return jax.random.normal(k, shape, f32) * fan_in ** -0.5

    def gain(k, shape):
        return 1.0 + 0.1 * jax.random.normal(k, shape, f32)

    return {
        "x": jax.random.normal(ks[0], (BATCH, SEQ, D_MODEL), f32),
        "ffn1_norm": gain(ks[1], (L, D_MODEL)),
        "ffn1_w_gate": nrm(ks[2], (L, D_MODEL, D_FF), D_MODEL),
        "ffn1_w_up": nrm(ks[3], (L, D_MODEL, D_FF), D_MODEL),
        "ffn1_w_down": nrm(ks[4], (L, D_FF, D_MODEL), D_FF),
        "mix_norm": gain(ks[5], (L, D_MODEL)),
        "w_in": nrm(ks[6], (L, D_MODEL, D_IN), D_MODEL),
        "q_norm": gain(ks[7], (L, HEAD_DIM)),
        "k_norm": gain(ks[8], (L, HEAD_DIM)),
        "rel_bias": 0.5 * jax.random.normal(ks[9], (L, N_HEADS, N_REL), f32),
        "pool_w": nrm(ks[10], (L, N_POOL_GROUPS, POOL_GROUP_DIM, POOL_GROUP_DIM), POOL_GROUP_DIM),
        "pool_scale": gain(ks[11], (L, D_POOL)),
        "w_out": nrm(ks[12], (L, D_MIX, D_MODEL), D_MIX),
        "ffn2_norm": gain(ks[13], (L, D_MODEL)),
        "ffn2_w_gate": nrm(ks[14], (L, D_MODEL, D_FF), D_MODEL),
        "ffn2_w_up": nrm(ks[15], (L, D_MODEL, D_FF), D_MODEL),
        "ffn2_w_down": nrm(ks[16], (L, D_FF, D_MODEL), D_FF),
        "final_norm": gain(ks[17], (L, D_MODEL)),
    }

def second_block(x, ffn1_norm, ffn1_w_gate, ffn1_w_up, ffn1_w_down, mix_norm, w_in,
              q_norm, k_norm, rel_bias, pool_w, pool_scale, w_out,
              ffn2_norm, ffn2_w_gate, ffn2_w_up, ffn2_w_down, final_norm):
    for l in range(DEPTH):
        x = x + 0.5 * swiglu_ffn(rmsnorm(x, ffn1_norm[l]), ffn1_w_gate[l], ffn1_w_up[l], ffn1_w_down[l])
        x = x + hybrid_mixer(rmsnorm(x, mix_norm[l]), w_in[l], q_norm[l], k_norm[l], rel_bias[l],
                             pool_w[l], pool_scale[l], w_out[l])
        x = x + 0.5 * swiglu_ffn(rmsnorm(x, ffn2_norm[l]), ffn2_w_gate[l], ffn2_w_up[l], ffn2_w_down[l])
        x = rmsnorm(x, final_norm[l])
    return x


def setup_inputs(seed=0):
    out = dict(first_inputs(seed))
    for name, value in second_inputs(seed + 1).items():
        if name != "x":
            out[name + "_2"] = value
    return out


def reference(
    x, positions, norm1_w, w_in, q_norm_w, k_norm_w, attn_sinks, hgrn_lower_bounds, hgrn_norm_w,
    w_branch_attn, w_branch_hgrn, w_out, norm2_w, w_router_group, b_router_group,
    w_router_expert, b_router_expert, w_gate_experts, w_up_experts, w_down_experts, ffn1_norm_2,
    ffn1_w_gate_2, ffn1_w_up_2, ffn1_w_down_2, mix_norm_2, w_in_2, q_norm_2, k_norm_2,
    rel_bias_2, pool_w_2, pool_scale_2, w_out_2, ffn2_norm_2, ffn2_w_gate_2, ffn2_w_up_2,
    ffn2_w_down_2, final_norm_2,
):
    x = first_block(
        x, positions, norm1_w, w_in, q_norm_w, k_norm_w, attn_sinks, hgrn_lower_bounds,
        hgrn_norm_w, w_branch_attn, w_branch_hgrn, w_out, norm2_w, w_router_group,
        b_router_group, w_router_expert, b_router_expert, w_gate_experts, w_up_experts,
        w_down_experts,
    )
    return second_block(
        x, ffn1_norm_2, ffn1_w_gate_2, ffn1_w_up_2, ffn1_w_down_2, mix_norm_2, w_in_2, q_norm_2,
        k_norm_2, rel_bias_2, pool_w_2, pool_scale_2, w_out_2, ffn2_norm_2, ffn2_w_gate_2,
        ffn2_w_up_2, ffn2_w_down_2, final_norm_2,
    )


_drawn_inputs = setup_inputs


def setup_inputs(seed=0):
    import zlib

    import numpy as np

    out = dict(_drawn_inputs(seed))
    spreads = {}
    factors = {'q_norm_w': 4.597,
     'k_norm_w': 7.335,
     'attn_sinks': 63.709,
     'hgrn_norm_w': 2.784,
     'b_router_group': 3.224,
     'q_norm_2': 7.971,
     'k_norm_2': 7.968}
    for name, (base, spread) in spreads.items():
        noise = np.random.default_rng([zlib.crc32(name.encode()), seed]).standard_normal(out[name].shape)
        drawn = base * np.exp(spread * noise) if base else spread * noise
        out[name] = __import__('jax').numpy.asarray(drawn.astype(out[name].dtype))
    for name, factor in factors.items():
        out[name] = (out[name] * factor).astype(out[name].dtype)
    return out
```

```python
from contextlib import ExitStack

import concourse.bass as bass
from concourse import mybir

ALU = mybir.AluOpType
ACT = mybir.ActivationFunctionType
AX = mybir.AxisListType
F32 = mybir.dt.float32
F32R = mybir.dt.float32r
I32 = mybir.dt.int32
U32 = mybir.dt.uint32

T, D, NB = 512, 1024, 4
EPS = 1e-6
WIN = 64
NE = 32
FF = 512
DFF = 2816
NEG = -1e30

CW = {}
_o = 0
for _n, _w in (("ident", 128), ("ustrict", 128), ("ones", 128), ("fold", 64), ("iota", WIN), ("cmask", 128),
               ("rc16", 64), ("e64", 32), ("step8", 8), ("dec8", 8), ("invf", 8)):
    CW[_n] = (_o, _w)
    _o += _w
NC1 = _o
NC2 = 256 + 512
NMASK = 8 * 128


class Eng:

    def __init__(self, sem):
        self.sem, self.n, self.seen, self.items = sem, 0, {}, []

    def op(self, fn, *deps, inc=True):
        waits = self.waits(deps)
        if inc:
            self.n += 1
        self.items.append(("op", waits, fn, (self.sem, 1) if inc else None))
        return (self.sem, self.n) if inc else None

    def dma(self, fn, slot, *deps):
        waits = self.waits(deps)
        slot[1] += 16
        self.items.append(("op", waits, fn, (slot[0], 16)))
        return (slot[0], slot[1])

    def waits(self, deps):
        out = []
        stack = list(deps)
        need = {}
        while stack:
            d = stack.pop()
            if d is None:
                continue
            if isinstance(d, list):
                stack.extend(d)
                continue
            s, v = d
            if need.get(id(s), (s, 0))[1] < v:
                need[id(s)] = (s, v)
        for k, (s, v) in need.items():
            if self.seen.get(k, 0) < v:
                self.seen[k] = v
                out.append((s, v))
        return out


class Banks:

    def __init__(self):
        self.free = [None] * 8
        self.at = 0

    def take(self, n=1):
        while self.at % n:
            self.at = (self.at + 1) % 8
        b = self.at
        self.at = (self.at + n) % 8
        return b, [self.free[b + i] for i in range(n)]

    def give(self, b, tok, n=1):
        for i in range(n):
            self.free[b + i] = tok


class Stream:

    def __init__(self, g, plan, slots, raw, hi, lo, pool_part):
        self.g, self.plan, self.slots = g, plan, slots
        self.raw, self.hi, self.lo = raw, hi, lo
        self.nr, self.nh = len(raw), len(hi)
        self.loaded = self.split = self.taken = 0
        self.fence = len(plan)
        self.ld, self.sp, self.dn = {}, {}, {}
        self.pool_part = pool_part

    def load_to(self, j):
        while self.loaded < min(j, self.fence):
            u = self.loaded
            _, src, kc, n = self.plan[u]
            r = self.raw[u % self.nr]
            dst = r[:, 0:kc * n].rearrange("p (k n) -> p k n", k=kc)
            self.ld[u] = self.g.sp.dma(lambda e, dst=dst, src=src: e.dma_start(dst, src), self.slots[u % self.nr],
                                       self.sp.get(u - self.nr))
            self.loaded += 1

    def split_to(self, j):
        while self.split < min(j, self.fence):
            u = self.split
            self.load_to(u + 1)
            _, _, kc, n = self.plan[u]
            w = kc * n
            r, h, l = self.raw[u % self.nr], self.hi[u % self.nh], self.lo[u % self.nh]
            t = self.g.act.op(lambda e, h=h, r=r, w=w: e.copy(h[:, 0:w], r[:, 0:w]), self.ld[u], self.dn.get(u - self.nh))
            c = w - int(w * self.pool_part) // 128 * 128
            a = self.g.dve.op(lambda e, h=h, r=r, l=l, c=c: e.tensor_tensor(l[:, 0:c], r[:, 0:c], h[:, 0:c].bitcast(F32),
                                                                                ALU.subtract),
                              t, self.ld[u], self.dn.get(u - self.nh))
            b = None
            if c < w:
                b = self.g.pool.op(lambda e, h=h, r=r, l=l, c=c, w=w: e.tensor_tensor(l[:, c:w], r[:, c:w], h[:, c:w].bitcast(F32),
                                                             ALU.subtract), t, self.ld[u], self.dn.get(u - self.nh))
            self.sp[u] = [t, a, b]
            self.split += 1
            self.load_to(u + 1 + self.nr)

    def take(self, key):
        u = self.taken
        assert self.plan[u][0] == key, (self.plan[u][0], key)
        self.split_to(u + self.nh)
        self.taken += 1
        _, _, kc, n = self.plan[u]
        h = self.hi[u % self.nh][:, 0:kc * n].rearrange("p (k n) -> p k n", k=kc)
        l = self.lo[u % self.nh][:, 0:kc * n].rearrange("p (k n) -> p k n", k=kc)
        return u, h, l, self.sp[u]

    def done(self, u, tok):
        self.dn[u] = tok


def units(key, w, k0, k1, c0, c1):
    out = []
    for k in range(k0, k1, 4):
        e = min(k + 4, k1)
        out.append((key, w[k * 128:e * 128, c0:c1].rearrange("(k p) n -> p k n", p=128), e - k, c1 - c0))
    return out


class G:
    pass


def make_plan_moe(I):
    plan = []

    def gu(e):
        plan.extend(units(("g", e), I["w_gate_experts"][0, e], 0, 8, 0, FF))
        plan.extend(units(("u", e), I["w_up_experts"][0, e], 0, 8, 0, FF))

    def dn(e):
        for c in range(2):
            plan.extend(units(("d", e), I["w_down_experts"][0, e], 0, 4, c * 512, c * 512 + 512))

    gu(0)
    for e in range(NE):
        if e + 1 < NE:
            gu(e + 1)
        dn(e)
    return plan


FCUTS = [(0, 512), (512, 1024), (1024, 1408)]


def make_plan_ffn(I, pre):
    plan = []
    for half in range(2):
        o = half * 1408
        for i, (a, b) in enumerate(FCUTS):
            plan.extend(units((pre, "g", half, i), I[pre + "_w_gate_2"][0], 0, 8, o + a, o + b))
            plan.extend(units((pre, "u", half, i), I[pre + "_w_up_2"][0], 0, 8, o + a, o + b))
        for c in range(2):
            plan.extend(units((pre, "d", half, c), I[pre + "_w_down_2"][0], half * 11, half * 11 + 11,
                              c * 512, c * 512 + 512))
    return plan


INP = [("qa", 0, 512), ("kv", 512, 768), ("qh", 768, 1280), ("fh", 1280, 1792), ("ih", 1792, 2304),
       ("gh", 2304, 2816), ("za0", 2816, 3328), ("za1", 3328, 3840), ("zb0", 3840, 4352), ("zb1", 4352, 4864)]


def make_plan(I):
    p1 = []
    for n, a, b in INP:
        p1.extend(units(n, I["w_in"][0], 0, 8, a, b))
    for c in range(2):
        p1.extend(units(("ba", c), I["w_branch_attn"][0], 0, 4, c * 512, c * 512 + 512))
        p1.extend(units(("bh", c), I["w_branch_hgrn"][0], 0, 4, c * 512, c * 512 + 512))
    for c in range(2):
        p1.extend(units(("wo", c), I["w_out"][0], 0, 8, c * 512, c * 512 + 512))
    p2 = make_plan_moe(I)
    p3 = make_plan_ffn(I, "ffn1")
    for c in range(4):
        p3.extend(units(("in2", c), I["w_in_2"][0], 0, 8, c * 512, c * 512 + 512))
    for c in range(2):
        p3.extend(units(("wo2", c), I["w_out_2"][0], 0, 8, c * 512, c * 512 + 512))
    p3.extend(make_plan_ffn(I, "ffn2"))
    return p1 + p2, p3


def program(nc, I, out):
    ctx = ExitStack()
    g = G()
    base = (nc.sbuf_base + 127) // 128 * 128
    end = nc.sbuf_usable_end
    KB = 1024
    NR, NH = 4, 2
    ring = base
    arena = base + (NR + 2 * NH) * 8 * KB

    def at(name, off, shape, dt=F32):
        n = 4
        for s in shape[1:]:
            n *= s
        o = arena + int(off * KB)
        assert o % 32 == 0 and o + n <= end, (name, off, n, end - arena)
        return nc.alloc_sbuf_tensor_at(name, shape, dt, offset=o)

    with ctx:
        def sem(name):
            return ctx.enter_context(nc.semaphore(name))

        def slot(name):
            return [sem(name), 0]

        PS = ctx.enter_context(nc.psum_tensor("PS", [128, 8, 512], F32))
        raw = [nc.alloc_sbuf_tensor_at(f"raw{i}", [128, 2048], F32, offset=ring + i * 8 * KB) for i in range(NR)]
        hi = [nc.alloc_sbuf_tensor_at(f"hi{i}", [128, 2048], F32R, offset=ring + (NR + i) * 8 * KB) for i in range(NH)]
        lo = [nc.alloc_sbuf_tensor_at(f"lo{i}", [128, 2048], F32R, offset=ring + (NR + NH + i) * 8 * KB)
              for i in range(NH)]

        zsp = nc.dram_tensor("zsp", [16, 128, 512], F32)
        ysp = nc.dram_tensor("ysp", [NE * WIN, D], F32)

        x_sb = at("x_sb", 0, [128, NB, D])
        C1 = at("C1", 16, [128, NC1])
        SM = at("SM", 19.25, [128, 176])

        def cst(n):
            o, w = CW[n]
            return C1[:, o:o + w]

        ident, ones, fold = cst("ident"), cst("ones"), cst("fold")
        n1c, n2c, f1c, mxc, f2c = (SM[:, 8 * i:8 * i + 8] for i in range(5))
        psc = SM[:, 40:44]
        lbr = SM[:, 44:52]
        sink = SM[:, 52:60]
        bfar = SM[:, 60:68]
        lbs = SM[:, 68:92]
        ss4, ms4, sd4, rs4 = (SM[:, 92 + 4 * i:96 + 4 * i] for i in range(4))
        gw = SM[:, 108:116]
        rk = SM[:, 116:124]
        ek = SM[:, 124:132]
        wt = SM[:, 132:140]
        rc1 = SM[:, 140:148]
        rc2 = SM[:, 148:156]
        SI = at("SI", 20.0, [128, 16], U32)
        PI = at("PI", 20.0625, [128, 8], I32)

        s_pe, s_act, s_dve, s_pool, s_sp = (sem("s_" + n) for n in ("pe", "act", "dve", "pool", "sp"))
        g.pe, g.act, g.dve, g.pool, g.sp = Eng(s_pe), Eng(s_act), Eng(s_dve), Eng(s_pool), Eng(s_sp)
        g.banks = Banks()
        engs = ("pe", "act", "dve", "pool", "sp")
        wslots = [slot(f"s_w{i}") for i in range(NR)]
        s_const = slot("s_const")
        s_late = slot("s_late")
        s_xin = slot("s_xin")

        pe = lambda *a, **k: g.pe.op(*a, **k)
        act = lambda *a, **k: g.act.op(*a, **k)
        dve = lambda *a, **k: g.dve.op(*a, **k)
        pool = lambda *a, **k: g.pool.op(*a, **k)

        def mm(o, l, r, st, sp, *deps, inc=False):
            return pe(lambda e: e.matmul(o, l, r, start=st, stop=sp), *deps, inc=inc)

        def tr(o, i, *deps, inc=False):
            return pe(lambda e: e.transpose(o, i, ident), *deps, inc=inc)

        def tt(o, a, b, op, *deps, on=dve):
            return on(lambda e: e.tensor_tensor(o, a, b, op), *deps)

        def ts(o, a, s1, s2, op0, op1, *deps, on=dve):
            if op1 is None:
                return on(lambda e: e.tensor_scalar(o, a, s1, None, op0), *deps)
            return on(lambda e: e.tensor_scalar(o, a, s1, s2, op0, op1), *deps)

        def stt(o, a, s, b, op0, op1, *deps):
            return dve(lambda e: e.scalar_tensor_tensor(out=o, in0=a, scalar=s, in1=b, op0=op0, op1=op1), *deps)

        def af(o, i, f, *deps, scale=1.0, bias=0.0, acc=None):
            if acc is not None:
                return act(lambda e: e.activation(o, i, f, bias=bias, scale=scale, accum_out=acc), *deps)
            return act(lambda e: e.activation(o, i, f, bias=bias, scale=scale), *deps)

        def red(o, i, op, *deps):
            return dve(lambda e: e.tensor_reduce(o, i, AX.X, op), *deps)

        def cp(o, i, *deps):
            return dve(lambda e: e.tensor_copy(o, i), *deps)

        def acp(o, i, *deps):
            return act(lambda e: e.copy(o, i), *deps)

        def rcp(o, i, *deps):
            return dve(lambda e: e.reciprocal(o, i), *deps)

        def bc(a, axis, shape):
            return a.unsqueeze(axis).broadcast_to(shape)

        def hilo(h, l, src, *deps):
            a = acp(h, src, *deps)
            b = tt(l, src, h.bitcast(F32), ALU.subtract, a, *deps)
            return [a, b]

        M1 = at("M1", 21, [128, NC2])
        MK = at("MK", 24, [128, NMASK], U32)
        WQK = at("WQK", 28, [128, 10, 64])
        HNW = at("HNW", 30.5, [128, 128])
        POS = at("POS", 31, [128, 4], I32)

        def cdma(dst, src, s=None):
            return g.sp.dma(lambda e: e.dma_start(dst, src), s or s_const)

        for tb in range(NB):
            cdma(x_sb[:, tb, :], I["x"][0, tb * 128:tb * 128 + 128, :], s_xin)
        t_x = (s_xin[0], s_xin[1])
        cdma(C1[:, :], I["c_f32"])
        cdma(SM[:, 0:68], I["c_par"])
        wplan, wplan3 = make_plan(I)
        st = Stream(g, wplan, wslots, raw, hi, lo, 0.0)
        g.st = st
        st.load_to(NR)
        cdma(M1[:, :], I["c_m1"])
        cdma(MK[:, :], I["c_mask"])
        cdma(POS[:, :], I["positions"])
        cdma(WQK[:, :, :].rearrange("p h d -> p (h d)"), I["qk_norm"].partition_broadcast(128)[:, 0, :])
        cdma(HNW[:, :], I["hgrn_norm_w"].partition_broadcast(128)[:, 0, :])
        t_c = (s_const[0], s_const[1])

        def stats(xs, *deps):
            a = [af(xs[:, tb, :], x_sb[:, tb, :], ACT.Square, *deps, acc=ss4[:, tb:tb + 1]) for tb in range(NB)]
            b = ts(ms4, ss4, 1.0 / D, EPS, ALU.mult, ALU.add, a)
            c = af(sd4, ms4, ACT.Sqrt, b)
            return rcp(rs4, sd4, c), a

        def norm_t(xs, wcol, th, tl, *deps):
            r, a = stats(xs, *deps)
            b = [ts(xs[:, tb, :], x_sb[:, tb, :], rs4[:, tb:tb + 1], None, ALU.mult, None, r, a) for tb in range(NB)]
            toks = []
            for c in range(8):
                bk, fr = g.banks.take()
                for tb in range(NB):
                    t = tr(PS[:, bk, tb * 128:tb * 128 + 128], xs[:, tb, c * 128:c * 128 + 128], b, fr, t_c, inc=tb == 3)
                h = af(th[:, c, :], PS[:, bk, :], ACT.Copy, t, t_c, *deps, scale=wcol[:, c:c + 1])
                l = stt(tl[:, c, :], PS[:, bk, :], wcol[:, c:c + 1], th[:, c, :].bitcast(F32), ALU.mult, ALU.subtract,
                        h, *deps)
                g.banks.give(bk, [h, l])
                toks.append([h, l])
            return toks

        def dense(st, key, nu, orient, xh, xl, xdeps, nbk, evac):
            bk, fr = g.banks.take(4)
            k0 = 0
            for ui in range(nu):
                u, h, l, tok = st.take(key)
                kc = h.shape[1]
                for i in range(nbk):
                    n = h.shape[2] if orient == "a" else 512
                    o = PS[:, bk + i, 0:n]
                    for kk in range(kc):
                        k = k0 + kk
                        s0 = ui == 0 and kk == 0
                        s1 = ui == nu - 1 and kk == kc - 1
                        dp = [tok, fr[i] if s0 else None, xdeps[k]] if ui * 100 + kk >= 0 else []
                        if orient == "a":
                            xa, xb = xh[:, k, i * 128:i * 128 + 128], xl[:, k, i * 128:i * 128 + 128]
                            mm(o, xa, h[:, kk, :], s0, False, dp)
                            mm(o, xa, l[:, kk, :], False, False)
                            t = mm(o, xb, h[:, kk, :], False, s1, inc=kk == kc - 1)
                        else:
                            wh, wl = h[:, kk, i * 128:i * 128 + 128], l[:, kk, i * 128:i * 128 + 128]
                            mm(o, wh, xh[:, k, :], s0, False, dp)
                            mm(o, wh, xl[:, k, :], False, False)
                            t = mm(o, wl, xh[:, k, :], False, s1, inc=kk == kc - 1)
                    if ui == nu - 1:
                        g.banks.give(bk + i, evac(i, bk + i, t))
                st.done(u, t)
                k0 += kc
            for i in range(nbk, 4):
                g.banks.give(bk + i, fr[i])
            return t

        xs = at("xs", 64, [128, NB, D])
        xTh, xTl = at("xTh", 32, [128, 8, T], F32R), at("xTl", 48, [128, 8, T], F32R)
        t_xT = norm_t(xs, n1c, xTh, xTl, t_x)
        t_xs_dead = t_xT

        qkn = at("qkn", 96, [128, NB, 10, 64])
        vn = at("vn", 106, [128, NB, 128])
        qT = at("qT", 108, [128, 4, T])
        kT = at("kT", 116, [128, 2, T])
        sA = [at("sA0", 120, [128, 4, 256]), at("sA1", 124, [128, 4, 256])]
        kd = at("kd", 120, [128, NB, 2, 128])
        pTb = at("pTb", 128, [128, 2, 4, 128])
        attnT = at("attnT", 132, [128, 4, T])
        stg = at("stg", 140, [128, 512])
        sq = at("sq", 116, [128, 2, 640])

        RP = at("RP", 31.125, [128, 4, 8])
        ANG, KF, CS, SN = (at(n, 128 + 0.125 * i, [128, 4, 8]) for i, n in enumerate(("ANG", "KF", "CSt", "SNt")))
        COS, SIN = at("COS", 31.25, [128, 4, 8]), at("SIN", 31.375, [128, 4, 8])
        KI = at("KI", 128.5, [128, 4, 8], I32)
        PF = at("PF", 128.625, [128, 4])
        t = cp(PF[:, :], POS[:, :], t_c)
        t = tt(ANG[:, :, :], bc(PF[:, :], 2, [128, 4, 8]), bc(cst("invf"), 1, [128, 4, 8]), ALU.mult, t, t_c)
        t = ts(KF[:, :, :], ANG[:, :, :], 0.15915494309189535, None, ALU.mult, None, t)
        t = cp(KI[:, :, :], KF[:, :, :], t)
        t = cp(KF[:, :, :], KI[:, :, :], t)
        for cc in (-6.28125, -0.0019350051879882812, -3.0199159819567876e-07):
            t = stt(ANG[:, :, :], KF[:, :, :], cc, ANG[:, :, :], ALU.mult, ALU.add, t)
        t = ts(SN[:, :, :], ANG[:, :, :], 3.1415925, -3.1415925, ALU.min, ALU.max, t)
        t2 = ts(CS[:, :, :], ANG[:, :, :], 1.5707963267948966, None, ALU.add, None, t)
        t2 = ts(KF[:, :, :], CS[:, :, :], 3.141592653589793, -6.283185307179586, ALU.is_gt, ALU.mult, t2)
        t2 = tt(CS[:, :, :], CS[:, :, :], KF[:, :, :], ALU.add, t2)
        t2 = ts(CS[:, :, :], CS[:, :, :], 3.1415925, -3.1415925, ALU.min, ALU.max, t2)
        t_rope = [af(SIN[:, :, :], SN[:, :, :], ACT.Sin, t), af(COS[:, :, :], CS[:, :, :], ACT.Sin, t2)]

        l0, l1 = lbr[:, 0:4], lbr[:, 4:8]
        lm, le0, le1, lsum, lb, oml = (lbs[:, 4 * i:4 * i + 4] for i in range(6))
        t = tt(lm, l0, l1, ALU.max, t_c)
        ta = tt(le0, l0, lm, ALU.subtract, t)
        tb_ = tt(le1, l1, lm, ALU.subtract, t)
        ta = af(le0, le0, ACT.Exp, ta)
        tb_ = af(le1, le1, ACT.Exp, tb_)
        t = tt(lsum, le0, le1, ALU.add, ta, tb_)
        t = rcp(lsum, lsum, t)
        t = tt(lb, le0, lsum, ALU.mult, t)
        t_lb = ts(oml, lb, -1.0, 1.0, ALU.mult, ALU.add, t)

        t_q, t_v = [], []

        def ev_q(i, b, t):
            a = cp(qkn[:, i, 0:8, :].rearrange("p h d -> p (h d)"), PS[:, b, :], t)
            t_q.append(a)
            return a

        def ev_kv(i, b, t):
            a = acp(qkn[:, i, 8:10, :].rearrange("p h d -> p (h d)"), PS[:, b, 0:128], t)
            c = acp(vn[:, i, :], PS[:, b, 128:256], t)
            t_q.append(a)
            t_v.append(c)
            return [a, c]

        dense(st, "qa", 2, "a", xTh, xTl, t_xT, 4, ev_q)
        dense(st, "kv", 2, "a", xTh, xTl, t_xT, 4, ev_kv)

        QS = at("QS", 31.5, [128, 40])
        t_ss = []
        t_prev = [None, None]
        for i in range(NB):
            a = af(sq[:, i % 2, :], qkn[:, i, :, :].rearrange("p h d -> p (h d)"), ACT.Square, t_q, t_prev[i % 2])
            r = red(QS[:, i * 10:i * 10 + 10], sq[:, i % 2, :].rearrange("p (h d) -> p h d", h=10), ALU.add, a)
            t_prev[i % 2] = r
            t_ss.append(r)
        t = ts(QS[:, :], QS[:, :], 1.0 / 64, EPS, ALU.mult, ALU.add, t_ss)
        t = af(QS[:, :], QS[:, :], ACT.Sqrt, t)
        t = rcp(QS[:, :], QS[:, :], t)
        t_n = []
        for i in range(NB):
            a = tt(qkn[:, i, :, :], qkn[:, i, :, :], bc(QS[:, i * 10:i * 10 + 10], 2, [128, 10, 64]), ALU.mult, t, t_q)
            t_n.append(tt(qkn[:, i, :, :], qkn[:, i, :, :], WQK[:, :, :], ALU.mult, a, t_c))
        R = [at(f"R{i}", 120 + 1.25 * i, [128, 4, 10, 8]) for i in range(4)]
        x1, x2 = qkn[:, :, :, 0:8], qkn[:, :, :, 8:16]
        cb = bc(COS[:, :, :], 2, [128, 4, 10, 8])
        sb_ = bc(SIN[:, :, :], 2, [128, 4, 10, 8])
        a1 = tt(R[0][:, :, :, :], x1, cb, ALU.mult, t_n, t_rope)
        a2 = tt(R[1][:, :, :, :], x2, sb_, ALU.mult, t_n, t_rope)
        a3 = tt(R[2][:, :, :, :], x2, cb, ALU.mult, t_n)
        a4 = tt(R[3][:, :, :, :], x1, sb_, ALU.mult, t_n)
        b1 = tt(x1, R[0][:, :, :, :], R[1][:, :, :, :], ALU.subtract, a1, a2, a4)
        b2 = tt(x2, R[2][:, :, :, :], R[3][:, :, :, :], ALU.add, a3, a4, a2)
        t_r = [b1, b2]
        t_kd = []
        for i in range(NB):
            for kv in range(2):
                for rep in range(2):
                    t_kd.append(cp(kd[:, i, kv, rep * 64:rep * 64 + 64], qkn[:, i, 8 + kv, :], t_r))
        t_qT = []
        for j in range(4):
            b, fr = g.banks.take()
            for i in range(NB):
                t = tr(PS[:, b, i * 128:i * 128 + 128], qkn[:, i, 2 * j:2 * j + 2, :].rearrange("p h d -> p (h d)"),
                       t_r, fr, inc=i == 3)
            a = acp(qT[:, j, :], PS[:, b, :], t)
            g.banks.give(b, a)
            t_qT.append(a)
        for j in range(2):
            b, fr = g.banks.take()
            for i in range(NB):
                t = tr(PS[:, b, i * 128:i * 128 + 128], kd[:, i, j, :], t_kd, fr, inc=i == 3)
            a = acp(kT[:, j, :], PS[:, b, :], t, t_ss)
            g.banks.give(b, a)
            t_qT.append(a)

        amask = M1[:, 0:256]
        SS = at("SS", 31.75, [128, 16])
        t_at = []
        t_sfree = [t_qT, t_qT]
        t_pT = None
        it = 0
        for n in range(NB):
            W = 256 if n else 128
            k0 = (n - 1) * 128 if n else 0
            nkb = W // 128
            for j in range(2):
                s = sA[it % 2][:, :, 0:W]
                b, fr = g.banks.take(2)
                for par in range(2):
                    for jj in range(2):
                        pr = 2 * j + jj
                        t = mm(PS[:, b + par, jj * 256:jj * 256 + W], qT[par * 64:par * 64 + 64, pr, n * 128:n * 128 + 128],
                               kT[par * 64:par * 64 + 64, j, k0:k0 + W], True, True, t_qT, fr, inc=jj == 1)
                pv = PS[:, b:b + 2, :].rearrange("p b (c w) -> p (b c) w", w=256)[:, :, 0:W]
                so = sink[:, 4 * j:4 * j + 4].rearrange("p (c e) -> p e c", e=2)
                mx = SS[:, 0:4]
                t = stt(s, pv, 0.125, bc(amask[:, 256 - W:256], 1, [128, 4, W]), ALU.mult, ALU.add, t, t_c,
                        t_sfree[it % 2])
                g.banks.give(b, t, 2)
                t2 = red(mx, s, ALU.max, t, t_at[-1:] if t_at else None)
                t2 = tt(mx.rearrange("p (e c) -> p e c", e=2), mx.rearrange("p (e c) -> p e c", e=2), so, ALU.max, t2)
                t3 = tt(s, s, bc(mx, 2, [128, 4, W]), ALU.subtract, t2, t)
                t4 = tt(SS[:, 4:8].rearrange("p (e c) -> p e c", e=2), so, mx.rearrange("p (e c) -> p e c", e=2),
                        ALU.subtract, t2)
                t3 = af(s, s, ACT.Exp, t3)
                t4 = af(SS[:, 4:8], SS[:, 4:8], ACT.Exp, t4)
                t5 = red(SS[:, 8:12], s, ALU.add, t3)
                t5 = tt(SS[:, 8:12], SS[:, 8:12], SS[:, 4:8], ALU.add, t5, t4)
                t5 = rcp(SS[:, 12:16], SS[:, 8:12], t5)
                t6 = tt(s, s, bc(SS[:, 12:16], 2, [128, 4, W]), ALU.mult, t5, t3)
                ev = []
                for kb in range(nkb):
                    b, fr = g.banks.take()
                    for hh in range(4):
                        t = tr(PS[:, b, hh * 128:hh * 128 + 128], s[:, hh, kb * 128:kb * 128 + 128], t6, fr, inc=hh == 3)
                    a = acp(pTb[:, kb, :, :].rearrange("p h q -> p (h q)"), PS[:, b, :], t, t_pT)
                    g.banks.give(b, a)
                    ev.append(a)
                t_sfree[it % 2] = ev
                b, fr = g.banks.take()
                for par in range(2):
                    for kb in range(nkb):
                        t = mm(PS[par * 64:par * 64 + 64, b, 0:256], vn[:, n - nkb + 1 + kb, j * 64:j * 64 + 64],
                               pTb[:, kb, 2 * par:2 * par + 2, :].rearrange("p h q -> p (h q)"), kb == 0, kb == nkb - 1,
                               ev, t_v, fr, inc=kb == nkb - 1)
                t_pT = t
                a = acp(attnT[:, 2 * j:2 * j + 2, n * 128:n * 128 + 128],
                        PS[:, b, 0:256].rearrange("p (c q) -> p c q", c=2), t)
                g.banks.give(b, a)
                t_at.append(a)
                it += 1
        t_attn = list(t_at) + [t_pT]

        qh, bb = at("qh", 64, [128, 4, T]), at("bb", 72, [128, 4, T])
        kh, vh = at("kh", 80, [128, 4, T]), at("vh", 88, [128, NB, 512])
        t_qh, t_fg, t_vh = {}, {}, []

        def ev_qh(i, b, t):
            t_qh[i] = af(qh[:, i, :], PS[:, b, :], ACT.Silu, t, t_xs_dead)
            return t_qh[i]

        def ev_fh(i, b, t):
            a = af(bb[:, i, :], PS[:, b, :], ACT.Sigmoid, t, t_xs_dead)
            t_fg[i] = ts(bb[:, i, :], bb[:, i, :], oml[:, i:i + 1], lb[:, i:i + 1], ALU.mult, ALU.add, a, t_lb)
            return a

        def ev_vh(i, b, t):
            t_vh.append(acp(vh[:, i, :], PS[:, b, :], t))
            return t_vh[-1]

        dense(st, "qh", 2, "b", xTh, xTl, t_xT, 4, ev_qh)
        dense(st, "fh", 2, "b", xTh, xTl, t_xT, 4, ev_fh)
        dense(st, "ih", 2, "a", xTh, xTl, t_xT, 4, ev_vh)

        gs = at("gs", 124, [128, NB, 512])
        t_gs = []

        def ev_gh(i, b, t):
            a = af(gs[:, i, :], PS[:, b, :], ACT.Silu, t, t_attn)
            v = gs[:, i, :].rearrange("p (h v) -> p h v", h=4)
            t_gs.append(tt(v, v, bc(HNW[:, :], 1, [128, 4, 128]), ALU.mult, a, t_c))
            return a

        dense(st, "gh", 2, "a", xTh, xTl, t_xT, 4, ev_gh)

        s_z = slot("s_z")
        t_z = [None]
        zi = [0]

        def ev_z(i, b, t):
            a = af(stg[:, :], PS[:, b, :], ACT.Sigmoid, t, t_z[0])
            c = zi[0]
            zi[0] += 1
            t_z[0] = g.sp.dma(lambda e: e.dma_start(zsp[c, :, :], stg[:, :]), s_z, a)
            return a

        def hgrn():
            E = [at("E0", 96, [128, T]), at("E1", 98, [128, T])]
            QE = [at("QE0", 100, [128, T]), at("QE1", 102, [128, T])]
            KE = [at("KE0", 104, [128, T]), at("KE1", 106, [128, T])]
            AT = [at("AT0", 108, [128, T]), at("AT1", 110, [128, T])]
            ho = at("ho", 112, [128, 4, NB, 128])
            St = at("St", 120, [128, 128])
            QB = at("QB", 120.5, [128, T])
            KN = at("KN", 122.5, [128, 3, 128])
            hss = at("hss", 31.5, [128, 16])
            eb = at("eb", 31.5625, [128, 4])
            z = [dve(lambda e, A=A: e.memset(A[:, :], 0.0), t_attn) for A in AT]
            t_ho = []
            tE, tQ, tK, tA = [None, None], [None, None], [None, None], [z[0], z[1]]
            tQB = tKN = tS = None
            k = 0
            lns = [af(kh[:, h, :], bb[:, h, :], ACT.Ln, t_fg[h]) for h in range(4)]
            scans, kks = [], []
            for h in range(4):
                tk = af(E[h % 2][:, :], bb[:, h, :], ACT.Copy, t_fg[h], lns[h], t_attn, tE[h % 2], scale=-1.0, bias=1.0)
                t = dve(lambda e, h=h: e.tensor_tensor_scan(bb[:, h, :], M1[:, 256:768], kh[:, h, :], 0.0, ALU.mult, ALU.add),
                        lns[h], t_c, tk)
                tc_ = cp(kh[:, h, :], E[h % 2][:, :], tk, t)
                tE[h % 2] = tc_
                scans.append(t)
                kks.append(tc_)
            yield
            for h in range(4):
                AH = AT[h % 2]
                b3 = bb[:, h, :]
                tb0 = [scans[h], kks[h]]
                for lv in range(8):
                    if lv == 7:
                        qs, ks, tq, tk = qh[:, h, :], kh[:, h, :], [t_qh[h], kks[h]], None
                    else:
                        hw = 64 >> lv
                        nb = T // (2 * hw)
                        e_, q_, k_ = E[k % 2], QE[k % 2], KE[k % 2]
                        bv = b3.rearrange("p (n w) -> p n w", w=2 * hw)
                        t = tt(e_[:, :].rearrange("p (n w) -> p n w", w=2 * hw), bv,
                               bv[:, :, hw - 1:hw].broadcast_to([128, nb, 2 * hw]), ALU.subtract, tb0, tE[k % 2])
                        t = af(e_[:, :], e_[:, :], ACT.Abs, t)
                        t = af(e_[:, :], e_[:, :], ACT.Exp, t, scale=-1.0)
                        tq = tt(q_[:, :], qh[:, h, :], e_[:, :], ALU.mult, t, t_qh[h], tQ[k % 2])
                        tk = tt(k_[:, :], kh[:, h, :], e_[:, :], ALU.mult, t, tK[k % 2], on=pool)
                        tE[k % 2] = [tq, tk]
                        qs, ks = q_[:, :], k_[:, :]
                    b, fr = g.banks.take()
                    for c in range(4):
                        t = mm(PS[:, b, c * 128:c * 128 + 128], ks[:, c * 128:c * 128 + 128], qs[:, c * 128:c * 128 + 128],
                               True, True, tq, tk, fr, inc=c == 3)
                    if lv < 7:
                        tQ[k % 2] = tK[k % 2] = t
                        k += 1
                    av = AH[:, :].rearrange("p (c t) -> p c t", c=4)
                    a = dve(lambda e, av=av, b=b, lv=lv: e.copy_predicated(
                        av, bc(MK[:, lv * 128:lv * 128 + 128], 1, [128, 4, 128]),
                        PS[:, b, :].rearrange("p (c t) -> p c t", c=4)), t, tA[h % 2], t_c)
                    g.banks.give(b, a)
                    tA[h % 2] = a
                    yield
                e_, q_, k_ = E[k % 2], QE[k % 2], KE[k % 2]
                t1 = af(QB[:, :], b3, ACT.Exp, tb0, tQB)
                t1 = tt(QB[:, :], QB[:, :], qh[:, h, :], ALU.mult, t1)
                bv = b3.rearrange("p (n w) -> p n w", w=128)
                t = tt(e_[:, :].rearrange("p (n w) -> p n w", w=128), bv, bv[:, :, 127:128].broadcast_to([128, 4, 128]),
                       ALU.subtract, tb0, tE[k % 2])
                t = af(e_[:, :], e_[:, :], ACT.Exp, t, scale=-1.0)
                t = tt(k_[:, :], e_[:, :], kh[:, h, :], ALU.mult, t, tK[k % 2])
                tE[k % 2] = t
                te = af(eb[:, :], bv[:, :, 127], ACT.Exp, tb0, tS)
                b, fr = g.banks.take()
                for c in range(3):
                    t2 = tr(PS[:, b, c * 128:c * 128 + 128], k_[:, c * 128:c * 128 + 128], t, fr, inc=c == 2)
                tK[k % 2] = t2
                a = acp(KN[:, :, :].rearrange("p c k -> p (c k)"), PS[:, b, 0:384], t2, tKN)
                g.banks.give(b, a)
                k += 1
                bo, fro = g.banks.take()
                yield
                for c in range(4):
                    o = PS[:, bo, c * 128:c * 128 + 128]
                    v = vh[:, c, h * 128:h * 128 + 128]
                    t = mm(o, AH[:, c * 128:c * 128 + 128], v, True, c == 0, tA[h % 2], t_vh, fro, inc=c == 0)
                    if c:
                        t = mm(o, QB[:, c * 128:c * 128 + 128], St[:, :], False, True, t1, tS, inc=True)
                    if c < 3:
                        b, fr = g.banks.take()
                        if b == bo:
                            b, fr = g.banks.take()
                        t3 = mm(PS[:, b, 0:128], KN[:, c, :], v, True, True, a, fr, inc=True)
                        if c == 0:
                            tS = cp(St[:, :], PS[:, b, 0:128], t3, tS, t)
                        else:
                            tS = stt(St[:, :], St[:, :], eb[:, c:c + 1], PS[:, b, 0:128], ALU.mult, ALU.add, t3, tS, te, t)
                        g.banks.give(b, tS)
                tKN = t3
                tQB = t
                tA[h % 2] = [t, tA[h % 2]]
                hv = ho[:, h, :, :].rearrange("p c v -> p (c v)")
                tS = [tS, t]
                a = cp(hv, PS[:, bo, :], t)
                g.banks.give(bo, a)
                e_ = E[k % 2]
                t = af(e_[:, :], hv, ACT.Square, a, tE[k % 2])
                t = red(hss[:, 4 * h:4 * h + 4], e_[:, :].rearrange("p (c v) -> p c v", c=4), ALU.add, t)
                tE[k % 2] = t
                k += 1
                t_ho.append([a, t])
                yield
            t = ts(hss[:, :], hss[:, :], 1.0 / 128, EPS, ALU.mult, ALU.add, t_ho)
            t = af(hss[:, :], hss[:, :], ACT.Sqrt, t)
            t = rcp(hss[:, :], hss[:, :], t)
            hTh, hTl = at("hTh", 64, [128, 4, T], F32R), at("hTl", 72, [128, 4, T], F32R)
            g.t_hT = []
            for h in range(4):
                a = tt(ho[:, h, :, :], ho[:, h, :, :], bc(hss[:, 4 * h:4 * h + 4], 2, [128, NB, 128]), ALU.mult, t, t_ho)
                a = tt(ho[:, h, :, :], ho[:, h, :, :], gs[:, :, h * 128:h * 128 + 128], ALU.mult, a, t_gs)
                b, fr = g.banks.take()
                for c in range(4):
                    t2 = tr(PS[:, b, c * 128:c * 128 + 128], ho[:, h, c, :], a, fr, inc=c == 3)
                x = hilo(hTh[:, h, :], hTl[:, h, :], PS[:, b, :], t2, t_ho, scans, tE, tQ, tK, tQB)
                g.banks.give(b, x)
                g.t_hT.append(x)
                yield
            g.hgrn_end = [t_ho, g.t_hT, tE, tQ, tK, tKN, tQB, tA]
            g.hTh, g.hTl = hTh, hTl

        def zproj():
            for n in ("za0", "za1", "zb0", "zb1"):
                yield from dense_steps(st, n, 2, "b", xTh, xTl, t_xT, 4, ev_z)

        def dense_steps(*a):
            dense(*a)
            yield

        def interleave(*gens):
            gens = list(gens)
            while gens:
                for ge in list(gens):
                    try:
                        next(ge)
                    except StopIteration:
                        gens.remove(ge)

        interleave(hgrn(), zproj())
        t_in_end = (g.pe.sem, g.pe.n)

        aTh, aTl = at("aTh", 96, [128, 4, T], F32R), at("aTl", 104, [128, 4, T], F32R)
        t_aT = []
        for c in range(4):
            t_aT.append(hilo(aTh[:, c, :], aTl[:, c, :], attnT[:, c, :], t_attn, g.hgrn_end))
        zr = [at(f"zr{i}", 112 + 2 * i, [128, 512]) for i in range(8)]
        mTh, mTl = at("mTh", 32, [128, 8, T], F32R), at("mTl", 48, [128, 8, T], F32R)
        s_zr = [slot(f"s_zr{i}") for i in range(8)]
        t_mT, t_zfree = [], [None] * 8
        for c in range(2):
            zl = []
            for i in range(4):
                for w in range(2):
                    q = 2 * i + w
                    zl.append(g.sp.dma(lambda e, q=q, w=w, i=i, c=c: e.dma_start(zr[q][:, :], zsp[8 * w + 4 * c + i, :, :]),
                                       s_zr[q], t_z[0], g.hgrn_end, t_zfree[q]))
            ta_ = {}

            def ev_ba(i, b, t):
                ta_[i] = tt(zr[2 * i][:, :], zr[2 * i][:, :], PS[:, b, :], ALU.mult, t, zl[2 * i])
                return ta_[i]

            def ev_bh(i, b, t):
                z0, z1 = zr[2 * i][:, :], zr[2 * i + 1][:, :]
                a = tt(z1, z1, PS[:, b, :], ALU.mult, t, zl[2 * i + 1])
                s = tt(z0, z0, z1, ALU.add, a, ta_[i])
                x = hilo(mTh[:, 4 * c + i, :], mTl[:, 4 * c + i, :], z0, s, t_in_end)
                t_zfree[2 * i] = t_zfree[2 * i + 1] = x
                t_mT.append(x)
                return a

            dense(st, ("ba", c), 1, "b", aTh, aTl, t_aT, 4, ev_ba)
            dense(st, ("bh", c), 1, "b", g.hTh, g.hTl, g.t_hT, 4, ev_bh)
        t_x2 = []

        def ev_add(c):
            def f(i, b, t):
                v = x_sb[:, i, c * 512:c * 512 + 512]
                a = tt(v, v, PS[:, b, :], ALU.add, t)
                t_x2.append(a)
                return a
            return f

        for c in range(2):
            t_wo = dense(st, ("wo", c), 2, "a", mTh, mTl, t_mT, 4, ev_add(c))

        hn = at("hn", 32, [128, NB, D])
        hnT = at("hnT", 48, [128, 8, T])
        hnh, hnl = at("hnh", 64, [128, NB, D], F32R), at("hnl", 80, [128, NB, D], F32R)
        n2b = at("n2b", 96, [128, D])
        WR = at("WR", 100, [128, 8, 36])
        BR = at("BR", 101.25, [128, 36])
        Lg = at("Lg", 102, [128, 4, 36])
        s_r = slot("s_r")
        moe_free = [t_wo, g.t_hT, t_aT, t_mT, t_x2, g.hgrn_end]
        g.sp.dma(lambda e: e.dma_start(n2b[:, :], I["norm2_w"].partition_broadcast(128)[:, 0, :]), s_r, moe_free)
        g.sp.dma(lambda e: e.dma_start(WR[:, :, :], I["w_router"]), s_r)
        g.sp.dma(lambda e: e.dma_start(BR[:, :], I["b_router"].partition_broadcast(128)[:, 0, :]), s_r)
        t_r = (s_r[0], s_r[1])
        r, a = stats(hn, moe_free)
        t_hn = [stt(hn[:, tb, :], x_sb[:, tb, :], rs4[:, tb:tb + 1], n2b[:, :], ALU.mult, ALU.mult, r, a, t_r)
                for tb in range(NB)]
        t_hT2 = []
        for c in range(8):
            b, fr = g.banks.take()
            for tb in range(NB):
                t = tr(PS[:, b, tb * 128:tb * 128 + 128], hn[:, tb, c * 128:c * 128 + 128], t_hn, fr, inc=tb == 3)
            a = acp(hnT[:, c, :], PS[:, b, :], t, moe_free)
            g.banks.give(b, a)
            t_hT2.append(a)
        b, fr = g.banks.take()
        for tb in range(NB):
            for k in range(8):
                t = mm(PS[:, b, tb * 36:tb * 36 + 36], hnT[:, k, tb * 128:tb * 128 + 128], WR[:, k, :], k == 0, k == 7,
                       t_hT2, t_r, fr, inc=k == 7)
        t_lg = tt(Lg[:, :, :], PS[:, b, 0:144].rearrange("p (b n) -> p b n", b=4), bc(BR[:, :], 1, [128, 4, 36]), ALU.add, t, t_r)
        g.banks.give(b, t_lg)
        t_hs = []
        for tb in range(NB):
            a = acp(hnh[:, tb, :], hn[:, tb, :], t_hn, moe_free)
            t_hs.append([a, tt(hnl[:, tb, :], hn[:, tb, :], hnh[:, tb, :].bitcast(F32), ALU.subtract, a, on=pool)])

        RT = at("RT", 103, [128, 1600])
        ro = [0]

        def rt(n):
            o = ro[0]
            ro[0] += n
            assert ro[0] <= 1600
            return RT[:, o:o + n]

        lg, le = Lg[:, :, 0:4], Lg[:, :, 4:36].rearrange("p b (g j) -> p b g j", g=4)

        def first_max(v, n, t, dec):
            m = rt(4)
            eq, s = rt(4 * n).rearrange("p (b n) -> p b n", b=4), rt(4)
            t1 = red(m, v, ALU.max, t)
            t2 = tt(eq, v, bc(m, 2, [128, 4, n]), ALU.is_equal, t1)
            t2 = tt(eq, eq, bc(dec, 1, [128, 4, n]), ALU.mult, t2)
            t2 = red(s, eq, ALU.max, t2)
            t2 = tt(eq, eq, bc(s, 2, [128, 4, n]), ALU.is_equal, t2)
            return m, eq, t1, t2

        dec8 = cst("dec8")
        gm, g1h, t1, tg = first_max(lg, 4, t_lg, dec8[:, 4:8])
        dlg, gsum = rt(16).rearrange("p (b n) -> p b n", b=4), rt(4)
        t = tt(dlg, lg, bc(gm, 2, [128, 4, 4]), ALU.subtract, t1)
        t = af(dlg, dlg, ACT.Exp, t)
        t = red(gsum, dlg, ALU.add, t)
        t_pg = rcp(gsum, gsum, t)
        ls = rt(128).rearrange("p (b g j) -> p b g j", b=4, g=4)
        lsel = rt(32).rearrange("p (b j) -> p b j", b=4)
        t = tt(ls, le, bc(g1h, 3, [128, 4, 4, 8]), ALU.mult, tg)
        t = red(lsel, ls.rearrange("p b g j -> p b j g"), ALU.add, t)
        m1, o1, t1, to1 = first_max(lsel, 8, t, dec8)
        l2 = rt(32).rearrange("p (b j) -> p b j", b=4)
        t = stt(l2, o1, -3e38, lsel, ALU.mult, ALU.add, to1)
        m2, o2, t2, to2 = first_max(l2, 8, t, dec8)
        e2, den = rt(4), rt(4)
        t = tt(e2, m2, m1, ALU.subtract, t1, t2)
        t = af(e2, e2, ACT.Exp, t)
        t3 = ts(den, e2, 1.0, None, ALU.add, None, t)
        t3 = rcp(den, den, t3)
        gwv = gw.rearrange("p (b k) -> p b k", k=2)
        t3 = tt(gwv[:, :, 0], gsum, den, ALU.mult, t3, t_pg)
        t_gw = tt(gwv[:, :, 1], gwv[:, :, 0], e2, ALU.mult, t3, t)
        O = [rt(128).rearrange("p (b g j) -> p b g j", b=4, g=4) for _ in range(2)]
        t_o = [tt(O[k], bc(g1h, 3, [128, 4, 4, 8]), bc(o, 2, [128, 4, 4, 8]), ALU.mult, tg, tt_)
               for k, (o, tt_) in enumerate(((o1, to1), (o2, to2)))]
        Of = [o.rearrange("p b g j -> p b (g j)") for o in O]
        M = rt(128).rearrange("p (b e) -> p b e", b=4)
        t_m = tt(M, Of[0], Of[1], ALU.add, t_o)
        b, fr = g.banks.take()
        for tb in range(NB):
            for q in range(tb + 1):
                t = mm(PS[:, b, tb * 32:tb * 32 + 32], ones if q < tb else cst("ustrict"), M[:, q, :], q == 0, q == tb,
                       t_m, fr, inc=q == tb)
        for q in range(NB):
            t = mm(PS[:, b, 128:160], ones, M[:, q, :], q == 0, q == 3, inc=q == 3)
        rank = rt(128).rearrange("p (b e) -> p b e", b=4)
        cnt = rt(32)
        t_k = cp(rank, PS[:, b, 0:128].rearrange("p (b e) -> p b e", b=4), t)
        t_n = cp(cnt, PS[:, b, 128:160], t)
        g.banks.give(b, [t_k, t_n])
        mxn, stp, pf = rt(1), rt(8), rt(1)
        t = red(mxn, cnt, ALU.max, t_n)
        t = ts(stp, cst("step8"), mxn, None, ALU.is_lt, None, t, t_c)
        t = red(pf, stp, ALU.add, t)
        t_P = cp(PI[:, 0:1], pf, t)
        tmp = rt(128).rearrange("p (b e) -> p b e", b=4)
        rkv, ekv = rk.rearrange("p (b k) -> p b k", k=2), ek.rearrange("p (b k) -> p b k", k=2)
        t_e = []
        t = t_k
        for k in range(2):
            t = tt(tmp, Of[k], rank, ALU.mult, t, t_k, t_o)
            t = red(rkv[:, :, k], tmp, ALU.add, t)
            t_e.append(t)
            t = tt(tmp, Of[k], bc(cst("e64"), 1, [128, 4, 32]), ALU.mult, t)
            t = red(ekv[:, :, k], tmp, ALU.add, t)
            t_e.append(t)
        rkm = rt(128).rearrange("p (b e) -> p b e", b=4)
        t = stt(rkm, rank, 1.0, M, ALU.add, ALU.mult, t_k, t_m)
        t_rkm = ts(rkm, rkm, -1.0, None, ALU.add, None, t)

        S = [at(f"S{i}", 109.5 + 2 * i, [128, NB, 2, WIN], F32R) for i in range(2)]
        XG = [at(f"XG{i}", 32 + 8 * i, [128, 8, 2, 2, WIN], F32R) for i in range(2)]
        GS = [at(f"GS{i}", 48 + 2 * i, [128, 512]) for i in range(2)]
        US = [at(f"US{i}", 52 + 2 * i, [128, 512]) for i in range(2)]
        HT = [at(f"HT{i}", 56 + 2 * i, [128, 4, 2, WIN], F32R) for i in range(2)]
        SG = [at(f"SG{i}", 60 + i, [128, 256]) for i in range(2)]
        HF = [at(f"HF{i}", 62 + i, [128, 256]) for i in range(2)]
        YT = [at(f"YT{i}", 113.5 + 4 * i, [128, D]) for i in range(2)]
        GT = [at(f"GT{i}", 121.5 + 4 * i, [128, D]) for i in range(4)]

        def experts(st, s_y, s_g, t0, t_rkm, t_idx):
            tS, tXG, tGS, tHT, tY = [None] * 2, [None] * 2, [None] * 2, [None] * 2, [None] * 2
            xg = {}
            ywr = []

            def gather(i):
                p = i % 2
                t = tt(S[p][:, :, :, :], bc(rkm[:, :, 2 * i:2 * i + 2], 3, [128, NB, 2, WIN]),
                       cst("iota").unsqueeze(1).unsqueeze(1).broadcast_to([128, NB, 2, WIN]), ALU.is_equal, t_rkm, tS[p], t0)
                ev = []
                for hl, src in ((0, hnh), (1, hnl)):
                    for c4 in range(2):
                        b, fr = g.banks.take()
                        for c in range(4):
                            cc = 4 * c4 + c
                            for tb in range(NB):
                                t2 = mm(PS[:, b, c * 128:c * 128 + 128], src[:, tb, cc * 128:cc * 128 + 128],
                                        S[p][:, tb, :, :].rearrange("p e s -> p (e s)"), tb == 0, tb == 3,
                                        t, t_hs, fr, inc=c == 3 and tb == 3)
                        f = acp if c4 else cp
                        for e in range(2):
                            a = f(XG[p][:, 4 * c4:4 * c4 + 4, e, hl, :],
                                  PS[:, b, :].rearrange("p (c e s) -> p c e s", c=4, e=2)[:, :, e, :], t2, tXG[p], t0)
                            ev.append(a)
                        g.banks.give(b, ev[-2:])
                tS[p] = t2
                xg[i] = ev

            fold_in = {}

            def gate_up(e):
                i, p = e // 2, (e // 2) % 2
                if e % 2 == 0:
                    gather(i)
                q = e % 2
                toks = []
                for kind, dst, cpy in (("g", GS[q], acp), ("u", US[q], cp)):
                    b, fr = g.banks.take()
                    for ui in range(2):
                        u, h, l, tok = st.take((kind, e))
                        for kk in range(4):
                            k = 4 * ui + kk
                            xw = XG[p][:, k, q, :, :].rearrange("p a s -> p (a s)")
                            mm(PS[:, b, :], xw, h[:, kk, :], k == 0, False, tok, xg[i], fr)
                            t = mm(PS[:, b, :], xw, l[:, kk, :], False, k == 7, inc=kk == 3)
                        st.done(u, t)
                    a = cpy(dst[:, :], PS[:, b, :], t, tGS[q])
                    g.banks.give(b, a)
                    toks.append(a)
                tXG[p] = t
                fold_in[e] = toks

            def act_fold(e):
                q = e % 2
                b, fr = g.banks.take()
                for o, src in ((0, GS[q]), (256, US[q])):
                    for j in range(4):
                        t = mm(PS[:, b, o + j * 64:o + j * 64 + 64], src[:, j * 128:j * 128 + 128], fold, True, True,
                               fold_in[e], fr, t_c, inc=j == 3)
                tGS[q] = t
                a = af(SG[q][:, :], PS[:, b, 0:256], ACT.Silu, t, t0)
                m = tt(HF[q][:, :], SG[q][:, :], PS[:, b, 256:512], ALU.mult, a)
                g.banks.give(b, [a, m])
                hv = HF[q][:, :].rearrange("p (j s) -> p j s", j=4)
                a = acp(HT[q][:, :, 0, :], hv, m, tHT[q])
                l = tt(HT[q][:, :, 1, :], hv, HT[q][:, :, 0, :].bitcast(F32), ALU.subtract, a, tHT[q])
                return [a, l]

            def down(e, th):
                q, y = e % 2, YT[(e // 2) % 2]
                r0, r1 = (0, 64) if q == 0 else (64, 0)
                outs = []
                for c in range(2):
                    b, fr = g.banks.take()
                    u, h, l, tok = st.take(("d", e))
                    for j in range(4):
                        hw = HT[q][:, j, :, :].rearrange("p a s -> p (a s)")
                        mm(PS[:, b, :], hw, h[:, j, :], j == 0, False, tok, th, fr)
                        t = mm(PS[:, b, :], hw, l[:, j, :], False, j == 3, inc=j == 3)
                    st.done(u, t)
                    yv = y[r0:r0 + 64, c * 512:c * 512 + 512]
                    a = acp(yv, PS[r0:r0 + 64, b, :], t, tY[(e // 2) % 2], t0)
                    m = tt(yv, PS[r1:r1 + 64, b, :], yv, ALU.add, a)
                    g.banks.give(b, [a, m])
                    outs.append(m)
                tHT[q] = t
                return outs

            gate_up(0)
            yo = []
            for e in range(NE):
                th = act_fold(e)
                if e + 1 < NE:
                    gate_up(e + 1)
                yo += down(e, th)
                if e % 2:
                    i = e // 2
                    tY[i % 2] = g.act.dma(lambda q, i=i: q.dma_start(ysp[i * 128:i * 128 + 128, :], YT[i % 2][:, :]),
                                          s_y[i % 2], yo)
                    yo = []
            last = []
            gfree = [None] * 4
            n = 0
            xt = None
            for b in range(NB):
                for k in range(2):
                    j = 2 * b + k
                    gt = GT[n % 4]
                    t = g.pool.dma(lambda q, gt=gt, j=j: q.indirect_dma_start(
                        gt[:, :], None, ysp[:, :], bass.IndirectOffsetOnAxis(ap=SI[:, j:j + 1], axis=0)),
                        s_g[n % 4], tY, t_idx, gfree[n % 4], t0)
                    v = x_sb[:, b, :]
                    xt = stt(v, gt[:, :], wt[:, j:j + 1], v, ALU.mult, ALU.add, t, t_idx, last[-1:])
                    gfree[n % 4] = xt
                    last.append(xt)
                    n += 1
            return last

        def index(*deps):
            a = ts(rc1, rk, 0.0, None, ALU.is_ge, None, *deps)
            b_ = ts(rc2, rk, float(WIN), None, ALU.is_lt, None, *deps)
            a = tt(rc1, rc1, rc2, ALU.mult, a, b_)
            w = tt(wt, gw, rc1, ALU.mult, a, t_gw)
            c = ts(rc2, rk, 0.0, float(WIN - 1), ALU.max, ALU.min, a)
            c = tt(rc2, rc2, ek, ALU.add, c)
            return [w, cp(SI[:, 0:8], rc2, c)]

        s_y = [slot(f"s_y{i}") for i in range(2)]
        s_g = [slot(f"s_g{i}") for i in range(4)]
        t_idx = index(*t_e)
        t_moe = experts(st, s_y, s_g, [t_lg, t_hs, t_hT2, t_hn], t_rkm, t_idx)

        main, main_banks = (g.pe, g.act, g.dve, g.pool, g.sp), g.banks
        lsems = []

        def lsem(n):
            s = sem(n)
            lsems.append(s)
            return s

        loop = tuple(Eng(lsem("l_" + n)) for n in engs)
        g.pe, g.act, g.dve, g.pool, g.sp = loop
        g.banks = Banks()
        lw = [[lsem(f"l_w{i}"), 0] for i in range(NR)]
        ly = [[lsem(f"l_y{i}"), 0] for i in range(2)]
        lg_ = [[lsem(f"l_g{i}"), 0] for i in range(4)]
        keep = (t_c, t_hs, t_gw)
        t_c = t_hs = t_gw = None
        lst = Stream(g, make_plan_moe(I), lw, raw, hi, lo, 0.0)
        a = ts(rkm, rkm, -float(WIN), None, ALU.add, None)
        b_ = ts(rk, rk, -float(WIN), None, ALU.add, None)
        ti = index(b_)
        experts(lst, ly, lg_, None, a, ti)
        t_c, t_hs, t_gw = keep
        bar = [sem(f"bar{i}") for i in range(4)]
        for q, lq, n in zip(main, loop, engs):
            q.items.append(("loop", q.waits([t_P]), lq.items, n))
        g.pe, g.act, g.dve, g.pool, g.sp = main
        g.banks = main_banks

        st = Stream(g, wplan3, wslots, raw, hi, lo, 0.0)
        g.st = st
        st.sp = {u - NR: g_ for u, g_ in ()}
        last_sp = [(g.act.sem, g.act.n), (g.dve.sem, g.dve.n), (g.pool.sem, g.pool.n)]
        for u in range(NR):
            st.sp[u - NR] = last_sp
        for u in range(NH):
            st.dn[u - NH] = (g.pe.sem, g.pe.n)
        st.load_to(NR)
        s_b = slot("s_b")
        FNB = at("FNB", 128, [128, D])

        def ffn(pre, wcol, scale_half, deps):
            xs = at("xs_" + pre, 32, [128, NB, D])
            xh, xl = at("xh_" + pre, 48, [128, 8, T], F32R), at("xl_" + pre, 64, [128, 8, T], F32R)
            th, tl = at("th_" + pre, 80, [128, 11, T], F32R), at("tl_" + pre, 102, [128, 11, T], F32R)
            sg = [at(f"sg{i}_" + pre, 124 + 2 * i, [128, 512]) for i in range(4)]
            t_xT = norm_t(xs, wcol, xh, xl, deps)
            t_sg = [None] * 4
            t_dn = None
            xt = []
            for half in range(2):
                t_h = {}
                for gi, (a0, b0) in enumerate(FCUTS):
                    nb = (b0 - a0) // 128
                    tg_ = {}

                    def ev_g(i, b, t):
                        tg_[i] = af(sg[i][:, :], PS[:, b, :], ACT.Silu, t, t_sg[i], deps)
                        return tg_[i]

                    def ev_u(i, b, t):
                        m = tt(sg[i][:, :], sg[i][:, :], PS[:, b, :], ALU.mult, t, tg_[i])
                        f = a0 // 128 + i
                        x = hilo(th[:, f, :], tl[:, f, :], sg[i][:, :], m, t_dn, deps)
                        t_sg[i] = x
                        t_h[f] = x
                        return m

                    dense(st, (pre, "g", half, gi), 2, "b", xh, xl, t_xT, nb, ev_g)
                    dense(st, (pre, "u", half, gi), 2, "b", xh, xl, t_xT, nb, ev_u)

                for c in range(2):
                    def ev_d(i, b, t):
                        v = x_sb[:, i, c * 512:c * 512 + 512]
                        a = stt(v, PS[:, b, :], 0.5, v, ALU.mult, ALU.add, t)
                        xt.append(a)
                        return a

                    t_dn = dense(st, (pre, "d", half, c), 3, "a", th, tl, t_h, 4, ev_d)
            return [xt, t_dn, t_sg]

        t_f1 = ffn("ffn1", f1c, 0.5, [t_moe, t_rkm, t_idx])

        xs = at("xs2", 32, [128, NB, D])
        xh, xl = at("xh2", 48, [128, 8, T], F32R), at("xl2", 64, [128, 8, T], F32R)
        t_xT = norm_t(xs, mxc, xh, xl, t_f1)
        qn, kn, v2 = (at(n, 80 + 8 * i, [128, NB, 512]) for i, n in enumerate(("qn2", "kn2", "v2")))
        up = at("up", 104, [128, 4, 16 + T])
        q2T, k2T = at("q2T", 112.5, [128, 4, T]), at("k2T", 120.5, [128, 4, T])
        s2 = at("s2", 128.5, [128, 4, T])
        P2 = [at(f"P2{i}", o, [128, 4, 128]) for i, o in enumerate((136.5, 138.5, 140.5, 90))]
        Bt = at("Bt", 32, [128, 8, 256])
        a2T = at("a2T", 40, [128, 4, T])
        QW = at("QW", 21, [128, 2, 64])
        QS2 = at("QS2", 21.5, [128, 64])
        PW = at("PW", 22, [128, 4, 128])
        S4 = at("S4", 24, [128, 16])
        g.sp.dma(lambda e: e.dma_start(QW[:, 0, :], I["q_norm_2"].partition_broadcast(128)[:, 0, :]), s_b, t_attn, t_gs,
                 g.hgrn_end)
        g.sp.dma(lambda e: e.dma_start(QW[:, 1, :], I["k_norm_2"].partition_broadcast(128)[:, 0, :]), s_b)
        g.sp.dma(lambda e: e.dma_start(PW[:, :, :], I["pool_w_2"][0].rearrange("g c d -> c g d")), s_b)
        t_b = (s_b[0], s_b[1])
        s_bt = slot("s_bt")
        t_bt = g.sp.dma(lambda e: e.dma_start(Bt[:, :, :], I["rel_tile"]), s_bt, t_xT)
        t_bt = tt(Bt[:, :, 128:256], Bt[:, :, 128:256], bc(cst("cmask"), 1, [128, 8, 128]), ALU.add, t_bt)
        t_p = [dve(lambda e: e.memset(up[:, :, 0:16], 0.0), t_f1)]
        t_q2, t_k2, t_v2, t_u2 = [], [], [], []

        def ev_nat(dst, toks, f):
            def ev(i, b, t):
                a = f(dst[:, i, :], PS[:, b, :], t, t_f1)
                toks.append(a)
                return a
            return ev

        def ev_up(i, b, t):
            a = acp(up[:, i, 16:16 + T], PS[:, b, :], t, t_f1)
            t_u2.append(a)
            return a

        dense(st, ("in2", 0), 2, "a", xh, xl, t_xT, 4, ev_nat(qn, t_q2, cp))
        dense(st, ("in2", 1), 2, "a", xh, xl, t_xT, 4, ev_nat(kn, t_k2, acp))
        dense(st, ("in2", 2), 2, "a", xh, xl, t_xT, 4, ev_nat(v2, t_v2, acp))
        t_in2 = dense(st, ("in2", 3), 2, "b", xh, xl, t_xT, 4, ev_up)

        t_ss, tp = [], [None] * 4
        for w, (src, tk) in enumerate(((qn, t_q2), (kn, t_k2))):
            for i in range(NB):
                sv = s2[:, i, :]
                a = af(sv, src[:, i, :], ACT.Square, tk, tp[i], t_f1)
                r = red(QS2[:, 32 * w + 8 * i:32 * w + 8 * i + 8], sv.rearrange("p (h d) -> p h d", h=8), ALU.add, a, t_b)
                tp[i] = r
                t_ss.append(r)
        t = ts(QS2[:, :], QS2[:, :], 1.0 / 64, EPS, ALU.mult, ALU.add, t_ss)
        t = af(QS2[:, :], QS2[:, :], ACT.Sqrt, t)
        t = rcp(QS2[:, :], QS2[:, :], t)
        t_qk = []
        for w, (src, dst, tk) in enumerate(((qn, q2T, t_q2), (kn, k2T, t_k2))):
            t_n = []
            for i in range(NB):
                v = src[:, i, :].rearrange("p (h d) -> p h d", h=8)
                a = tt(v, v, bc(QS2[:, 32 * w + 8 * i:32 * w + 8 * i + 8], 2, [128, 8, 64]), ALU.mult, t, tk)
                t_n.append(tt(v, v, bc(QW[:, w, :], 1, [128, 8, 64]), ALU.mult, a, t_b))
            for j in range(4):
                b, fr = g.banks.take()
                for i in range(NB):
                    t2 = tr(PS[:, b, i * 128:i * 128 + 128], src[:, i, j * 128:j * 128 + 128], t_n, fr, inc=i == 3)
                a = acp(dst[:, j, :], PS[:, b, :], t2, t_f1)
                g.banks.give(b, a)
                t_qk.append(a)
        pTh, pTl = at("pTh", 48, [128, 4, T], F32R), at("pTl", 56, [128, 4, T], F32R)
        a2h, a2l = at("a2h", 64, [128, 4, T], F32R), at("a2l", 72, [128, 4, T], F32R)
        W0 = [at(f"PP{i}", 80 + 2.0625 * i, [128, 16 + T]) for i in range(3)]
        dd = at("dd", 88, [128, T])
        z = [dve(lambda e, w=w: e.memset(w[:, 0:16], 0.0), t_qk) for w in W0[:2]]
        t_pool = []
        tdd = None
        tpp = [None, None]
        for gi in range(4):
            cur, tcur = up[:, gi, :], [t_u2, t_p]
            for stp_ in range(gi + 1):
                d = 1 << stp_
                nx = W0[stp_ % 2]
                tcur = tt(nx[:, 16:16 + T], cur[:, 16:16 + T], cur[:, 16 - d:16 - d + T], ALU.add, tcur, z, t_qk, tpp)
                cur = nx
            w = 2 << gi
            t = stt(dd[:, :], cur[:, 16:16 + T], 1.0 / w, up[:, gi, 16:16 + T], ALU.mult, ALU.subtract, tcur, tdd, t_qk)
            fx = W0[2][:, 0:16]
            t2 = tt(fx, cur[:, 16:32], cst("rc16")[:, gi * 16:gi * 16 + 16], ALU.mult, tcur, t, t_c)
            t2 = tt(dd[:, 0:16], fx, up[:, gi, 16:32], ALU.subtract, t2, t)
            b, fr = g.banks.take()
            t3 = mm(PS[:, b, :], PW[:, gi, :], dd[:, :], True, True, t, t2, t_b, fr, inc=True)
            tdd = t3
            h = af(pTh[:, gi, :], PS[:, b, :], ACT.Copy, t3, t_in2, scale=psc[:, gi:gi + 1])
            l = stt(pTl[:, gi, :], PS[:, b, :], psc[:, gi:gi + 1], pTh[:, gi, :].bitcast(F32), ALU.mult, ALU.subtract, h, t_in2)
            g.banks.give(b, [h, l])
            t_pool.append([h, l])

        t_at = []
        tsf = [t_qk, t_ss]
        tpT = None
        for qb in range(NB):
            W = (qb + 1) * 128
            Wn = min(W, 256)
            Wf = W - Wn
            for j in range(2):
                b, fr = g.banks.take(4)
                for hh in range(4):
                    h = 4 * j + hh
                    p0 = (h % 2) * 64
                    t = mm(PS[:, b + hh, 0:W], q2T[p0:p0 + 64, h // 2, qb * 128:qb * 128 + 128], k2T[p0:p0 + 64, h // 2, 0:W],
                           True, True, t_qk, fr, inc=hh == 3)
                t1 = stt(s2[:, :, Wf:W], PS[:, b:b + 4, Wf:W], 0.125, Bt[:, 4 * j:4 * j + 4, 256 - Wn:256], ALU.mult, ALU.add,
                         t, t_bt, tsf)
                t2 = None
                if Wf:
                    t2 = stt(s2[:, :, 0:Wf], PS[:, b:b + 4, 0:Wf], 0.125, bc(bfar[:, 4 * j:4 * j + 4], 2, [128, 4, Wf]),
                             ALU.mult, ALU.add, t, t_b, tsf)
                g.banks.give(b, [t1, t2], 4)
                s = s2[:, :, 0:W]
                t = red(S4[:, 0:4], s, ALU.max, t1, t2, t_b)
                t = tt(s, s, bc(S4[:, 0:4], 2, [128, 4, W]), ALU.subtract, t)
                t = af(s, s, ACT.Exp, t)
                t5 = red(S4[:, 4:8], s, ALU.add, t)
                t5 = rcp(S4[:, 8:12], S4[:, 4:8], t5)
                t6 = tt(s, s, bc(S4[:, 8:12], 2, [128, 4, W]), ALU.mult, t5, t)
                bo, fro = g.banks.take()
                ev = []
                for kb in range(qb + 1):
                    b, fr = g.banks.take()
                    if b == bo:
                        b, fr = g.banks.take()
                    for hh in range(4):
                        t = tr(PS[:, b, hh * 128:hh * 128 + 128], s2[:, hh, kb * 128:kb * 128 + 128], t6, fr, inc=hh == 3)
                    a = acp(P2[kb][:, :, :].rearrange("p h q -> p (h q)"), PS[:, b, :], t, tpT)
                    g.banks.give(b, a)
                    ev.append(a)
                tsf = [ev]
                for hh in range(4):
                    h = 4 * j + hh
                    o = PS[(h % 2) * 64:(h % 2) * 64 + 64, bo, (hh // 2) * 128:(hh // 2) * 128 + 128]
                    for kb in range(qb + 1):
                        t = mm(o, v2[:, kb, h * 64:h * 64 + 64], P2[kb][:, hh, :], kb == 0, kb == qb, ev, t_v2, fro,
                               inc=kb == qb)
                tpT = t
                a = acp(a2T[:, 2 * j:2 * j + 2, qb * 128:qb * 128 + 128],
                        PS[:, bo, 0:256].rearrange("p (c q) -> p c q", c=2), t, t_xT)
                g.banks.give(bo, a)
                t_at.append(a)
        t_cat = [hilo(a2h[:, c, :], a2l[:, c, :], a2T[:, c, :], t_at, t_in2) for c in range(4)] + t_pool

        class Cat:

            def __init__(self, a, b):
                self.a, self.b = a, b

            def __getitem__(self, key):
                k = key[1]
                src, k = (self.a, k) if k < 4 else (self.b, k - 4)
                return src[:, k, key[2]]

        t_x3 = []

        def ev_add2(c):
            def f(i, b, t):
                v = x_sb[:, i, c * 512:c * 512 + 512]
                a = tt(v, v, PS[:, b, :], ALU.add, t)
                t_x3.append(a)
                return a
            return f

        for c in range(2):
            t_wo = dense(st, ("wo2", c), 2, "a", Cat(a2h, pTh), Cat(a2l, pTl), t_cat, 4, ev_add2(c))

        t_f2 = ffn("ffn2", f2c, 0.5, [t_x3, t_wo, t_at, tpT, t_cat, tsf])

        t_fn = g.sp.dma(lambda e: e.dma_start(FNB[:, :], I["final_norm_2"].partition_broadcast(128)[:, 0, :]), s_late, t_f2)
        ot = at("ot", 32, [128, NB, D])
        r, a = stats(ot, t_f2)
        s_o = slot("s_o")
        for tb in range(NB):
            t = stt(ot[:, tb, :], x_sb[:, tb, :], rs4[:, tb:tb + 1], FNB[:, :], ALU.mult, ALU.mult, r, a, t_fn)
            t = g.sp.dma(lambda e, tb=tb: e.dma_start(out[0, tb * 128:tb * 128 + 128, :], ot[:, tb, :]), s_o, t)
        g.sp.items.append(("wait", [t, (s_y[0][0], s_y[0][1]), (s_y[1][0], s_y[1][1]), (s_z[0], s_z[1])]))

        def play(e, items):
            for it in items:
                if it[0] == "op":
                    _, waits, fn, inc = it
                    for s, v in waits:
                        e.wait_ge(s, v)
                    ins = fn(e)
                    if inc:
                        ins.then_inc(*inc)
                elif it[0] == "wait":
                    for s, v in it[1]:
                        e.wait_ge(s, v)
                else:
                    _, waits, body, name = it
                    for s, v in waits:
                        e.wait_ge(s, v)
                    r = e.value_load(PI[0:1, 0:1], min_val=0, max_val=T // WIN)
                    with e.If(r > 1):
                        meet(e, name)
                        with e.Fori(1, r):
                            play(e, body)
                            if name == "pool":
                                for q, v in lg_:
                                    e.wait_ge(q, v)
                                e.dma_reset(range(lg_[0][0].num, lg_[-1][0].num + 1))
                            meet(e, name)

        def meet(e, name):
            e.drain().then_inc(bar[0], 1)
            if name == "sp":
                e.wait_ge(bar[0], 5)
                for q in lsems:
                    e.sem_clear(q)
                e.sem_clear(bar[0])
                e.sem_inc(bar[1], 1)
                e.wait_ge(bar[2], 4)
                e.sem_clear(bar[1])
                e.sem_clear(bar[2])
            else:
                e.wait_ge(bar[1], 1)
                e.sem_inc(bar[2], 1)

        blk = ctx.enter_context(nc.Block())

        @blk.sync
        def _(e):
            play(e, g.sp.items)

        @blk.scalar
        def _(e):
            play(e, g.act.items)

        @blk.vector
        def _(e):
            play(e, g.dve.items)

        @blk.gpsimd
        def _(e):
            play(e, g.pool.items)

        @blk.tensor
        def _(e):
            play(e, g.pe.items)


def constants():
    import numpy as np
    p = np.arange(128)
    c = np.zeros((128, NC1), np.float32)

    def put(n, v):
        o, w = CW[n]
        c[:, o:o + w] = v

    put("ident", np.eye(128))
    put("ustrict", p[:, None] < p[None, :])
    put("ones", 1.0)
    put("fold", (p[:, None] % 64) == np.arange(64)[None, :])
    put("iota", np.arange(WIN)[None, :])
    put("cmask", np.where((p[:, None] < 64) & (p[None, :] >= 64), NEG, 0.0))
    put("rc16", np.concatenate([1.0 / np.minimum(np.arange(16) + 1, 2 << i) for i in range(4)])[None, :])
    put("e64", WIN * np.arange(32)[None, :])
    put("step8", (WIN * np.arange(8))[None, :])
    put("dec8", (8 - np.arange(8))[None, :])
    put("invf", (np.float32(500000.0) ** (-np.arange(0, 16, 2, dtype=np.float32) / np.float32(16)))[None, :])
    m1 = np.zeros((128, NC2), np.float32)
    k = np.arange(256)[None, :]
    m1[:, 0:256] = np.where((k <= p[:, None] + 128) & (p[:, None] + 128 - k < 128), 0.0, NEG)
    m1[:, 256:768] = (np.arange(512) % 128 != 0)[None, :]
    mk = np.zeros((128, 8, 128), np.uint32)
    s, t = p[:, None], p[None, :]
    for lv in range(7):
        h = 64 >> lv
        mk[:, lv, :] = (s // (2 * h) == t // (2 * h)) & (s // h % 2 == 0) & (t // h % 2 == 1)
    mk[:, 7, :] = s == t
    return c, m1, mk.reshape(128, NMASK)


NAMES = ["x", "w_in", "hgrn_norm_w", "w_branch_attn", "w_branch_hgrn", "w_out", "norm2_w", "w_gate_experts",
         "w_up_experts", "w_down_experts", "ffn1_w_gate_2", "ffn1_w_up_2", "ffn1_w_down_2", "w_in_2", "q_norm_2", "k_norm_2",
         "pool_w_2", "w_out_2", "ffn2_w_gate_2", "ffn2_w_up_2", "ffn2_w_down_2", "final_norm_2"]


def kernel(**inputs):
    import numpy as np
    import concourse.bacc as bacc
    from concourse.bass_utils import run_bass_kernel_spmd as run

    arrays = {n: np.ascontiguousarray(inputs[n]) for n in NAMES}
    rb = np.ascontiguousarray(inputs["rel_bias_2"])[0]
    rev = np.concatenate([np.repeat(rb[:, 256:257], 127, axis=1), rb[:, 256:0:-1]], axis=1)
    arrays["rel_tile"] = np.ascontiguousarray(np.stack([rev[:, 127 - q:383 - q] for q in range(128)]))
    def cols(n):
        a = np.ascontiguousarray(inputs[n])
        return a.reshape(a.shape[0], -1, 128).transpose(2, 0, 1).reshape(128, -1)

    def rows(a):
        return np.broadcast_to(a.reshape(1, -1), (128, a.size))

    arrays["c_par"] = np.ascontiguousarray(np.concatenate(
        [cols(n) for n in ("norm1_w", "norm2_w", "ffn1_norm_2", "mix_norm_2", "ffn2_norm_2", "pool_scale_2",
                           "hgrn_lower_bounds")]
        + [rows(np.ascontiguousarray(inputs["attn_sinks"])), rows(rb[:, 256])], axis=1))
    arrays["positions"] = np.ascontiguousarray(np.ascontiguousarray(inputs["positions"]).reshape(NB, 128).T)
    arrays["qk_norm"] = np.concatenate([np.ascontiguousarray(inputs["q_norm_w"])] * 8
                                       + [np.ascontiguousarray(inputs["k_norm_w"])] * 2, axis=1)
    wr = np.concatenate([np.ascontiguousarray(inputs["w_router_group"])[0],
                         np.ascontiguousarray(inputs["w_router_expert"])[0]], axis=1)
    arrays["w_router"] = np.ascontiguousarray(wr.reshape(8, 128, 36).transpose(1, 0, 2))
    arrays["b_router"] = np.concatenate([np.ascontiguousarray(inputs["b_router_group"]),
                                         np.ascontiguousarray(inputs["b_router_expert"])], axis=1)
    arrays["c_f32"], arrays["c_m1"], arrays["c_mask"] = constants()
    nc = bacc.Bacc("TRN2", target_bir_lowering=False, num_devices=1)
    I = {n: nc.dram_tensor("in_" + n, a.shape, mybir.dt.from_np(a.dtype), kind="ExternalInput").ap()
         for n, a in arrays.items()}
    out = nc.dram_tensor("out_0", (1, T, D), F32, kind="ExternalOutput").ap()
    program(nc, I, out)
    r = run(nc, [{"in_" + n: a for n, a in arrays.items()}], core_ids=[0])
    return r.results[0]["out_0"]
```

```python
from contextlib import ExitStack

import concourse.bass as bass
from concourse import mybir

ALU = mybir.AluOpType
ACT = mybir.ActivationFunctionType
AX = mybir.AxisListType
F32 = mybir.dt.float32
F32R = mybir.dt.float32r
I32 = mybir.dt.int32
U32 = mybir.dt.uint32

T, D, NB = 512, 1024, 4
EPS = 1e-6
WIN = 64
NE = 32
FF = 512
DFF = 2816
NEG = -1e30

CW = {}
_o = 0
for _n, _w in (("ident", 128), ("ustrict", 128), ("ones", 128), ("fold", 64), ("iota", WIN), ("cmask", 128),
               ("rc16", 64), ("e64", 32), ("step8", 8), ("dec8", 8), ("invf", 8)):
    CW[_n] = (_o, _w)
    _o += _w
NC1 = _o
NC2 = 256 + 512
NMASK = 8 * 128


class Eng:

    def __init__(self, sem):
        self.sem, self.n, self.seen, self.items = sem, 0, {}, []

    def op(self, fn, *deps, inc=True):
        waits = self.waits(deps)
        if inc:
            self.n += 1
        self.items.append(("op", waits, fn, (self.sem, 1) if inc else None))
        return (self.sem, self.n) if inc else None

    def dma(self, fn, slot, *deps):
        waits = self.waits(deps)
        slot[1] += 16
        self.items.append(("op", waits, fn, (slot[0], 16)))
        return (slot[0], slot[1])

    def waits(self, deps):
        out = []
        stack = list(deps)
        need = {}
        while stack:
            d = stack.pop()
            if d is None:
                continue
            if isinstance(d, list):
                stack.extend(d)
                continue
            s, v = d
            if need.get(id(s), (s, 0))[1] < v:
                need[id(s)] = (s, v)
        for k, (s, v) in need.items():
            if self.seen.get(k, 0) < v:
                self.seen[k] = v
                out.append((s, v))
        return out


class Banks:

    def __init__(self):
        self.free = [None] * 8
        self.held = [False] * 8
        self.at = 0
        self.lo, self.hi = 0, 8

    def span(self, lo, hi):
        self.lo, self.hi, self.at = lo, hi, lo

    def take(self, n=1):
        for _ in range(16):
            b = self.at
            if b % n == 0 and b + n <= self.hi and not any(self.held[b:b + n]):
                break
            self.at = self.at + 1 if self.at + 1 < self.hi else self.lo
        else:
            raise ValueError("no bank is free")
        self.at = b + n if b + n < self.hi else self.lo
        return self.hold(b, n)

    def hold(self, b, n=1):
        for i in range(b, b + n):
            assert not self.held[i]
            self.held[i] = True
        return b, [self.free[b + i] for i in range(n)]

    def give(self, b, tok, n=1):
        for i in range(n):
            self.free[b + i] = tok
            self.held[b + i] = False


class Stream:

    def __init__(self, g, plan, slots, raw, hi, lo, pool_part, raw_first=None, hl_first=None):
        self.g, self.plan, self.slots = g, plan, slots
        self.raw, self.hi, self.lo = raw, hi, lo
        self.nr, self.nh = len(raw), len(hi)
        self.loaded = self.split = self.taken = 0
        self.fence = len(plan)
        self.ld, self.sp, self.dn = {}, {}, {}
        self.pool_part = pool_part
        for u in range(self.nr):
            self.sp[u - self.nr] = raw_first[u] if raw_first else None
        for u in range(self.nh):
            self.dn[u - self.nh] = hl_first[u] if hl_first else None

    def load_to(self, j):
        while self.loaded < min(j, self.fence):
            u = self.loaded
            _, src, kc, n = self.plan[u]
            r = self.raw[u % self.nr]
            dst = r[:, 0:kc * n].rearrange("p (k n) -> p k n", k=kc)
            self.ld[u] = self.g.sp.dma(lambda e, dst=dst, src=src: e.dma_start(dst, src), self.slots[u % self.nr],
                                       self.sp.get(u - self.nr))
            self.loaded += 1

    def split_to(self, j):
        while self.split < min(j, self.fence):
            u = self.split
            self.load_to(u + 1)
            _, _, kc, n = self.plan[u]
            w = kc * n
            r, h, l = self.raw[u % self.nr], self.hi[u % self.nh], self.lo[u % self.nh]
            t = self.g.act.op(lambda e, h=h, r=r, w=w: e.copy(h[:, 0:w], r[:, 0:w]), self.ld[u], self.dn.get(u - self.nh))
            c = w - int(w * self.pool_part) // 128 * 128
            a = self.g.dve.op(lambda e, h=h, r=r, l=l, c=c: e.tensor_tensor(l[:, 0:c], r[:, 0:c], h[:, 0:c].bitcast(F32),
                                                                                ALU.subtract),
                              t, self.ld[u], self.dn.get(u - self.nh))
            b = None
            if c < w:
                b = self.g.pool.op(lambda e, h=h, r=r, l=l, c=c, w=w: e.tensor_tensor(l[:, c:w], r[:, c:w], h[:, c:w].bitcast(F32),
                                                             ALU.subtract), t, self.ld[u], self.dn.get(u - self.nh))
            self.sp[u] = [t, a, b]
            self.split += 1
            self.load_to(u + 1 + self.nr)

    def take(self, key):
        u = self.taken
        assert self.plan[u][0] == key, (self.plan[u][0], key)
        self.split_to(u + self.nh)
        self.taken += 1
        _, _, kc, n = self.plan[u]
        h = self.hi[u % self.nh][:, 0:kc * n].rearrange("p (k n) -> p k n", k=kc)
        l = self.lo[u % self.nh][:, 0:kc * n].rearrange("p (k n) -> p k n", k=kc)
        return u, h, l, self.sp[u]

    def done(self, u, tok):
        self.dn[u] = tok

    def raw_end(self, i):
        return self.sp[max(u for u in range(-self.nr, len(self.plan)) if u % self.nr == i)]

    def hl_end(self, i):
        return self.dn[max(u for u in range(-self.nh, len(self.plan)) if u % self.nh == i)]


def units(key, w, k0, k1, c0, c1):
    out = []
    for k in range(k0, k1, 4):
        e = min(k + 4, k1)
        out.append((key, w[k * 128:e * 128, c0:c1].rearrange("(k p) n -> p k n", p=128), e - k, c1 - c0))
    return out


class G:
    pass


def make_plan_moe(I):
    plan = []

    def gu(e):
        plan.extend(units(("g", e), I["w_gate_experts"][0, e], 0, 8, 0, FF))
        plan.extend(units(("u", e), I["w_up_experts"][0, e], 0, 8, 0, FF))

    def dn(e):
        for c in range(2):
            plan.extend(units(("d", e), I["w_down_experts"][0, e], 0, 4, c * 512, c * 512 + 512))

    gu(0)
    for e in range(NE):
        if e + 1 < NE:
            gu(e + 1)
        dn(e)
    return plan


FCUTS = [(0, 512), (512, 1024), (1024, 1408)]


def make_plan_ffn(I, pre):
    plan = []
    for half in range(2):
        o = half * 1408
        for i, (a, b) in enumerate(FCUTS):
            plan.extend(units((pre, "g", half, i), I[pre + "_w_gate_2"][0], 0, 8, o + a, o + b))
            plan.extend(units((pre, "u", half, i), I[pre + "_w_up_2"][0], 0, 8, o + a, o + b))
        for c in range(2):
            plan.extend(units((pre, "d", half, c), I[pre + "_w_down_2"][0], half * 11, half * 11 + 11,
                              c * 512, c * 512 + 512))
    return plan


INP = [("qa", 0, 512), ("kv", 512, 768), ("qh", 768, 1280), ("fh", 1280, 1792), ("ih", 1792, 2304),
       ("gh", 2304, 2816), ("za0", 2816, 3328), ("za1", 3328, 3840), ("zb0", 3840, 4352), ("zb1", 4352, 4864)]


def make_plan(I):
    p1 = []
    for n, a, b in INP:
        p1.extend(units(n, I["w_in"][0], 0, 8, a, b))
    for c in range(2):
        p1.extend(units(("ba", c), I["w_branch_attn"][0], 0, 4, c * 512, c * 512 + 512))
        p1.extend(units(("bh", c), I["w_branch_hgrn"][0], 0, 4, c * 512, c * 512 + 512))
    for c in range(2):
        p1.extend(units(("wo", c), I["w_out"][0], 0, 8, c * 512, c * 512 + 512))
    p2 = make_plan_moe(I)
    p3 = make_plan_ffn(I, "ffn1")
    for c in range(4):
        p3.extend(units(("in2", c), I["w_in_2"][0], 0, 8, c * 512, c * 512 + 512))
    for c in range(2):
        p3.extend(units(("wo2", c), I["w_out_2"][0], 0, 8, c * 512, c * 512 + 512))
    p3.extend(make_plan_ffn(I, "ffn2"))
    return p1, p2, p3


def program(nc, I, out):
    ctx = ExitStack()
    g = G()
    base = (nc.sbuf_base + 127) // 128 * 128
    end = nc.sbuf_usable_end
    KB = 1024
    ring = base
    arena = base + 64 * KB

    def at(name, off, shape, dt=F32):
        n = 4
        for s in shape[1:]:
            n *= s
        o = arena + int(off * KB)
        assert o % 32 == 0 and o + n <= end, (name, off, n, end - arena)
        return nc.alloc_sbuf_tensor_at(name, shape, dt, offset=o)

    with ctx:
        def sem(name):
            return ctx.enter_context(nc.semaphore(name))

        def slot(name):
            return [sem(name), 0]

        PS = ctx.enter_context(nc.psum_tensor("PS", [128, 8, 512], F32))
        raw = [nc.alloc_sbuf_tensor_at(f"raw{i}", [128, 2048], F32, offset=ring + i * 8 * KB) for i in range(4)]
        hi = [nc.alloc_sbuf_tensor_at(f"hi{i}", [128, 2048], F32R, offset=ring + (4 + i) * 8 * KB) for i in range(2)]
        lo = [nc.alloc_sbuf_tensor_at(f"lo{i}", [128, 2048], F32R, offset=ring + (6 + i) * 8 * KB) for i in range(2)]
        spare = ring + 24 * KB
        rawx = at("rawx", 21, [128, 2048])
        hix, lox = at("hix", 117.5, [128, 2048], F32R), at("lox", 125.5, [128, 2048], F32R)

        zsp = nc.dram_tensor("zsp", [16, 128, 512], F32)
        ysp = nc.dram_tensor("ysp", [NE * WIN, D], F32)

        x_sb = at("x_sb", 0, [128, NB, D])
        C1 = at("C1", 16, [128, NC1])
        SM = at("SM", 19.25, [128, 176])

        def cst(n):
            o, w = CW[n]
            return C1[:, o:o + w]

        ident, ones, fold = cst("ident"), cst("ones"), cst("fold")
        n1c, n2c, f1c, mxc, f2c = (SM[:, 8 * i:8 * i + 8] for i in range(5))
        psc = SM[:, 40:44]
        lbr = SM[:, 44:52]
        sink = SM[:, 52:60]
        bfar = SM[:, 60:68]
        lbs = SM[:, 68:92]
        ss4, ms4, sd4, rs4 = (SM[:, 92 + 4 * i:96 + 4 * i] for i in range(4))
        gw = SM[:, 108:116]
        rk = SM[:, 116:124]
        ek = SM[:, 124:132]
        wt = SM[:, 132:140]
        rc1 = SM[:, 140:148]
        rc2 = SM[:, 148:156]
        SI = at("SI", 20.0, [128, 16], U32)
        PI = at("PI", 20.0625, [128, 8], I32)

        s_pe, s_act, s_dve, s_pool, s_sp = (sem("s_" + n) for n in ("pe", "act", "dve", "pool", "sp"))
        g.pe, g.act, g.dve, g.pool, g.sp = Eng(s_pe), Eng(s_act), Eng(s_dve), Eng(s_pool), Eng(s_sp)
        g.banks = Banks()
        engs = ("pe", "act", "dve", "pool", "sp")
        wslots = [slot(f"s_w{i}") for i in range(4)]
        mslots = [slot(f"s_m{i}") for i in range(5)]
        s_const = slot("s_const")
        s_late = slot("s_late")
        s_xin = [slot(f"s_xin{i}") for i in range(NB)]

        pe = lambda *a, **k: g.pe.op(*a, **k)
        act = lambda *a, **k: g.act.op(*a, **k)
        dve = lambda *a, **k: g.dve.op(*a, **k)
        pool = lambda *a, **k: g.pool.op(*a, **k)

        def mm(o, l, r, st, sp, *deps, inc=False):
            return pe(lambda e: e.matmul(o, l, r, start=st, stop=sp), *deps, inc=inc)

        def tr(o, i, *deps, inc=False):
            return pe(lambda e: e.transpose(o, i, ident), *deps, inc=inc)

        def tt(o, a, b, op, *deps, on=dve):
            return on(lambda e: e.tensor_tensor(o, a, b, op), *deps)

        def ts(o, a, s1, s2, op0, op1, *deps, on=dve):
            if op1 is None:
                return on(lambda e: e.tensor_scalar(o, a, s1, None, op0), *deps)
            return on(lambda e: e.tensor_scalar(o, a, s1, s2, op0, op1), *deps)

        def stt(o, a, s, b, op0, op1, *deps):
            return dve(lambda e: e.scalar_tensor_tensor(out=o, in0=a, scalar=s, in1=b, op0=op0, op1=op1), *deps)

        def af(o, i, f, *deps, scale=1.0, bias=0.0, acc=None):
            if acc is not None:
                return act(lambda e: e.activation(o, i, f, bias=bias, scale=scale, accum_out=acc), *deps)
            return act(lambda e: e.activation(o, i, f, bias=bias, scale=scale), *deps)

        def red(o, i, op, *deps):
            return dve(lambda e: e.tensor_reduce(o, i, AX.X, op), *deps)

        def cp(o, i, *deps):
            return dve(lambda e: e.tensor_copy(o, i), *deps)

        def acp(o, i, *deps):
            return act(lambda e: e.copy(o, i), *deps)

        def rcp(o, i, *deps):
            return dve(lambda e: e.reciprocal(o, i), *deps)

        def bc(a, axis, shape):
            return a.unsqueeze(axis).broadcast_to(shape)

        def hilo(h, l, src, *deps):
            a = acp(h, src, *deps)
            b = tt(l, src, h.bitcast(F32), ALU.subtract, a, *deps)
            return [a, b]

        M1 = at("M1", 21, [128, NC2])
        MK = at("MK", 24, [128, NMASK], U32)
        WQK = at("WQK", 28, [128, 10, 64])
        HNW = at("HNW", 30.5, [128, 128])
        POS = at("POS", 31, [128, 4], I32)

        def cdma(dst, src, s=None):
            return g.sp.dma(lambda e: e.dma_start(dst, src), s or s_const)

        for tb in range(NB):
            cdma(x_sb[:, tb, :], I["x"][0, tb * 128:tb * 128 + 128, :], s_xin[tb])
        t_xin = [(q[0], q[1]) for q in s_xin]
        s_first = slot("s_first")
        cdma(C1[:, :], I["c_f32"], s_first)
        cdma(SM[:, 0:68], I["c_par"], s_first)
        t_c0 = (s_first[0], s_first[1])
        wplan, wplan2, wplan3 = make_plan(I)
        st = Stream(g, wplan, wslots[0:3], raw[0:3], hi, lo, 0.0)
        st.load_to(3)
        cdma(M1[:, :], I["c_m1"])
        cdma(MK[:, :], I["c_mask"])
        cdma(POS[:, :], I["positions"])
        cdma(WQK[:, :, :].rearrange("p h d -> p (h d)"), I["qk_norm"].partition_broadcast(128)[:, 0, :])
        cdma(HNW[:, :], I["hgrn_norm_w"].partition_broadcast(128)[:, 0, :])
        t_c = [(s_const[0], s_const[1]), t_c0]

        def norm_steps(xs, tx, *deps):
            for tb in range(NB):
                c = slice(tb, tb + 1)
                a = af(xs[:, tb, :], x_sb[:, tb, :], ACT.Square, tx[tb], *deps, acc=ss4[:, c])
                b = ts(ms4[:, c], ss4[:, c], 1.0 / D, EPS, ALU.mult, ALU.add, a)
                b = af(sd4[:, c], ms4[:, c], ACT.Sqrt, b)
                yield tb, [rcp(rs4[:, c], sd4[:, c], b), a]

        def transposed(xs, toks, evac):
            fr = {c: g.banks.hold(c)[1] for c in range(8)}
            for tb in range(NB):
                for c in range(8):
                    t = tr(PS[:, c, tb * 128:tb * 128 + 128], xs[:, tb, c * 128:c * 128 + 128], toks[tb],
                           fr[c] if tb == 0 else None, t_c0, inc=tb == 3)
                    if tb == 3:
                        fr[c] = t
            for c in range(8):
                g.banks.give(c, evac(c, fr[c]))

        def norm_t(xs, wcol, th, tl, tx, *deps):
            b = [ts(xs[:, tb, :], x_sb[:, tb, :], rs4[:, tb:tb + 1], None, ALU.mult, None, r)
                 for tb, r in norm_steps(xs, tx, *deps)]
            toks = []

            def evac(c, t):
                h = af(th[:, c, :], PS[:, c, :], ACT.Copy, t, t_c0, *deps, scale=wcol[:, c:c + 1])
                l = stt(tl[:, c, :], PS[:, c, :], wcol[:, c:c + 1], th[:, c, :].bitcast(F32), ALU.mult, ALU.subtract,
                        h, *deps)
                toks.append([h, l])
                return [h, l]

            transposed(xs, b, evac)
            return toks

        def dense_steps(st, key, nu, orient, xh, xl, xdeps, nbk, evac):
            k0 = 0
            for ui in range(nu):
                u, h, l, tok = st.take(key)
                kc = h.shape[1]
                for i in range(nbk):
                    n = h.shape[2] if orient == "a" else 512
                    fr = g.banks.hold(i)[1] if ui == 0 else None
                    o = PS[:, i, 0:n]
                    for kk in range(kc):
                        k = k0 + kk
                        s0 = ui == 0 and kk == 0
                        s1 = ui == nu - 1 and kk == kc - 1
                        dp = [tok, fr if s0 else None, xdeps[k]]
                        if orient == "a":
                            xa, xb = xh[:, k, i * 128:i * 128 + 128], xl[:, k, i * 128:i * 128 + 128]
                            mm(o, xa, h[:, kk, :], s0, False, dp)
                            mm(o, xa, l[:, kk, :], False, False)
                            t = mm(o, xb, h[:, kk, :], False, s1, inc=kk == kc - 1)
                        else:
                            wh, wl = h[:, kk, i * 128:i * 128 + 128], l[:, kk, i * 128:i * 128 + 128]
                            mm(o, wh, xh[:, k, :], s0, False, dp)
                            mm(o, wh, xl[:, k, :], False, False)
                            t = mm(o, wl, xh[:, k, :], False, s1, inc=kk == kc - 1)
                    if i == nbk - 1:
                        st.done(u, t)
                    if ui == nu - 1:
                        g.banks.give(i, evac(i, i, t))
                    g.last = t
                    yield
                k0 += kc

        def dense(*a):
            for _ in dense_steps(*a):
                pass
            return g.last

        def interleave(main, side):
            for n in side:
                for _ in range(n):
                    next(main, None)

        def chain(*gens):
            for ge in gens:
                yield from ge

        xs = at("xs", 64, [128, NB, D])
        xTh, xTl = at("xTh", 32, [128, 8, T], F32R), at("xTl", 48, [128, 8, T], F32R)
        t_xT = norm_t(xs, n1c, xTh, xTl, t_xin)
        t_xs_dead = t_xT

        qkn = at("qkn", 96, [128, NB, 10, 64])
        vn = at("vn", 106, [128, NB, 128])
        qT = at("qT", 108, [128, 4, T])
        kT = at("kT", 116, [128, 2, T])
        sA = [at("sA0", 120, [128, 4, 256]), at("sA1", 124, [128, 4, 256])]
        kd = at("kd", 120, [128, NB, 2, 128])
        pTb = [at("pTb0", 128, [128, 2, 4, 128]), nc.alloc_sbuf_tensor_at("pTb1", [128, 2, 4, 128], F32, offset=spare)]
        attnT = at("attnT", 132, [128, 4, T])
        stg = [at("stg0", 140, [128, 512]), nc.alloc_sbuf_tensor_at("stg1", [128, 512], F32, offset=spare + 4 * KB)]
        sq = at("sq", 116, [128, 2, 640])

        RP = at("RP", 31.125, [128, 4, 8])
        ANG, KF, CS, SN = (at(n, 128 + 0.125 * i, [128, 4, 8]) for i, n in enumerate(("ANG", "KF", "CSt", "SNt")))
        COS, SIN = at("COS", 31.25, [128, 4, 8]), at("SIN", 31.375, [128, 4, 8])
        KI = at("KI", 128.5, [128, 4, 8], I32)
        PF = at("PF", 128.625, [128, 4])
        t = cp(PF[:, :], POS[:, :], t_c)
        t = tt(ANG[:, :, :], bc(PF[:, :], 2, [128, 4, 8]), bc(cst("invf"), 1, [128, 4, 8]), ALU.mult, t, t_c)
        t = ts(KF[:, :, :], ANG[:, :, :], 0.15915494309189535, None, ALU.mult, None, t)
        t = cp(KI[:, :, :], KF[:, :, :], t)
        t = cp(KF[:, :, :], KI[:, :, :], t)
        for cc in (-6.28125, -0.0019350051879882812, -3.0199159819567876e-07):
            t = stt(ANG[:, :, :], KF[:, :, :], cc, ANG[:, :, :], ALU.mult, ALU.add, t)
        t = ts(SN[:, :, :], ANG[:, :, :], 3.1415925, -3.1415925, ALU.min, ALU.max, t)
        t2 = ts(CS[:, :, :], ANG[:, :, :], 1.5707963267948966, None, ALU.add, None, t)
        t2 = ts(KF[:, :, :], CS[:, :, :], 3.141592653589793, -6.283185307179586, ALU.is_gt, ALU.mult, t2)
        t2 = tt(CS[:, :, :], CS[:, :, :], KF[:, :, :], ALU.add, t2)
        t2 = ts(CS[:, :, :], CS[:, :, :], 3.1415925, -3.1415925, ALU.min, ALU.max, t2)
        t_rope = [af(SIN[:, :, :], SN[:, :, :], ACT.Sin, t), af(COS[:, :, :], CS[:, :, :], ACT.Sin, t2)]

        l0, l1 = lbr[:, 0:4], lbr[:, 4:8]
        lm, le0, le1, lsum, lb, oml = (lbs[:, 4 * i:4 * i + 4] for i in range(6))
        t = tt(lm, l0, l1, ALU.max, t_c)
        ta = tt(le0, l0, lm, ALU.subtract, t)
        tb_ = tt(le1, l1, lm, ALU.subtract, t)
        ta = af(le0, le0, ACT.Exp, ta)
        tb_ = af(le1, le1, ACT.Exp, tb_)
        t = tt(lsum, le0, le1, ALU.add, ta, tb_)
        t = rcp(lsum, lsum, t)
        t = tt(lb, le0, lsum, ALU.mult, t)
        t_lb = ts(oml, lb, -1.0, 1.0, ALU.mult, ALU.add, t)

        t_q, t_v = [], []

        def ev_q(i, b, t):
            a = cp(qkn[:, i, 0:8, :].rearrange("p h d -> p (h d)"), PS[:, b, :], t)
            t_q.append(a)
            return a

        def ev_kv(i, b, t):
            a = acp(qkn[:, i, 8:10, :].rearrange("p h d -> p (h d)"), PS[:, b, 0:128], t)
            c = acp(vn[:, i, :], PS[:, b, 128:256], t)
            t_q.append(a)
            t_v.append(c)
            return [a, c]

        dense(st, "qa", 2, "a", xTh, xTl, t_xT, 4, ev_q)
        dense(st, "kv", 2, "a", xTh, xTl, t_xT, 4, ev_kv)

        QS = at("QS", 31.5, [128, 40])
        amask = M1[:, 0:256]
        SS = at("SS", 31.75, [128, 40])
        t_at = []

        def attention():
            t_ss = []
            t_prev = [None, None]
            for i in range(NB):
                a = af(sq[:, i % 2, :], qkn[:, i, :, :].rearrange("p h d -> p (h d)"), ACT.Square, t_q, t_prev[i % 2])
                r = red(QS[:, i * 10:i * 10 + 10], sq[:, i % 2, :].rearrange("p (h d) -> p h d", h=10), ALU.add, a)
                t_prev[i % 2] = r
                t_ss.append(r)
            t = ts(QS[:, :], QS[:, :], 1.0 / 64, EPS, ALU.mult, ALU.add, t_ss)
            t = af(QS[:, :], QS[:, :], ACT.Sqrt, t)
            t = rcp(QS[:, :], QS[:, :], t)
            t_n = []
            for i in range(NB):
                a = tt(qkn[:, i, :, :], qkn[:, i, :, :], bc(QS[:, i * 10:i * 10 + 10], 2, [128, 10, 64]), ALU.mult, t, t_q)
                t_n.append(tt(qkn[:, i, :, :], qkn[:, i, :, :], WQK[:, :, :], ALU.mult, a, t_c))
            R = [at(f"R{i}", 120 + 1.25 * i, [128, 4, 10, 8]) for i in range(4)]
            x1, x2 = qkn[:, :, :, 0:8], qkn[:, :, :, 8:16]
            cb = bc(COS[:, :, :], 2, [128, 4, 10, 8])
            sb_ = bc(SIN[:, :, :], 2, [128, 4, 10, 8])
            a1 = tt(R[0][:, :, :, :], x1, cb, ALU.mult, t_n, t_rope)
            a2 = tt(R[1][:, :, :, :], x2, sb_, ALU.mult, t_n, t_rope)
            a3 = tt(R[2][:, :, :, :], x2, cb, ALU.mult, t_n)
            a4 = tt(R[3][:, :, :, :], x1, sb_, ALU.mult, t_n)
            b1 = tt(x1, R[0][:, :, :, :], R[1][:, :, :, :], ALU.subtract, a1, a2, a4)
            b2 = tt(x2, R[2][:, :, :, :], R[3][:, :, :, :], ALU.add, a3, a4, a2)
            t_r = [b1, b2]
            t_kd = []
            for i in range(NB):
                for rep in range(2):
                    t_kd.append(cp(kd[:, i, :, rep * 64:rep * 64 + 64], qkn[:, i, 8:10, :], t_r))
            t_qT = []
            yield 6
            for j in range(4):
                b, fr = g.banks.take()
                for i in range(NB):
                    t = tr(PS[:, b, i * 128:i * 128 + 128], qkn[:, i, 2 * j:2 * j + 2, :].rearrange("p h d -> p (h d)"),
                           t_r, fr, inc=i == 3)
                a = acp(qT[:, j, :], PS[:, b, :], t)
                g.banks.give(b, a)
                t_qT.append(a)
            for j in range(2):
                b, fr = g.banks.take()
                for i in range(NB):
                    t = tr(PS[:, b, i * 128:i * 128 + 128], kd[:, i, j, :], t_kd, fr, inc=i == 3)
                a = acp(kT[:, j, :], PS[:, b, :], t, t_ss)
                g.banks.give(b, a)
                t_qT.append(a)
            yield 1
            t_sfree = [t_qT, t_qT]
            t_pT = [None, None]

            def scores(it):
                n, j = it // 2, it % 2
                W = 256 if n else 128
                k0 = (n - 1) * 128 if n else 0
                s = sA[it % 2][:, :, 0:W]
                c = SS[:, 20 * (it % 2):20 * (it % 2) + 20]
                mx, es, l, nm = c[:, 0:4], c[:, 4:8], c[:, 8:12], c[:, 12:16]
                b, fr = g.banks.take(2)
                for par in range(2):
                    for jj in range(2):
                        pr = 2 * j + jj
                        t = mm(PS[:, b + par, jj * 256:jj * 256 + W], qT[par * 64:par * 64 + 64, pr, n * 128:n * 128 + 128],
                               kT[par * 64:par * 64 + 64, j, k0:k0 + W], True, True, t_qT, fr, inc=jj == 1)
                pv = PS[:, b:b + 2, :].rearrange("p b (c w) -> p (b c) w", w=256)[:, :, 0:W]
                so = sink[:, 4 * j:4 * j + 4].rearrange("p (c e) -> p e c", e=2)
                t = stt(s, pv, 0.125, bc(amask[:, 256 - W:256], 1, [128, 4, W]), ALU.mult, ALU.add, t, t_c,
                        t_sfree[it % 2])
                g.banks.give(b, t, 2)
                t2 = red(mx, s, ALU.max, t)
                t2 = tt(mx.rearrange("p (e c) -> p e c", e=2), mx.rearrange("p (e c) -> p e c", e=2), so, ALU.max, t2)
                t4 = tt(es.rearrange("p (e c) -> p e c", e=2), so, mx.rearrange("p (e c) -> p e c", e=2), ALU.subtract, t2)
                t3 = ts(nm, mx, -1.0, None, ALU.mult, None, t2)
                te = [af(s[:, q, :], s[:, q, :], ACT.Exp, t3, t, bias=nm[:, q:q + 1], acc=l[:, q:q + 1]) for q in range(4)]
                te.append(af(es, es, ACT.Exp, t4))
                return n, j, W, s, c, te

            def weights(st_):
                n, j, W, s, c, te = st_
                it = 2 * n + j
                t5 = tt(c[:, 8:12], c[:, 8:12], c[:, 4:8], ALU.add, te)
                t5 = rcp(c[:, 16:20], c[:, 8:12], t5)
                t6 = tt(s, s, bc(c[:, 16:20], 2, [128, 4, W]), ALU.mult, t5, te)
                ev = []
                for kb in range(W // 128):
                    b, fr = g.banks.take()
                    for hh in range(4):
                        t = tr(PS[:, b, hh * 128:hh * 128 + 128], s[:, hh, kb * 128:kb * 128 + 128], t6, fr, inc=hh == 3)
                    a = acp(pTb[it % 2][:, kb, :, :].rearrange("p h q -> p (h q)"), PS[:, b, :], t, t_pT[it % 2])
                    g.banks.give(b, a)
                    ev.append(a)
                t_sfree[it % 2] = ev
                return ev

            def values(st_, ev):
                n, j, W, s, c, te = st_
                it, nkb = 2 * n + j, W // 128
                b, fr = g.banks.take()
                for par in range(2):
                    for kb in range(nkb):
                        t = mm(PS[par * 64:par * 64 + 64, b, 0:256], vn[:, n - nkb + 1 + kb, j * 64:j * 64 + 64],
                               pTb[it % 2][:, kb, 2 * par:2 * par + 2, :].rearrange("p h q -> p (h q)"), kb == 0,
                               kb == nkb - 1, ev, t_v, fr, inc=kb == nkb - 1)
                t_pT[it % 2] = t
                a = acp(attnT[:, 2 * j:2 * j + 2, n * 128:n * 128 + 128],
                        PS[:, b, 0:256].rearrange("p (c q) -> p c q", c=2), t)
                g.banks.give(b, a)
                t_at.extend([a, t])

            sc, ev = {}, {}
            for it in range(10):
                if it < 8:
                    sc[it] = scores(it)
                    yield 1
                if 0 <= it - 1 < 8:
                    ev[it - 1] = weights(sc[it - 1])
                if it >= 2:
                    values(sc[it - 2], ev[it - 2])
                yield 1

        qh, bb = at("qh", 64, [128, 4, T]), at("bb", 72, [128, 4, T])
        kh, vh = at("kh", 80, [128, 4, T]), at("vh", 88, [128, NB, 512])
        t_qh, t_fg, t_vh = {}, {}, []

        def ev_qh(i, b, t):
            t_qh[i] = af(qh[:, i, :], PS[:, b, :], ACT.Silu, t, t_xs_dead)
            return t_qh[i]

        def ev_fh(i, b, t):
            t_fg[i] = acp(bb[:, i, :], PS[:, b, :], t, t_xs_dead)
            return t_fg[i]

        def ev_vh(i, b, t):
            t_vh.append(acp(vh[:, i, :], PS[:, b, :], t))
            return t_vh[-1]


        gs = at("gs", 124, [128, NB, 512])
        t_gs = []

        def ev_gh(i, b, t):
            t_gs.append(acp(gs[:, i, :], PS[:, b, :], t, t_attn))
            return t_gs[-1]

        s_z = [slot("s_z0"), slot("s_z1")]
        t_z = [None, None]
        zi = [0]

        def ev_z(i, b, t):
            c = zi[0]
            zi[0] += 1
            sg = stg[c % 2]
            a = acp(sg[:, :], PS[:, b, :], t, t_z[c % 2])
            t_z[c % 2] = g.act.dma(lambda e: e.dma_start(zsp[c, :, :], sg[:, :]), s_z[c % 2], a)
            return a

        g.banks.span(4, 8)
        evs = {"qh": ev_qh, "fh": ev_fh, "ih": ev_vh, "gh": ev_gh}
        inproj = chain(*[dense_steps(st, n, 2, "a" if n in ("ih", "gh") else "b", xTh, xTl, t_xT, 4, evs.get(n, ev_z))
                         for n, _, _ in INP[2:]])
        interleave(inproj, attention())
        t_attn = list(t_at)

        def hgrn():
            E = [at("E0", 96, [128, T]), at("E1", 98, [128, T])]
            QE = [at("QE0", 100, [128, T]), at("QE1", 102, [128, T])]
            KE = [at("KE0", 104, [128, T]), at("KE1", 106, [128, T])]
            AT = [at("AT0", 108, [128, T]), at("AT1", 110, [128, T])]
            ho = at("ho", 112, [128, 4, NB, 128])
            St = at("St", 120, [128, 128])
            QB = at("QB", 120.5, [128, T])
            KN = at("KN", 122.5, [128, 3, 128])
            TK = nc.alloc_sbuf_tensor_at("TK", [128, T], F32, offset=spare)
            hss = at("hss", 31.5, [128, 16])
            eb = at("eb", 31.5625, [128, 4])
            z = [dve(lambda e, A=A: e.memset(A[:, :], 0.0), t_attn) for A in AT]
            t_ho = []
            tE, tQ, tK, tA = [None, None], [None, None], [None, None], [z[0], z[1]]
            tsg = [af(bb[:, h, :], bb[:, h, :], ACT.Sigmoid, t_fg[h]) for h in range(4)]
            for h in range(4):
                t_fg[h] = ts(bb[:, h, :], bb[:, h, :], oml[:, h:h + 1], lb[:, h:h + 1], ALU.mult, ALU.add, tsg[h], t_lb)
            lns = [af(kh[:, h, :], bb[:, h, :], ACT.Ln, t_fg[h]) for h in range(4)]
            scans, kks = [], []
            for h in range(4):
                tk = af(E[h % 2][:, :], bb[:, h, :], ACT.Copy, t_fg[h], lns[h], t_attn, tE[h % 2], scale=-1.0, bias=1.0)
                t = dve(lambda e, h=h: e.tensor_tensor_scan(bb[:, h, :], M1[:, 256:768], kh[:, h, :], 0.0, ALU.mult, ALU.add),
                        lns[h], t_c, tk)
                tc_ = cp(kh[:, h, :], E[h % 2][:, :], tk, t)
                tE[h % 2] = tc_
                scans.append(t)
                kks.append(tc_)
            yield 3

            def decay(h, lv, p):
                e_ = E[p]
                hw = 64 >> lv
                nb = T // (2 * hw)
                bv = bb[:, h, :].rearrange("p (n w) -> p n w", w=2 * hw)
                t = tt(e_[:, :].rearrange("p (n w) -> p n w", w=2 * hw), bv,
                       bv[:, :, hw - 1:hw].broadcast_to([128, nb, 2 * hw]), ALU.subtract, scans[h], kks[h], tE[p])
                t = af(e_[:, :], e_[:, :], ACT.Abs, t)
                return af(e_[:, :], e_[:, :], ACT.Exp, t, scale=-1.0)

            def scaled(h, lv, p, td):
                if lv == 7:
                    return qh[:, h, :], kh[:, h, :], [t_qh[h], kks[h]]
                q_, k_ = QE[p], KE[p]
                tk = tt(k_[:, :], kh[:, h, :], E[p][:, :], ALU.mult, td, kks[h], tK[p], on=pool)
                tq = tt(q_[:, :], qh[:, h, :], E[p][:, :], ALU.mult, td, t_qh[h], tQ[p])
                tE[p] = [tq, tk]
                return q_[:, :], k_[:, :], [tq, tk]

            def products(h, lv, p, qs, ks, tq):
                b, fr = g.banks.take()
                for c in range(4):
                    t = mm(PS[:, b, c * 128:c * 128 + 128], ks[:, c * 128:c * 128 + 128], qs[:, c * 128:c * 128 + 128],
                           True, True, tq, fr, inc=c == 3)
                if lv < 7:
                    tQ[p] = tK[p] = t
                return b, t

            def place(h, lv, b, t):
                av = AT[h % 2][:, :].rearrange("p (c t) -> p c t", c=4)
                a = dve(lambda e: e.copy_predicated(
                    av, bc(MK[:, lv * 128:lv * 128 + 128], 1, [128, 4, 128]),
                    PS[:, b, :].rearrange("p (c t) -> p c t", c=4)), t, tA[h % 2], t_c)
                g.banks.give(b, a)
                tA[h % 2] = a

            s_free = [None, None, None, None]

            hTh, hTl = at("hTh", 64, [128, 4, T], F32R), at("hTl", 72, [128, 4, T], F32R)
            g.t_hT = []

            def gates():
                for i in range(NB):
                    a = af(gs[:, i, :], gs[:, i, :], ACT.Silu, t_gs[i])
                    v = gs[:, i, :].rearrange("p (h v) -> p h v", h=4)
                    t_gs[i] = tt(v, v, bc(HNW[:, :], 1, [128, 4, 128]), ALU.mult, a, t_c, on=pool)

            def tail(h):
                AH = AT[h % 2]
                b3 = bb[:, h, :]
                tb0 = [scans[h], kks[h]]
                t1 = af(QB[:, :], b3, ACT.Exp, tb0, s_free[0])
                bv = b3.rearrange("p (n w) -> p n w", w=128)
                t = tt(TK[:, :].rearrange("p (n w) -> p n w", w=128), bv, bv[:, :, 127:128].broadcast_to([128, 4, 128]),
                       ALU.subtract, tb0, s_free[1])
                t = af(TK[:, :], TK[:, :], ACT.Exp, t, scale=-1.0)
                te = af(eb[:, :], bv[:, :, 127], ACT.Exp, tb0, s_free[3])
                t1 = tt(QB[:, :], QB[:, :], qh[:, h, :], ALU.mult, t1, on=pool)
                t = tt(TK[:, :], TK[:, :], kh[:, h, :], ALU.mult, t, on=pool)
                yield 1
                yield 1
                b, fr = g.banks.take()
                for c in range(3):
                    t2 = tr(PS[:, b, c * 128:c * 128 + 128], TK[:, c * 128:c * 128 + 128], t, fr, inc=c == 2)
                a = acp(KN[:, :, :].rearrange("p c k -> p (c k)"), PS[:, b, 0:384], t2, s_free[2])
                g.banks.give(b, a)
                yield 1
                bo, fro = g.banks.take()
                tS = s_free[3]
                for c in range(4):
                    o = PS[:, bo, c * 128:c * 128 + 128]
                    v = vh[:, c, h * 128:h * 128 + 128]
                    if c < 3:
                        b, fr = g.banks.take()
                        t3 = mm(PS[:, b, 0:128], KN[:, c, :], v, True, True, a, t_vh, fr, inc=True)
                    t = mm(o, AH[:, c * 128:c * 128 + 128], v, True, c == 0, tA[h % 2], t_vh, fro, inc=c == 0)
                    if c:
                        t = mm(o, QB[:, c * 128:c * 128 + 128], St[:, :], False, True, t1, tS, inc=True)
                    if c < 3:
                        if c == 0:
                            tS = cp(St[:, :], PS[:, b, 0:128], t3, tS, t)
                        else:
                            tS = stt(St[:, :], St[:, :], eb[:, c:c + 1], PS[:, b, 0:128], ALU.mult, ALU.add, t3, tS, te, t)
                        g.banks.give(b, tS)
                    yield 1
                tA[h % 2] = [t, tA[h % 2]]
                hv = ho[:, h, :, :].rearrange("p c v -> p (c v)")
                a = cp(hv, PS[:, bo, :], t)
                g.banks.give(bo, a)
                t4 = tsq = af(TK[:, :], hv, ACT.Square, a, t2)
                hs = hss[:, 4 * h:4 * h + 4]
                t4 = red(hs, TK[:, :].rearrange("p (c v) -> p c v", c=4), ALU.add, t4)
                s_free[0], s_free[1], s_free[2], s_free[3] = t, t4, t3, [tS, t]
                t4 = ts(hs, hs, 1.0 / 128, EPS, ALU.mult, ALU.add, t4)
                t4 = af(hs, hs, ACT.Ln, t4)
                t4 = af(hs, hs, ACT.Exp, t4, scale=-0.5)
                a = tt(ho[:, h, :, :], ho[:, h, :, :], gs[:, :, h * 128:h * 128 + 128], ALU.mult, a, tsq, t_gs, on=pool)
                a = tt(ho[:, h, :, :], ho[:, h, :, :], bc(hs, 2, [128, NB, 128]), ALU.mult, a, t4)
                yield 1
                yield 1
                b, fr = g.banks.take()
                for c in range(4):
                    t2 = tr(PS[:, b, c * 128:c * 128 + 128], ho[:, h, c, :], a, fr, inc=c == 3)
                x = hilo(hTh[:, h, :], hTl[:, h, :], PS[:, b, :], t2, scans[h], kks[h], tE, tQ, tK, s_free)
                g.banks.give(b, x)
                g.t_hT.append(x)
                t_ho.append([a, t2])
                yield 1

            todo = [(h, lv) for h in range(4) for lv in range(8)]
            tails = []
            td, sc, pr = {}, {}, {}
            for i in range(len(todo) + 3):
                if 0 <= i - 1 < len(todo):
                    sc[i - 1] = scaled(*todo[i - 1], (i - 1) % 2, td.get(i - 1))
                if i < len(todo) and todo[i][1] < 7:
                    td[i] = decay(*todo[i], i % 2)
                if 0 <= i - 2 < len(todo):
                    pr[i - 2] = products(*todo[i - 2], (i - 2) % 2, *sc[i - 2])
                if i >= 3:
                    place(*todo[i - 3], *pr[i - 3])
                    if todo[i - 3][1] == 7:
                        if not tails:
                            gates()
                        tails.append(tail(todo[i - 3][0]))
                for q in list(tails):
                    next(q, None)
                yield 1
            for q in tails:
                yield from q
            g.hgrn_end = [t_ho, g.t_hT, tE, tQ, tK, tA, s_free, t_gs]
            g.hTh, g.hTl = hTh, hTl

        interleave(inproj, hgrn())
        for _ in inproj:
            pass
        t_in_end = (g.pe.sem, g.pe.n)
        g.banks.span(0, 8)
        n2b = at("n2b", 128, [128, D])
        WR = at("WR", 29, [128, 8, 36])
        BR = at("BR", 30.25, [128, 36])
        s_r = slot("s_r")
        g.pool.dma(lambda e: e.dma_start(n2b[:, :], I["norm2_w"].partition_broadcast(128)[:, 0, :]), s_r, g.hgrn_end,
                   t_attn, t_gs)
        g.pool.dma(lambda e: e.dma_start(WR[:, :, :], I["w_router"]), s_r)
        g.pool.dma(lambda e: e.dma_start(BR[:, :], I["b_router"].partition_broadcast(128)[:, 0, :]), s_r)
        t_r = (s_r[0], s_r[1])

        aTh, aTl = at("aTh", 96, [128, 4, T], F32R), at("aTl", 104, [128, 4, T], F32R)
        t_aT = []
        for c in range(4):
            t_aT.append(hilo(aTh[:, c, :], aTl[:, c, :], attnT[:, c, :], t_attn, g.hgrn_end))
        zr = [at(f"zr{i}", 112 + 2 * i, [128, 512]) for i in range(8)]
        mTh, mTl = at("mTh", 32, [128, 8, T], F32R), at("mTl", 48, [128, 8, T], F32R)
        s_zr = [slot(f"s_zr{i}") for i in range(8)]
        t_mT, t_zfree = [], [None] * 8
        for c in range(2):
            zl = []
            for i in range(4):
                for w in range(2):
                    q = 2 * i + w
                    zl.append(g.pool.dma(lambda e, q=q, w=w, i=i, c=c: e.dma_start(zr[q][:, :], zsp[8 * w + 4 * c + i, :, :]),
                                       s_zr[q], t_z, g.hgrn_end, t_zfree[q]))
            zl = [af(zr[q][:, :], zr[q][:, :], ACT.Sigmoid, zl[q]) for q in range(8)]
            ta_ = {}

            def ev_ba(i, b, t):
                ta_[i] = tt(zr[2 * i][:, :], zr[2 * i][:, :], PS[:, b, :], ALU.mult, t, zl[2 * i])
                return ta_[i]

            def ev_bh(i, b, t):
                z0, z1 = zr[2 * i][:, :], zr[2 * i + 1][:, :]
                a = tt(z1, z1, PS[:, b, :], ALU.mult, t, zl[2 * i + 1])
                s = tt(z0, z0, z1, ALU.add, a, ta_[i])
                x = hilo(mTh[:, 4 * c + i, :], mTl[:, 4 * c + i, :], z0, s, t_in_end)
                t_zfree[2 * i] = t_zfree[2 * i + 1] = x
                t_mT.append(x)
                return a

            dense(st, ("ba", c), 1, "b", aTh, aTl, t_aT, 4, ev_ba)
            dense(st, ("bh", c), 1, "b", g.hTh, g.hTl, g.t_hT, 4, ev_bh)
        t_x2 = [None] * NB

        def ev_add(c):
            def f(i, b, t):
                v = x_sb[:, i, c * 512:c * 512 + 512]
                a = tt(v, v, PS[:, b, :], ALU.add, t)
                t_x2[i] = a
                return a
            return f

        for c in range(2):
            t_wo = dense(st, ("wo", c), 2, "a", mTh, mTl, t_mT, 4, ev_add(c))

        hn = at("hn", 32, [128, NB, D])
        hnT = at("hnT", 48, [128, 8, T])
        hnh, hnl = at("hnh", 64, [128, NB, D], F32R), at("hnl", 80, [128, NB, D], F32R)
        Lg = at("Lg", 102, [128, 4, 36])
        moe_free = [t_wo, g.t_hT, t_aT, t_mT, g.hgrn_end]
        t_hn = [stt(hn[:, tb, :], x_sb[:, tb, :], rs4[:, tb:tb + 1], n2b[:, :], ALU.mult, ALU.mult, r, t_r)
                for tb, r in norm_steps(hn, t_x2, moe_free)]
        t_hT2 = []

        def ev_hnT(c, t):
            t_hT2.append((cp if c % 2 else acp)(hnT[:, c, :], PS[:, c, :], t, moe_free))
            return t_hT2[-1]

        transposed(hn, t_hn, ev_hnT)
        b, fr = g.banks.take()
        for tb in range(NB):
            for k in range(8):
                t = mm(PS[:, b, tb * 36:tb * 36 + 36], hnT[:, k, tb * 128:tb * 128 + 128], WR[:, k, :], k == 0, k == 7,
                       t_hT2, t_r, fr, inc=k == 7)
        t_lg = tt(Lg[:, :, :], PS[:, b, 0:144].rearrange("p (b n) -> p b n", b=4), bc(BR[:, :], 1, [128, 4, 36]), ALU.add, t, t_r)
        g.banks.give(b, t_lg)
        t_hs = []
        for tb in range(NB):
            a = acp(hnh[:, tb, :], hn[:, tb, :], t_hn, moe_free)
            t_hs.append([a, tt(hnl[:, tb, :], hn[:, tb, :], hnh[:, tb, :].bitcast(F32), ALU.subtract, a, on=pool)])

        mraw = [raw[3], rawx, raw[0], raw[1], raw[2]]
        mhi, mlo = hi + [hix], lo + [lox]
        mst = Stream(g, wplan2, mslots, mraw, mhi, mlo, 0.25,
                     [[g.hgrn_end, t_attn, t_z], [g.hgrn_end, t_attn, t_gs]] + [st.raw_end(i) for i in range(3)],
                     [st.hl_end(0), st.hl_end(1), [moe_free, t_hn, t_attn, t_z]])
        mst.split_to(2)

        RT = at("RT", 103, [128, 1600])
        ro = [0]

        def rt(n):
            o = ro[0]
            ro[0] += n
            assert ro[0] <= 1600
            return RT[:, o:o + n]

        lg, le = Lg[:, :, 0:4], Lg[:, :, 4:36].rearrange("p b (g j) -> p b g j", g=4)

        def first_max(v, n, t, dec):
            m = rt(4)
            eq, s = rt(4 * n).rearrange("p (b n) -> p b n", b=4), rt(4)
            t1 = red(m, v, ALU.max, t)
            t2 = tt(eq, v, bc(m, 2, [128, 4, n]), ALU.is_equal, t1)
            t2 = tt(eq, eq, bc(dec, 1, [128, 4, n]), ALU.mult, t2)
            t2 = red(s, eq, ALU.max, t2)
            t2 = tt(eq, eq, bc(s, 2, [128, 4, n]), ALU.is_equal, t2)
            return m, eq, t1, t2

        dec8 = cst("dec8")
        gm, g1h, t1, tg = first_max(lg, 4, t_lg, dec8[:, 4:8])
        dlg, gsum = rt(16).rearrange("p (b n) -> p b n", b=4), rt(4)
        t = tt(dlg, lg, bc(gm, 2, [128, 4, 4]), ALU.subtract, t1)
        t = af(dlg, dlg, ACT.Exp, t)
        t = red(gsum, dlg, ALU.add, t)
        t_pg = rcp(gsum, gsum, t)
        ls = rt(128).rearrange("p (b g j) -> p b g j", b=4, g=4)
        lsel = rt(32).rearrange("p (b j) -> p b j", b=4)
        t = tt(ls, le, bc(g1h, 3, [128, 4, 4, 8]), ALU.mult, tg)
        t = red(lsel, ls.rearrange("p b g j -> p b j g"), ALU.add, t)
        m1, o1, t1, to1 = first_max(lsel, 8, t, dec8)
        l2 = rt(32).rearrange("p (b j) -> p b j", b=4)
        t = stt(l2, o1, -3e38, lsel, ALU.mult, ALU.add, to1)
        m2, o2, t2, to2 = first_max(l2, 8, t, dec8)
        e2, den = rt(4), rt(4)
        t = tt(e2, m2, m1, ALU.subtract, t1, t2)
        t = af(e2, e2, ACT.Exp, t)
        t3 = ts(den, e2, 1.0, None, ALU.add, None, t)
        t3 = rcp(den, den, t3)
        gwv = gw.rearrange("p (b k) -> p b k", k=2)
        t3 = tt(gwv[:, :, 0], gsum, den, ALU.mult, t3, t_pg)
        t_gw = tt(gwv[:, :, 1], gwv[:, :, 0], e2, ALU.mult, t3, t)
        O = [rt(128).rearrange("p (b g j) -> p b g j", b=4, g=4) for _ in range(2)]
        t_o = [tt(O[k], bc(g1h, 3, [128, 4, 4, 8]), bc(o, 2, [128, 4, 4, 8]), ALU.mult, tg, tt_)
               for k, (o, tt_) in enumerate(((o1, to1), (o2, to2)))]
        Of = [o.rearrange("p b g j -> p b (g j)") for o in O]
        M = rt(128).rearrange("p (b e) -> p b e", b=4)
        t_m = tt(M, Of[0], Of[1], ALU.add, t_o)
        b, fr = g.banks.take()
        for tb in range(NB):
            for q in range(tb + 1):
                t = mm(PS[:, b, tb * 32:tb * 32 + 32], ones if q < tb else cst("ustrict"), M[:, q, :], q == 0, q == tb,
                       t_m, fr, inc=q == tb)
        for q in range(NB):
            t = mm(PS[:, b, 128:160], ones, M[:, q, :], q == 0, q == 3, inc=q == 3)
        rank = rt(128).rearrange("p (b e) -> p b e", b=4)
        cnt = rt(32)
        t_k = cp(rank, PS[:, b, 0:128].rearrange("p (b e) -> p b e", b=4), t)
        t_n = cp(cnt, PS[:, b, 128:160], t)
        g.banks.give(b, [t_k, t_n])
        mxn, stp, pf = rt(1), rt(8), rt(1)
        t = red(mxn, cnt, ALU.max, t_n)
        t = ts(stp, cst("step8"), mxn, None, ALU.is_lt, None, t, t_c)
        t = red(pf, stp, ALU.add, t)
        t_P = cp(PI[:, 0:1], pf, t)
        tmp = rt(128).rearrange("p (b e) -> p b e", b=4)
        rkv, ekv = rk.rearrange("p (b k) -> p b k", k=2), ek.rearrange("p (b k) -> p b k", k=2)
        t_e = []
        t = t_k
        for k in range(2):
            t = tt(tmp, Of[k], rank, ALU.mult, t, t_k, t_o)
            t = red(rkv[:, :, k], tmp, ALU.add, t)
            t_e.append(t)
            t = tt(tmp, Of[k], bc(cst("e64"), 1, [128, 4, 32]), ALU.mult, t)
            t = red(ekv[:, :, k], tmp, ALU.add, t)
            t_e.append(t)
        rkm = rt(128).rearrange("p (b e) -> p b e", b=4)
        t = stt(rkm, rank, 1.0, M, ALU.add, ALU.mult, t_k, t_m)
        t_rkm = ts(rkm, rkm, -1.0, None, ALU.add, None, t)

        S = [at(f"S{i}", 137.5 + 2 * i, [128, NB, 2, WIN], F32R) for i in range(2)]
        XG = [at(f"XG{i}", 32 + 8 * i, [128, 8, 2, 2, WIN], F32R) for i in range(2)]
        GS = [at(f"GS{i}", 48 + 2 * i, [128, 512]) for i in range(2)]
        US = [at(f"US{i}", 52 + 2 * i, [128, 512]) for i in range(2)]
        HT = [at(f"HT{i}", 56 + 2 * i, [128, 4, 2, WIN], F32R) for i in range(2)]
        SG = [at(f"SG{i}", 60 + i, [128, 256]) for i in range(2)]
        HF = [at(f"HF{i}", 62 + i, [128, 256]) for i in range(2)]
        YT = [at(f"YT{i}", 109.5 + 4 * i, [128, D]) for i in range(2)]
        GT = [at(f"GT{i}", 32 + 4 * i, [128, D]) for i in range(4)]

        def experts(st, s_y, s_g, t0, t_rkm, t_idx):
            tS, tXG, tGS, tHT, tY = [None] * 2, [None] * 2, [None] * 2, [None] * 2, [None] * 2
            xg = {}
            ywr = []

            def gather(i):
                p = i % 2
                if i >= NE // 2:
                    return
                t = tt(S[p][:, :, :, :], bc(rkm[:, :, 2 * i:2 * i + 2], 3, [128, NB, 2, WIN]),
                       cst("iota").unsqueeze(1).unsqueeze(1).broadcast_to([128, NB, 2, WIN]), ALU.is_equal, t_rkm, tS[p], t0)
                xg[i] = ev = []
                yield
                for hl, src in ((0, hnh), (1, hnl)):
                    for c4 in range(2):
                        b, fr = g.banks.take()
                        for c in range(4):
                            cc = 4 * c4 + c
                            for tb in range(NB):
                                t2 = mm(PS[:, b, c * 128:c * 128 + 128], src[:, tb, cc * 128:cc * 128 + 128],
                                        S[p][:, tb, :, :].rearrange("p e s -> p (e s)"), tb == 0, tb == 3,
                                        t, t_hs, fr, inc=c == 3 and tb == 3)
                        f = acp if c4 else cp
                        for e in range(2):
                            a = f(XG[p][:, 4 * c4:4 * c4 + 4, e, hl, :],
                                  PS[:, b, :].rearrange("p (c e s) -> p c e s", c=4, e=2)[:, :, e, :], t2, tXG[p], t0)
                            ev.append(a)
                        g.banks.give(b, ev[-2:])
                        if hl and c4:
                            tS[p] = t2
                        yield

            fold_in = {}

            def product(kind, e, dst, cpy):
                p, q = (e // 2) % 2, e % 2
                b, fr = g.banks.take()
                for ui in range(2):
                    u, h, l, tok = st.take((kind, e))
                    for kk in range(4):
                        k = 4 * ui + kk
                        xw = XG[p][:, k, q, :, :].rearrange("p a s -> p (a s)")
                        mm(PS[:, b, :], xw, h[:, kk, :], k == 0, False, tok, xg[e // 2], fr)
                        t = mm(PS[:, b, :], xw, l[:, kk, :], False, k == 7, inc=kk == 3)
                    st.done(u, t)
                a = cpy(dst[:, :], PS[:, b, :], t, tGS[q], t0)
                g.banks.give(b, a)
                tXG[p] = t
                return a

            def gate(e):
                fold_in[e] = [product("g", e, GS[e % 2], acp)]

            def up_(e):
                fold_in[e].append(product("u", e, US[e % 2], cp))

            def act_fold(e):
                q = e % 2
                b, fr = g.banks.take()
                for o, src in ((0, GS[q]), (256, US[q])):
                    for j in range(4):
                        t = mm(PS[:, b, o + j * 64:o + j * 64 + 64], src[:, j * 128:j * 128 + 128], fold, True, True,
                               fold_in[e], fr, t_c, inc=j == 3)
                tGS[q] = t
                a = af(SG[q][:, :], PS[:, b, 0:256], ACT.Silu, t, t0)
                m = tt(HF[q][:, :], SG[q][:, :], PS[:, b, 256:512], ALU.mult, a)
                g.banks.give(b, [a, m])
                hv = HF[q][:, :].rearrange("p (j s) -> p j s", j=4)
                a = acp(HT[q][:, :, 0, :], hv, m, tHT[q])
                l = tt(HT[q][:, :, 1, :], hv, HT[q][:, :, 0, :].bitcast(F32), ALU.subtract, a, tHT[q])
                return [a, l]

            def down(e, th):
                q, y = e % 2, YT[(e // 2) % 2]
                r0, r1 = (0, 64) if q == 0 else (64, 0)
                outs = []
                for c in range(2):
                    b, fr = g.banks.take()
                    u, h, l, tok = st.take(("d", e))
                    for j in range(4):
                        hw = HT[q][:, j, :, :].rearrange("p a s -> p (a s)")
                        mm(PS[:, b, :], hw, h[:, j, :], j == 0, False, tok, th, fr)
                        t = mm(PS[:, b, :], hw, l[:, j, :], False, j == 3, inc=j == 3)
                    st.done(u, t)
                    yv = y[r0:r0 + 64, c * 512:c * 512 + 512]
                    a = acp(yv, PS[r0:r0 + 64, b, :], t, tY[(e // 2) % 2], t0)
                    m = tt(yv, PS[r1:r1 + 64, b, :], yv, ALU.add, a)
                    g.banks.give(b, [a, m])
                    outs.append(m)
                tHT[q] = t
                return outs

            def write(i, yo):
                tY[i % 2] = g.act.dma(lambda q: q.dma_start(ysp[i * 128:i * 128 + 128, :], YT[i % 2][:, :]), s_y[i % 2], yo)

            for _ in gather(0):
                pass
            gate(0)
            up_(0)
            yo, full = [], None
            ga = gather(1)
            next(ga)
            for e in range(NE):
                if e + 1 < NE:
                    gate(e + 1)
                if full:
                    write(*full)
                    full = None
                if e % 2 == 0 and e:
                    next(ga, None)
                th = act_fold(e)
                if e + 1 < NE:
                    up_(e + 1)
                if e % 2 == 0:
                    next(ga, None)
                yo += down(e, th)
                next(ga, None)
                if e % 2 == 0:
                    for _ in ga:
                        pass
                    ga = gather(e // 2 + 2)
                    next(ga, None)
                if e % 2:
                    full, yo = (e // 2, yo), []
            write(*full)
            last = []
            gfree = [None] * 4
            n = 0
            xt = None
            for b in range(NB):
                for k in range(2):
                    j = 2 * b + k
                    gt = GT[n % 4]
                    t = g.pool.dma(lambda q, gt=gt, j=j: q.indirect_dma_start(
                        gt[:, :], None, ysp[:, :], bass.IndirectOffsetOnAxis(ap=SI[:, j:j + 1], axis=0)),
                        s_g[n % 4], tY, tXG, t_idx, gfree[n % 4], t0)
                    v = x_sb[:, b, :]
                    xt = stt(v, gt[:, :], wt[:, j:j + 1], v, ALU.mult, ALU.add, t, t_idx, last[-1:] if k else None)
                    gfree[n % 4] = xt
                    last.append(xt)
                    n += 1
            return [last[2 * b + 1] for b in range(NB)], last

        def index(*deps):
            a = ts(rc1, rk, 0.0, None, ALU.is_ge, None, *deps)
            b_ = ts(rc2, rk, float(WIN), None, ALU.is_lt, None, *deps)
            a = tt(rc1, rc1, rc2, ALU.mult, a, b_)
            w = tt(wt, gw, rc1, ALU.mult, a, t_gw)
            c = ts(rc2, rk, 0.0, float(WIN - 1), ALU.max, ALU.min, a)
            c = tt(rc2, rc2, ek, ALU.add, c)
            return [w, cp(SI[:, 0:8], rc2, c)]

        s_y = [slot(f"s_y{i}") for i in range(2)]
        s_g = [slot(f"s_g{i}") for i in range(4)]
        t_idx = index(*t_e)
        t_moe, t_gth = experts(mst, s_y, s_g, [t_lg, t_hs, t_hT2, t_hn], t_rkm, t_idx)

        main, main_banks = (g.pe, g.act, g.dve, g.pool, g.sp), g.banks
        lsems = []

        def lsem(n):
            s = sem(n)
            lsems.append(s)
            return s

        loop = tuple(Eng(lsem("l_" + n)) for n in engs)
        g.pe, g.act, g.dve, g.pool, g.sp = loop
        g.banks = Banks()
        lw = [[lsem(f"l_w{i}"), 0] for i in range(5)]
        ly = [[lsem(f"l_y{i}"), 0] for i in range(2)]
        lg_ = [[lsem(f"l_g{i}"), 0] for i in range(4)]
        keep = (t_c, t_hs, t_gw)
        t_c = t_hs = t_gw = None
        lst = Stream(g, make_plan_moe(I), lw, mraw, mhi, mlo, 0.25)
        a = ts(rkm, rkm, -float(WIN), None, ALU.add, None)
        b_ = ts(rk, rk, -float(WIN), None, ALU.add, None)
        ti = index(b_)
        experts(lst, ly, lg_, None, a, ti)
        t_c, t_hs, t_gw = keep
        bar = [sem(f"bar{i}") for i in range(4)]
        for q, lq, n in zip(main, loop, engs):
            q.items.append(("loop", q.waits([t_P]), lq.items, n))
        g.pe, g.act, g.dve, g.pool, g.sp = main
        g.banks = main_banks

        st = Stream(g, wplan3, wslots, raw, hi, lo, 0.0, [mst.raw_end(i) for i in (2, 3, 4, 0)],
                    [mst.hl_end(0), mst.hl_end(1)])
        st.load_to(4)
        s_small = [mst.raw_end(1), t_lg, t_r]
        s_b = slot("s_b")
        FNB = at("FNB", 128, [128, D])

        def ffn(pre, wcol, tx, deps):
            xs = at("xs_" + pre, 32, [128, NB, D])
            xh, xl = at("xh_" + pre, 48, [128, 8, T], F32R), at("xl_" + pre, 64, [128, 8, T], F32R)
            th, tl = at("th_" + pre, 80, [128, 11, T], F32R), at("tl_" + pre, 102, [128, 11, T], F32R)
            sg = [at(f"sg{i}_" + pre, 124 + 2 * i, [128, 512]) for i in range(4)]
            t_xT = norm_t(xs, wcol, xh, xl, tx, deps)
            t_sg = [None] * 4
            t_dn = None
            xt = [None] * NB
            for half in range(2):
                t_h = {}
                for gi, (a0, b0) in enumerate(FCUTS):
                    nb = (b0 - a0) // 128
                    tg_ = {}

                    def ev_g(i, b, t):
                        tg_[i] = af(sg[i][:, :], PS[:, b, :], ACT.Silu, t, t_sg[i], deps)
                        return tg_[i]

                    def ev_u(i, b, t):
                        m = tt(sg[i][:, :], sg[i][:, :], PS[:, b, :], ALU.mult, t, tg_[i])
                        f = a0 // 128 + i
                        x = hilo(th[:, f, :], tl[:, f, :], sg[i][:, :], m, t_dn, deps)
                        t_sg[i] = x
                        t_h[f] = x
                        return m

                    dense(st, (pre, "g", half, gi), 2, "b", xh, xl, t_xT, nb, ev_g)
                    dense(st, (pre, "u", half, gi), 2, "b", xh, xl, t_xT, nb, ev_u)

                for c in range(2):
                    def ev_d(i, b, t):
                        v = x_sb[:, i, c * 512:c * 512 + 512]
                        a = stt(v, PS[:, b, :], 0.5, v, ALU.mult, ALU.add, t)
                        xt[i] = a
                        return a

                    t_dn = dense(st, (pre, "d", half, c), 3, "a", th, tl, t_h, 4, ev_d)
            return xt, [t_dn, t_sg]

        t_x4, t_f1 = ffn("ffn1", f1c, t_moe, [t_gth, t_rkm, t_idx])

        xs = at("xs2", 32, [128, NB, D])
        xh, xl = at("xh2", 48, [128, 8, T], F32R), at("xl2", 64, [128, 8, T], F32R)
        t_xT = norm_t(xs, mxc, xh, xl, t_x4, t_f1)
        qn, kn, v2 = (at(n, 80 + 8 * i, [128, NB, 512]) for i, n in enumerate(("qn2", "kn2", "v2")))
        up = at("up", 104, [128, 4, 16 + T])
        q2T, k2T = at("q2T", 112.5, [128, 4, T]), at("k2T", 120.5, [128, 4, T])
        s2 = at("s2", 128.5, [128, 4, T])
        P2 = [at(f"P2{i}", o, [128, 4, 128]) for i, o in enumerate((136.5, 138.5, 140.5, 90))]
        Bt = at("Bt", 32, [128, 8, 256])
        a2T = at("a2T", 40, [128, 4, T])
        QW = at("QW", 21, [128, 2, 64])
        QS2 = at("QS2", 21.5, [128, 64])
        PW = at("PW", 22, [128, 4, 128])
        S4 = at("S4", 24, [128, 16])
        g.pool.dma(lambda e: e.dma_start(QW[:, 0, :], I["q_norm_2"].partition_broadcast(128)[:, 0, :]), s_b, s_small)
        g.pool.dma(lambda e: e.dma_start(QW[:, 1, :], I["k_norm_2"].partition_broadcast(128)[:, 0, :]), s_b)
        g.pool.dma(lambda e: e.dma_start(PW[:, :, :], I["pool_w_2"][0].rearrange("g c d -> c g d")), s_b)
        t_b = (s_b[0], s_b[1])
        s_bt = slot("s_bt")
        t_bt = g.pool.dma(lambda e: e.dma_start(Bt[:, :, :], I["rel_tile"]), s_bt, t_xT)
        t_bt = tt(Bt[:, :, 128:256], Bt[:, :, 128:256], bc(cst("cmask"), 1, [128, 8, 128]), ALU.add, t_bt)
        t_p = [dve(lambda e: e.memset(up[:, :, 0:16], 0.0), t_f1)]
        t_q2, t_k2, t_v2, t_u2 = [], [], [], []

        def ev_nat(dst, toks, f):
            def ev(i, b, t):
                a = f(dst[:, i, :], PS[:, b, :], t, t_f1)
                toks.append(a)
                return a
            return ev

        def ev_up(i, b, t):
            a = acp(up[:, i, 16:16 + T], PS[:, b, :], t, t_f1)
            t_u2.append(a)
            return a

        dense(st, ("in2", 0), 2, "a", xh, xl, t_xT, 4, ev_nat(qn, t_q2, cp))
        dense(st, ("in2", 1), 2, "a", xh, xl, t_xT, 4, ev_nat(kn, t_k2, acp))
        dense(st, ("in2", 2), 2, "a", xh, xl, t_xT, 4, ev_nat(v2, t_v2, acp))
        t_in2 = dense(st, ("in2", 3), 2, "b", xh, xl, t_xT, 4, ev_up)

        t_ss, tp = [], [None] * 4
        for w, (src, tk) in enumerate(((qn, t_q2), (kn, t_k2))):
            for i in range(NB):
                sv = s2[:, i, :]
                a = af(sv, src[:, i, :], ACT.Square, tk, tp[i], t_f1)
                r = red(QS2[:, 32 * w + 8 * i:32 * w + 8 * i + 8], sv.rearrange("p (h d) -> p h d", h=8), ALU.add, a, t_b)
                tp[i] = r
                t_ss.append(r)
        t = ts(QS2[:, :], QS2[:, :], 1.0 / 64, EPS, ALU.mult, ALU.add, t_ss)
        t = af(QS2[:, :], QS2[:, :], ACT.Sqrt, t)
        t = rcp(QS2[:, :], QS2[:, :], t)
        t_qk = []
        for w, (src, dst, tk) in enumerate(((qn, q2T, t_q2), (kn, k2T, t_k2))):
            t_n = []
            for i in range(NB):
                v = src[:, i, :].rearrange("p (h d) -> p h d", h=8)
                a = tt(v, v, bc(QS2[:, 32 * w + 8 * i:32 * w + 8 * i + 8], 2, [128, 8, 64]), ALU.mult, t, tk)
                t_n.append(tt(v, v, bc(QW[:, w, :], 1, [128, 8, 64]), ALU.mult, a, t_b))
            for j in range(4):
                b, fr = g.banks.take()
                for i in range(NB):
                    t2 = tr(PS[:, b, i * 128:i * 128 + 128], src[:, i, j * 128:j * 128 + 128], t_n, fr, inc=i == 3)
                a = acp(dst[:, j, :], PS[:, b, :], t2, t_f1)
                g.banks.give(b, a)
                t_qk.append(a)
        pTh, pTl = at("pTh", 48, [128, 4, T], F32R), at("pTl", 56, [128, 4, T], F32R)
        a2h, a2l = at("a2h", 64, [128, 4, T], F32R), at("a2l", 72, [128, 4, T], F32R)
        W0 = [at(f"PP{i}", 80 + 2.0625 * i, [128, 16 + T]) for i in range(3)]
        dd = at("dd", 88, [128, T])
        z = [dve(lambda e, w=w: e.memset(w[:, 0:16], 0.0), t_qk) for w in W0[:2]]
        t_pool = []
        tdd = None
        tpp = [None, None]
        for gi in range(4):
            cur, tcur = up[:, gi, :], [t_u2, t_p]
            for stp_ in range(gi + 1):
                d = 1 << stp_
                nx = W0[stp_ % 2]
                tcur = tt(nx[:, 16:16 + T], cur[:, 16:16 + T], cur[:, 16 - d:16 - d + T], ALU.add, tcur, z, t_qk, tpp)
                cur = nx
            w = 2 << gi
            t = stt(dd[:, :], cur[:, 16:16 + T], 1.0 / w, up[:, gi, 16:16 + T], ALU.mult, ALU.subtract, tcur, tdd, t_qk)
            fx = W0[2][:, 0:16]
            t2 = tt(fx, cur[:, 16:32], cst("rc16")[:, gi * 16:gi * 16 + 16], ALU.mult, tcur, t, t_c)
            t2 = tt(dd[:, 0:16], fx, up[:, gi, 16:32], ALU.subtract, t2, t)
            b, fr = g.banks.take()
            t3 = mm(PS[:, b, :], PW[:, gi, :], dd[:, :], True, True, t, t2, t_b, fr, inc=True)
            tdd = t3
            h = af(pTh[:, gi, :], PS[:, b, :], ACT.Copy, t3, t_in2, scale=psc[:, gi:gi + 1])
            l = stt(pTl[:, gi, :], PS[:, b, :], psc[:, gi:gi + 1], pTh[:, gi, :].bitcast(F32), ALU.mult, ALU.subtract, h, t_in2)
            g.banks.give(b, [h, l])
            t_pool.append([h, l])

        t_at = []
        tsf = [t_qk, t_ss]
        tpT = None
        for qb in range(NB):
            W = (qb + 1) * 128
            Wn = min(W, 256)
            Wf = W - Wn
            for j in range(2):
                b, fr = g.banks.take(4)
                for hh in range(4):
                    h = 4 * j + hh
                    p0 = (h % 2) * 64
                    t = mm(PS[:, b + hh, 0:W], q2T[p0:p0 + 64, h // 2, qb * 128:qb * 128 + 128], k2T[p0:p0 + 64, h // 2, 0:W],
                           True, True, t_qk, fr, inc=hh == 3)
                t1 = stt(s2[:, :, Wf:W], PS[:, b:b + 4, Wf:W], 0.125, Bt[:, 4 * j:4 * j + 4, 256 - Wn:256], ALU.mult, ALU.add,
                         t, t_bt, tsf)
                t2 = None
                if Wf:
                    t2 = stt(s2[:, :, 0:Wf], PS[:, b:b + 4, 0:Wf], 0.125, bc(bfar[:, 4 * j:4 * j + 4], 2, [128, 4, Wf]),
                             ALU.mult, ALU.add, t, t_b, tsf)
                g.banks.give(b, [t1, t2], 4)
                s = s2[:, :, 0:W]
                t = red(S4[:, 0:4], s, ALU.max, t1, t2, t_b)
                t = tt(s, s, bc(S4[:, 0:4], 2, [128, 4, W]), ALU.subtract, t)
                t = af(s, s, ACT.Exp, t)
                t5 = red(S4[:, 4:8], s, ALU.add, t)
                t5 = rcp(S4[:, 8:12], S4[:, 4:8], t5)
                t6 = tt(s, s, bc(S4[:, 8:12], 2, [128, 4, W]), ALU.mult, t5, t)
                bo, fro = g.banks.take()
                ev = []
                for kb in range(qb + 1):
                    b, fr = g.banks.take()
                    for hh in range(4):
                        t = tr(PS[:, b, hh * 128:hh * 128 + 128], s2[:, hh, kb * 128:kb * 128 + 128], t6, fr, inc=hh == 3)
                    a = acp(P2[kb][:, :, :].rearrange("p h q -> p (h q)"), PS[:, b, :], t, tpT)
                    g.banks.give(b, a)
                    ev.append(a)
                tsf = [ev]
                for hh in range(4):
                    h = 4 * j + hh
                    o = PS[(h % 2) * 64:(h % 2) * 64 + 64, bo, (hh // 2) * 128:(hh // 2) * 128 + 128]
                    for kb in range(qb + 1):
                        t = mm(o, v2[:, kb, h * 64:h * 64 + 64], P2[kb][:, hh, :], kb == 0, kb == qb, ev, t_v2, fro,
                               inc=kb == qb)
                tpT = t
                a = acp(a2T[:, 2 * j:2 * j + 2, qb * 128:qb * 128 + 128],
                        PS[:, bo, 0:256].rearrange("p (c q) -> p c q", c=2), t, t_xT)
                g.banks.give(bo, a)
                t_at.append(a)
        t_cat = [hilo(a2h[:, c, :], a2l[:, c, :], a2T[:, c, :], t_at, t_in2) for c in range(4)] + t_pool

        class Cat:

            def __init__(self, a, b):
                self.a, self.b = a, b

            def __getitem__(self, key):
                k = key[1]
                src, k = (self.a, k) if k < 4 else (self.b, k - 4)
                return src[:, k, key[2]]

        t_x3 = [None] * NB

        def ev_add2(c):
            def f(i, b, t):
                v = x_sb[:, i, c * 512:c * 512 + 512]
                a = tt(v, v, PS[:, b, :], ALU.add, t)
                t_x3[i] = a
                return a
            return f

        for c in range(2):
            t_wo = dense(st, ("wo2", c), 2, "a", Cat(a2h, pTh), Cat(a2l, pTl), t_cat, 4, ev_add2(c))

        t_x5, t_f2 = ffn("ffn2", f2c, t_x3, [t_wo, t_at, tpT, t_cat, tsf])

        t_fn = g.sp.dma(lambda e: e.dma_start(FNB[:, :], I["final_norm_2"].partition_broadcast(128)[:, 0, :]), s_late, t_f2)
        ot = at("ot", 32, [128, NB, D])
        s_o = slot("s_o")
        for tb, r in norm_steps(ot, t_x5, t_f2):
            t = stt(ot[:, tb, :], x_sb[:, tb, :], rs4[:, tb:tb + 1], FNB[:, :], ALU.mult, ALU.mult, r, t_fn)
            t = g.sp.dma(lambda e, tb=tb: e.dma_start(out[0, tb * 128:tb * 128 + 128, :], ot[:, tb, :]), s_o, t)
        g.sp.items.append(("wait", [t, (s_y[0][0], s_y[0][1]), (s_y[1][0], s_y[1][1]), (s_z[0][0], s_z[0][1]), (s_z[1][0], s_z[1][1])]))

        def play(e, items):
            for it in items:
                if it[0] == "op":
                    _, waits, fn, inc = it
                    for s, v in waits:
                        e.wait_ge(s, v)
                    ins = fn(e)
                    if inc:
                        ins.then_inc(*inc)
                elif it[0] == "wait":
                    for s, v in it[1]:
                        e.wait_ge(s, v)
                else:
                    _, waits, body, name = it
                    for s, v in waits:
                        e.wait_ge(s, v)
                    r = e.value_load(PI[0:1, 0:1], min_val=0, max_val=T // WIN)
                    with e.If(r > 1):
                        meet(e, name)
                        with e.Fori(1, r):
                            play(e, body)
                            if name == "pool":
                                for q, v in lg_:
                                    e.wait_ge(q, v)
                                e.dma_reset(range(lg_[0][0].num, lg_[-1][0].num + 1))
                            meet(e, name)

        def meet(e, name):
            e.drain().then_inc(bar[0], 1)
            if name == "sp":
                e.wait_ge(bar[0], 5)
                for q in lsems:
                    e.sem_clear(q)
                e.sem_clear(bar[0])
                e.sem_inc(bar[1], 1)
                e.wait_ge(bar[2], 4)
                e.sem_clear(bar[1])
                e.sem_clear(bar[2])
            else:
                e.wait_ge(bar[1], 1)
                e.sem_inc(bar[2], 1)

        blk = ctx.enter_context(nc.Block())

        @blk.sync
        def _(e):
            play(e, g.sp.items)

        @blk.scalar
        def _(e):
            play(e, g.act.items)

        @blk.vector
        def _(e):
            play(e, g.dve.items)

        @blk.gpsimd
        def _(e):
            play(e, g.pool.items)

        @blk.tensor
        def _(e):
            play(e, g.pe.items)


def constants():
    import numpy as np
    p = np.arange(128)
    c = np.zeros((128, NC1), np.float32)

    def put(n, v):
        o, w = CW[n]
        c[:, o:o + w] = v

    put("ident", np.eye(128))
    put("ustrict", p[:, None] < p[None, :])
    put("ones", 1.0)
    put("fold", (p[:, None] % 64) == np.arange(64)[None, :])
    put("iota", np.arange(WIN)[None, :])
    put("cmask", np.where((p[:, None] < 64) & (p[None, :] >= 64), NEG, 0.0))
    put("rc16", np.concatenate([1.0 / np.minimum(np.arange(16) + 1, 2 << i) for i in range(4)])[None, :])
    put("e64", WIN * np.arange(32)[None, :])
    put("step8", (WIN * np.arange(8))[None, :])
    put("dec8", (8 - np.arange(8))[None, :])
    put("invf", (np.float32(500000.0) ** (-np.arange(0, 16, 2, dtype=np.float32) / np.float32(16)))[None, :])
    m1 = np.zeros((128, NC2), np.float32)
    k = np.arange(256)[None, :]
    m1[:, 0:256] = np.where((k <= p[:, None] + 128) & (p[:, None] + 128 - k < 128), 0.0, NEG)
    m1[:, 256:768] = (np.arange(512) % 128 != 0)[None, :]
    mk = np.zeros((128, 8, 128), np.uint32)
    s, t = p[:, None], p[None, :]
    for lv in range(7):
        h = 64 >> lv
        mk[:, lv, :] = (s // (2 * h) == t // (2 * h)) & (s // h % 2 == 0) & (t // h % 2 == 1)
    mk[:, 7, :] = s == t
    return c, m1, mk.reshape(128, NMASK)


NAMES = ["x", "w_in", "hgrn_norm_w", "w_branch_attn", "w_branch_hgrn", "w_out", "norm2_w", "w_gate_experts",
         "w_up_experts", "w_down_experts", "ffn1_w_gate_2", "ffn1_w_up_2", "ffn1_w_down_2", "w_in_2", "q_norm_2", "k_norm_2",
         "pool_w_2", "w_out_2", "ffn2_w_gate_2", "ffn2_w_up_2", "ffn2_w_down_2", "final_norm_2"]


def kernel(**inputs):
    import numpy as np
    import concourse.bacc as bacc
    from concourse.bass_utils import run_bass_kernel_spmd as run

    arrays = {n: np.ascontiguousarray(inputs[n]) for n in NAMES}
    rb = np.ascontiguousarray(inputs["rel_bias_2"])[0]
    rev = np.concatenate([np.repeat(rb[:, 256:257], 127, axis=1), rb[:, 256:0:-1]], axis=1)
    arrays["rel_tile"] = np.ascontiguousarray(np.stack([rev[:, 127 - q:383 - q] for q in range(128)]))
    def cols(n):
        a = np.ascontiguousarray(inputs[n])
        return a.reshape(a.shape[0], -1, 128).transpose(2, 0, 1).reshape(128, -1)

    def rows(a):
        return np.broadcast_to(a.reshape(1, -1), (128, a.size))

    arrays["c_par"] = np.ascontiguousarray(np.concatenate(
        [cols(n) for n in ("norm1_w", "norm2_w", "ffn1_norm_2", "mix_norm_2", "ffn2_norm_2", "pool_scale_2",
                           "hgrn_lower_bounds")]
        + [rows(np.ascontiguousarray(inputs["attn_sinks"])), rows(rb[:, 256])], axis=1))
    arrays["positions"] = np.ascontiguousarray(np.ascontiguousarray(inputs["positions"]).reshape(NB, 128).T)
    arrays["qk_norm"] = np.concatenate([np.ascontiguousarray(inputs["q_norm_w"])] * 8
                                       + [np.ascontiguousarray(inputs["k_norm_w"])] * 2, axis=1)
    wr = np.concatenate([np.ascontiguousarray(inputs["w_router_group"])[0],
                         np.ascontiguousarray(inputs["w_router_expert"])[0]], axis=1)
    arrays["w_router"] = np.ascontiguousarray(wr.reshape(8, 128, 36).transpose(1, 0, 2))
    arrays["b_router"] = np.concatenate([np.ascontiguousarray(inputs["b_router_group"]),
                                         np.ascontiguousarray(inputs["b_router_expert"])], axis=1)
    arrays["c_f32"], arrays["c_m1"], arrays["c_mask"] = constants()
    nc = bacc.Bacc("TRN2", target_bir_lowering=False, num_devices=1)
    I = {n: nc.dram_tensor("in_" + n, a.shape, mybir.dt.from_np(a.dtype), kind="ExternalInput").ap()
         for n, a in arrays.items()}
    out = nc.dram_tensor("out_0", (1, T, D), F32, kind="ExternalOutput").ap()
    program(nc, I, out)
    r = run(nc, [{"in_" + n: a for n, a in arrays.items()}], core_ids=[0])
    return r.results[0]["out_0"]
```

```python
from contextlib import ExitStack

import concourse.bass as bass
from concourse import mybir

ALU = mybir.AluOpType
ACT = mybir.ActivationFunctionType
AX = mybir.AxisListType
F32 = mybir.dt.float32
F32R = mybir.dt.float32r
I32 = mybir.dt.int32
U32 = mybir.dt.uint32

T, D, NB = 512, 1024, 4
EPS = 1e-6
WIN = 64
NE = 32
FF = 512
DFF = 2816
NEG = -1e30

CW = {}
_o = 0
for _n, _w in (("ident", 128), ("ustrict", 128), ("ones", 128), ("fold", 64), ("iota", WIN), ("cmask", 128),
               ("rc16", 64), ("e64", 32), ("step8", 8), ("dec8", 8), ("invf", 8)):
    CW[_n] = (_o, _w)
    _o += _w
NC1 = _o
NC2 = 256 + 512
NMASK = 8 * 128


class Eng:

    def __init__(self, sem):
        self.sem, self.n, self.seen, self.items = sem, 0, {}, []

    def op(self, fn, *deps, inc=True):
        waits = self.waits(deps)
        if inc:
            self.n += 1
        self.items.append(("op", waits, fn, (self.sem, 1) if inc else None))
        return (self.sem, self.n) if inc else None

    def dma(self, fn, slot, *deps):
        waits = self.waits(deps)
        slot[1] += 16
        self.items.append(("op", waits, fn, (slot[0], 16)))
        return (slot[0], slot[1])

    def waits(self, deps):
        out = []
        stack = list(deps)
        need = {}
        while stack:
            d = stack.pop()
            if d is None:
                continue
            if isinstance(d, list):
                stack.extend(d)
                continue
            s, v = d
            if need.get(id(s), (s, 0))[1] < v:
                need[id(s)] = (s, v)
        for k, (s, v) in need.items():
            if self.seen.get(k, 0) < v:
                self.seen[k] = v
                out.append((s, v))
        return out


class Banks:

    def __init__(self):
        self.free = [None] * 8
        self.held = [False] * 8
        self.at = 0
        self.lo, self.hi = 0, 8

    def span(self, lo, hi):
        self.lo, self.hi, self.at = lo, hi, lo

    def take(self, n=1):
        for _ in range(16):
            b = self.at
            if b % n == 0 and b + n <= self.hi and not any(self.held[b:b + n]):
                break
            self.at = self.at + 1 if self.at + 1 < self.hi else self.lo
        else:
            raise ValueError("no bank is free")
        self.at = b + n if b + n < self.hi else self.lo
        return self.hold(b, n)

    def hold(self, b, n=1):
        for i in range(b, b + n):
            assert not self.held[i]
            self.held[i] = True
        return b, [self.free[b + i] for i in range(n)]

    def give(self, b, tok, n=1):
        for i in range(n):
            self.free[b + i] = tok
            self.held[b + i] = False


class Stream:

    def __init__(self, g, plan, slots, raw, hi, lo, pool_part, raw_first=None, hl_first=None):
        self.g, self.plan, self.slots = g, plan, slots
        self.raw, self.hi, self.lo = raw, hi, lo
        self.nr, self.nh = len(raw), len(hi)
        self.loaded = self.split = self.taken = 0
        self.fence = len(plan)
        self.spread, self.rounded = False, None
        self.ld, self.sp, self.dn = {}, {}, {}
        self.pool_part = pool_part
        for u in range(self.nr):
            self.sp[u - self.nr] = raw_first[u] if raw_first else None
        for u in range(self.nh):
            self.dn[u - self.nh] = hl_first[u] if hl_first else None

    def load_to(self, j):
        while self.loaded < min(j, self.fence):
            u = self.loaded
            _, src, kc, n = self.plan[u]
            r = self.raw[u % self.nr]
            dst = r[:, 0:kc * n].rearrange("p (k n) -> p k n", k=kc)
            self.ld[u] = self.g.sp.dma(lambda e, dst=dst, src=src: e.dma_start(dst, src), self.slots[u % self.nr],
                                       self.sp.get(u - self.nr))
            self.loaded += 1

    def split_to(self, j):
        while self.split < min(j, self.fence):
            self.split_hi()
            self.split_lo()

    def split_hi(self):
        u = self.split
        self.load_to(u + 1)
        _, _, kc, n = self.plan[u]
        w = kc * n
        r, h = self.raw[u % self.nr], self.hi[u % self.nh]
        self.rounded = self.g.act.op(lambda e: e.copy(h[:, 0:w], r[:, 0:w]), self.ld[u], self.dn.get(u - self.nh))

    def split_lo(self):
        u, t = self.split, self.rounded
        _, _, kc, n = self.plan[u]
        w = kc * n
        r, h, l = self.raw[u % self.nr], self.hi[u % self.nh], self.lo[u % self.nh]
        c = w - int(w * self.pool_part) // 128 * 128
        a = self.g.dve.op(lambda e: e.tensor_tensor(l[:, 0:c], r[:, 0:c], h[:, 0:c].bitcast(F32), ALU.subtract),
                          t, self.ld[u], self.dn.get(u - self.nh))
        b = None
        if c < w:
            b = self.g.pool.op(lambda e: e.tensor_tensor(l[:, c:w], r[:, c:w], h[:, c:w].bitcast(F32), ALU.subtract),
                               t, self.ld[u], self.dn.get(u - self.nh))
        self.sp[u] = [t, a, b]
        self.split += 1
        self.rounded = None
        self.load_to(u + 1 + self.nr)

    def ahead(self, i):
        if i == 0 and self.split < min(self.taken + 1, self.fence):
            self.split_hi()
        if i == 1 and self.rounded:
            self.split_lo()

    def take(self, key):
        u = self.taken
        assert self.plan[u][0] == key, (self.plan[u][0], key)
        self.split_to(u + (1 if self.spread else self.nh))
        self.taken += 1
        _, _, kc, n = self.plan[u]
        h = self.hi[u % self.nh][:, 0:kc * n].rearrange("p (k n) -> p k n", k=kc)
        l = self.lo[u % self.nh][:, 0:kc * n].rearrange("p (k n) -> p k n", k=kc)
        return u, h, l, self.sp[u]

    def done(self, u, tok):
        self.dn[u] = tok

    def raw_end(self, i):
        return self.sp[max(u for u in range(-self.nr, len(self.plan)) if u % self.nr == i)]

    def hl_end(self, i):
        return self.dn[max(u for u in range(-self.nh, len(self.plan)) if u % self.nh == i)]


def units(key, w, k0, k1, c0, c1):
    out = []
    for k in range(k0, k1, 4):
        e = min(k + 4, k1)
        out.append((key, w[k * 128:e * 128, c0:c1].rearrange("(k p) n -> p k n", p=128), e - k, c1 - c0))
    return out


class G:
    pass


def make_plan_moe(I):
    plan = []

    def gu(e):
        plan.extend(units(("g", e), I["w_gate_experts"][0, e], 0, 8, 0, FF))
        plan.extend(units(("u", e), I["w_up_experts"][0, e], 0, 8, 0, FF))

    def dn(e):
        for c in range(2):
            plan.extend(units(("d", e), I["w_down_experts"][0, e], 0, 4, c * 512, c * 512 + 512))

    gu(0)
    for e in range(NE):
        if e + 1 < NE:
            gu(e + 1)
        dn(e)
    return plan


FCUTS = [(0, 512), (512, 1024), (1024, 1408)]


def make_plan_ffn(I, pre):
    plan = []
    for half in range(2):
        o = half * 1408
        for i, (a, b) in enumerate(FCUTS):
            plan.extend(units((pre, "g", half, i), I[pre + "_w_gate_2"][0], 0, 8, o + a, o + b))
            plan.extend(units((pre, "u", half, i), I[pre + "_w_up_2"][0], 0, 8, o + a, o + b))
        for c in range(2):
            plan.extend(units((pre, "d", half, c), I[pre + "_w_down_2"][0], half * 11, half * 11 + 11,
                              c * 512, c * 512 + 512))
    return plan


INP = [("qa", 0, 512), ("kv", 512, 768), ("qh", 768, 1280), ("gh", 2304, 2816), ("fh", 1280, 1792), ("ih", 1792, 2304),
       ("za0", 2816, 3328), ("za1", 3328, 3840), ("zb0", 3840, 4352), ("zb1", 4352, 4864)]


def make_plan(I):
    p1 = []
    for n, a, b in INP:
        p1.extend(units(n, I["w_in"][0], 0, 8, a, b))
    for c in range(2):
        p1.extend(units(("ba", c), I["w_branch_attn"][0], 0, 4, c * 512, c * 512 + 512))
        p1.extend(units(("bh", c), I["w_branch_hgrn"][0], 0, 4, c * 512, c * 512 + 512))
    for c in range(2):
        p1.extend(units(("wo", c), I["w_out"][0], 0, 8, c * 512, c * 512 + 512))
    p2 = make_plan_moe(I)
    p3 = make_plan_ffn(I, "ffn1")
    for c in (0, 1, 3, 2):
        p3.extend(units(("in2", c), I["w_in_2"][0], 0, 8, c * 512, c * 512 + 512))
    p4 = []
    for c in range(2):
        p4.extend(units("wo2", I["w_out_2"][0], 0, 8, c * 512, c * 512 + 512))
    return p1, p2, p3, p4, make_plan_ffn(I, "ffn2")


def program(nc, I, out):
    ctx = ExitStack()
    g = G()
    base = (nc.sbuf_base + 127) // 128 * 128
    end = nc.sbuf_usable_end
    KB = 1024
    ring = base
    arena = base + 64 * KB

    def at(name, off, shape, dt=F32):
        n = 4
        for s in shape[1:]:
            n *= s
        o = arena + int(off * KB)
        assert o % 32 == 0 and o + n <= end, (name, off, n, end - arena)
        return nc.alloc_sbuf_tensor_at(name, shape, dt, offset=o)

    with ctx:
        def sem(name):
            return ctx.enter_context(nc.semaphore(name))

        def slot(name):
            return [sem(name), 0]

        PS = ctx.enter_context(nc.psum_tensor("PS", [128, 8, 512], F32))
        raw = [nc.alloc_sbuf_tensor_at(f"raw{i}", [128, 2048], F32, offset=ring + i * 8 * KB) for i in range(4)]
        hi = [nc.alloc_sbuf_tensor_at(f"hi{i}", [128, 2048], F32R, offset=ring + (4 + i) * 8 * KB) for i in range(2)]
        lo = [nc.alloc_sbuf_tensor_at(f"lo{i}", [128, 2048], F32R, offset=ring + (6 + i) * 8 * KB) for i in range(2)]
        spare = ring + 24 * KB
        rawx = at("rawx", 21, [128, 2048])
        hix, lox = at("hix", 117.5, [128, 2048], F32R), at("lox", 125.5, [128, 2048], F32R)

        zsp = nc.dram_tensor("zsp", [16, 128, 512], F32)

        x_sb = at("x_sb", 0, [128, NB, D])
        C1 = at("C1", 16, [128, NC1])
        SM = at("SM", 19.25, [128, 176])

        def cst(n):
            o, w = CW[n]
            return C1[:, o:o + w]

        ident, ones, fold = cst("ident"), cst("ones"), cst("fold")
        n1c, n2c, f1c, mxc, f2c = (SM[:, 8 * i:8 * i + 8] for i in range(5))
        psc = SM[:, 40:44]
        lbr = SM[:, 44:52]
        sink = SM[:, 52:60]
        bfar = SM[:, 60:68]
        lbs = SM[:, 68:92]
        ss4, ms4, sd4, rs4 = (SM[:, 92 + 4 * i:96 + 4 * i] for i in range(4))
        gw = SM[:, 108:116]
        ws = SM[:, 140:144]
        PI = at("PI", 20.0625, [128, 8], I32)

        s_pe, s_act, s_dve, s_pool, s_sp = (sem("s_" + n) for n in ("pe", "act", "dve", "pool", "sp"))
        g.pe, g.act, g.dve, g.pool, g.sp = Eng(s_pe), Eng(s_act), Eng(s_dve), Eng(s_pool), Eng(s_sp)
        g.banks = Banks()
        engs = ("pe", "act", "dve", "pool", "sp")
        wslots = [slot(f"s_w{i}") for i in range(4)]
        mslots = [slot(f"s_m{i}") for i in range(5)]
        s_const = slot("s_const")
        s_late = slot("s_late")
        s_xin = [slot(f"s_xin{i}") for i in range(NB)]

        pe = lambda *a, **k: g.pe.op(*a, **k)
        act = lambda *a, **k: g.act.op(*a, **k)
        dve = lambda *a, **k: g.dve.op(*a, **k)
        pool = lambda *a, **k: g.pool.op(*a, **k)

        def mm(o, l, r, st, sp, *deps, inc=False):
            return pe(lambda e: e.matmul(o, l, r, start=st, stop=sp), *deps, inc=inc)

        def tr(o, i, *deps, inc=False):
            return pe(lambda e: e.transpose(o, i, ident), *deps, inc=inc)

        def tt(o, a, b, op, *deps, on=dve):
            return on(lambda e: e.tensor_tensor(o, a, b, op), *deps)

        def ts(o, a, s1, s2, op0, op1, *deps, on=dve):
            if op1 is None:
                return on(lambda e: e.tensor_scalar(o, a, s1, None, op0), *deps)
            return on(lambda e: e.tensor_scalar(o, a, s1, s2, op0, op1), *deps)

        def stt(o, a, s, b, op0, op1, *deps):
            return dve(lambda e: e.scalar_tensor_tensor(out=o, in0=a, scalar=s, in1=b, op0=op0, op1=op1), *deps)

        def af(o, i, f, *deps, scale=1.0, bias=0.0, acc=None):
            if acc is not None:
                return act(lambda e: e.activation(o, i, f, bias=bias, scale=scale, accum_out=acc), *deps)
            return act(lambda e: e.activation(o, i, f, bias=bias, scale=scale), *deps)

        def red(o, i, op, *deps):
            return dve(lambda e: e.tensor_reduce(o, i, AX.X, op), *deps)

        def cp(o, i, *deps):
            return dve(lambda e: e.tensor_copy(o, i), *deps)

        def acp(o, i, *deps):
            return act(lambda e: e.copy(o, i), *deps)

        def rcp(o, i, *deps):
            return dve(lambda e: e.reciprocal(o, i), *deps)

        def bc(a, axis, shape):
            return a.unsqueeze(axis).broadcast_to(shape)

        def hilo(h, l, src, *deps):
            a = acp(h, src, *deps)
            b = tt(l, src, h.bitcast(F32), ALU.subtract, a, *deps)
            return [a, b]

        M1 = at("M1", 21, [128, NC2])
        MK = at("MK", 24, [128, NMASK], U32)
        WQK = at("WQK", 28, [128, 10, 64])
        HNW = at("HNW", 30.5, [128, 128])
        POS = at("POS", 31, [128, 4], I32)

        def cdma(dst, src, s=None):
            return g.sp.dma(lambda e: e.dma_start(dst, src), s or s_const)

        s_first = slot("s_first")
        cdma(C1[:, 0:128], I["c_f32"][:, 0:128], s_first)
        cdma(SM[:, 0:68], I["c_par"], s_first)
        t_c0 = (s_first[0], s_first[1])
        for tb in range(NB):
            cdma(x_sb[:, tb, :], I["x"][0, tb * 128:tb * 128 + 128, :], s_xin[tb])
        t_xin = [(q[0], q[1]) for q in s_xin]
        wplan, wplan2, wplan3, wplan4, wplan5 = make_plan(I)
        st = Stream(g, wplan, wslots[0:3], raw[0:3], hi, lo, 0.0)
        st.load_to(3)
        cdma(C1[:, 128:NC1], I["c_f32"][:, 128:NC1])
        cdma(M1[:, :], I["c_m1"])
        cdma(MK[:, :], I["c_mask"])
        cdma(POS[:, :], I["positions"])
        cdma(WQK[:, :, :].rearrange("p h d -> p (h d)"), I["qk_norm"].partition_broadcast(128)[:, 0, :])
        cdma(HNW[:, :], I["hgrn_norm_w"].partition_broadcast(128)[:, 0, :])
        t_c = [(s_const[0], s_const[1]), t_c0]

        def norm_steps(xs, x_done, xs_read, order=(0, 1, 2, 3)):
            for tb in order:
                c = slice(tb, tb + 1)
                a = af(xs[:, tb, :], x_sb[:, tb, :], ACT.Square, x_done[tb], xs_read, acc=ss4[:, c])
                b = ts(ms4[:, c], ss4[:, c], 1.0 / D, EPS, ALU.mult, ALU.add, a)
                b = af(sd4[:, c], ms4[:, c], ACT.Sqrt, b)
                yield tb, [rcp(rs4[:, c], sd4[:, c], b), a]

        def transposed(xs, scaled, evac, order=(0, 1, 2, 3)):
            fr = {c: g.banks.hold(c)[1] for c in range(8)}
            for tb in order:
                for c in range(8):
                    t = tr(PS[:, c, tb * 128:tb * 128 + 128], xs[:, tb, c * 128:c * 128 + 128], scaled[tb],
                           fr[c] if tb == order[0] else None, t_c0, inc=tb == order[3])
                    if tb == order[3]:
                        fr[c] = t
            for c in range(8):
                g.banks.give(c, evac(c, fr[c]))

        def norm_t(xs, wcol, th, tl, x_done, xs_read, t_read, st, order=(0, 1, 2, 3)):
            scaled = {}
            for tb, r in norm_steps(xs, x_done, xs_read, order):
                scaled[tb] = ts(xs[:, tb, :], x_sb[:, tb, :], rs4[:, tb:tb + 1], None, ALU.mult, None, r)
            st.split_to(st.taken + 1)
            toks = []

            def evac(c, t):
                h = af(th[:, c, :], PS[:, c, :], ACT.Copy, t, t_c0, t_read, scale=wcol[:, c:c + 1])
                l = stt(tl[:, c, :], PS[:, c, :], wcol[:, c:c + 1], th[:, c, :].bitcast(F32), ALU.mult, ALU.subtract,
                        h, t_read)
                toks.append([h, l])
                return [h, l]

            transposed(xs, scaled, evac, order)
            return toks

        def dense_steps(st, key, nu, orient, xh, xl, xdeps, nbk, evac):
            k0 = 0
            for ui in range(nu):
                u, h, l, tok = st.take(key)
                kc = h.shape[1]
                for i in range(nbk):
                    n = h.shape[2] if orient == "a" else 512
                    fr = g.banks.hold(i)[1] if ui == 0 else None
                    o = PS[:, i, 0:n]
                    for kk in range(kc):
                        k = k0 + kk
                        s0 = ui == 0 and kk == 0
                        s1 = ui == nu - 1 and kk == kc - 1
                        dp = [tok, fr if s0 else None, xdeps[k]]
                        if orient == "a":
                            xa, xb = xh[:, k, i * 128:i * 128 + 128], xl[:, k, i * 128:i * 128 + 128]
                            mm(o, xa, h[:, kk, :], s0, False, dp)
                            mm(o, xa, l[:, kk, :], False, False)
                            t = mm(o, xb, h[:, kk, :], False, s1, inc=kk == kc - 1)
                        else:
                            wh, wl = h[:, kk, i * 128:i * 128 + 128], l[:, kk, i * 128:i * 128 + 128]
                            mm(o, wh, xh[:, k, :], s0, False, dp)
                            mm(o, wh, xl[:, k, :], False, False)
                            t = mm(o, wl, xh[:, k, :], False, s1, inc=kk == kc - 1)
                    if i == nbk - 1:
                        st.done(u, t)
                    if ui == nu - 1:
                        g.banks.give(i, evac(i, i, t))
                    g.last = t
                    if st.spread:
                        st.ahead(i)
                    yield 1
                k0 += kc

        def dense(*a):
            for _ in dense_steps(*a):
                pass
            return g.last

        def interleave(main, side):
            def go():
                while main and next(main[0], 0) == 0:
                    main.pop(0)

            for n in side:
                for _ in range(n):
                    go()
            while main:
                go()

        def chain(*gens):
            for ge in gens:
                yield from ge

        xs = at("xs", 64, [128, NB, D])
        xTh, xTl = at("xTh", 32, [128, 8, T], F32R), at("xTl", 48, [128, 8, T], F32R)
        t_xT = norm_t(xs, n1c, xTh, xTl, t_xin, None, None, st)
        t_xs_dead = t_xT

        qkn = at("qkn", 96, [128, NB, 10, 64])
        vn = at("vn", 106, [128, NB, 128])
        qT = at("qT", 108, [128, 4, T])
        kT = at("kT", 116, [128, 2, T])
        sA = [at("sA0", 120, [128, 4, 256]), at("sA1", 80, [128, 4, 256])]
        kd = at("kd", 120, [128, NB, 2, 128])
        pTb = [at("pTb0", 84, [128, 2, 4, 128]), nc.alloc_sbuf_tensor_at("pTb1", [128, 2, 4, 128], F32, offset=spare)]
        attnT = at("attnT", 132, [128, 4, T])
        stg = [at("stg0", 140, [128, 512]), nc.alloc_sbuf_tensor_at("stg1", [128, 512], F32, offset=spare + 4 * KB)]
        sq = at("sq", 116, [128, 2, 640])

        t_q, t_v = [], []

        def ev_q(i, b, t):
            a = cp(qkn[:, i, 0:8, :].rearrange("p h d -> p (h d)"), PS[:, b, :], t)
            t_q.append(a)
            return a

        def ev_kv(i, b, t):
            a = acp(qkn[:, i, 8:10, :].rearrange("p h d -> p (h d)"), PS[:, b, 0:128], t)
            c = acp(vn[:, i, :], PS[:, b, 128:256], t)
            t_q.append(a)
            t_v.append(c)
            return [a, c]

        dense(st, "qa", 2, "a", xTh, xTl, t_xT, 4, ev_q)
        RP = at("RP", 31.125, [128, 4, 8])
        ANG, KF, CS, SN = (at(n, 128 + 0.125 * i, [128, 4, 8]) for i, n in enumerate(("ANG", "KF", "CSt", "SNt")))
        COS, SIN = at("COS", 31.25, [128, 4, 8]), at("SIN", 31.375, [128, 4, 8])
        KI = at("KI", 128.5, [128, 4, 8], I32)
        PF = at("PF", 128.625, [128, 4])
        t = cp(PF[:, :], POS[:, :], t_c)
        t = tt(ANG[:, :, :], bc(PF[:, :], 2, [128, 4, 8]), bc(cst("invf"), 1, [128, 4, 8]), ALU.mult, t, t_c)
        t = ts(KF[:, :, :], ANG[:, :, :], 0.15915494309189535, None, ALU.mult, None, t)
        t = cp(KI[:, :, :], KF[:, :, :], t)
        t = cp(KF[:, :, :], KI[:, :, :], t)
        for cc in (-6.28125, -0.0019350051879882812, -3.0199159819567876e-07):
            t = stt(ANG[:, :, :], KF[:, :, :], cc, ANG[:, :, :], ALU.mult, ALU.add, t)
        t = ts(SN[:, :, :], ANG[:, :, :], 3.1415925, -3.1415925, ALU.min, ALU.max, t)
        t2 = ts(CS[:, :, :], ANG[:, :, :], 1.5707963267948966, None, ALU.add, None, t)
        t2 = ts(KF[:, :, :], CS[:, :, :], 3.141592653589793, -6.283185307179586, ALU.is_gt, ALU.mult, t2)
        t2 = tt(CS[:, :, :], CS[:, :, :], KF[:, :, :], ALU.add, t2)
        t2 = ts(CS[:, :, :], CS[:, :, :], 3.1415925, -3.1415925, ALU.min, ALU.max, t2)
        t_rope = [af(SIN[:, :, :], SN[:, :, :], ACT.Sin, t), af(COS[:, :, :], CS[:, :, :], ACT.Sin, t2)]

        l0, l1 = lbr[:, 0:4], lbr[:, 4:8]
        lm, le0, le1, lsum, lb, oml = (lbs[:, 4 * i:4 * i + 4] for i in range(6))
        t = tt(lm, l0, l1, ALU.max, t_c)
        ta = tt(le0, l0, lm, ALU.subtract, t)
        tb_ = tt(le1, l1, lm, ALU.subtract, t)
        ta = af(le0, le0, ACT.Exp, ta)
        tb_ = af(le1, le1, ACT.Exp, tb_)
        t = tt(lsum, le0, le1, ALU.add, ta, tb_)
        t = rcp(lsum, lsum, t)
        t = tt(lb, le0, lsum, ALU.mult, t)
        t_lb = ts(oml, lb, -1.0, 1.0, ALU.mult, ALU.add, t)

        dense(st, "kv", 2, "a", xTh, xTl, t_xT, 4, ev_kv)

        QS = at("QS", 31.5, [128, 40])
        amask = M1[:, 0:256]
        SS = at("SS", 31.75, [128, 40])
        t_at = []

        def attention():
            t_ss = []
            t_prev = [None, None]
            for i in range(NB):
                a = af(sq[:, i % 2, :], qkn[:, i, :, :].rearrange("p h d -> p (h d)"), ACT.Square, t_q, t_prev[i % 2])
                r = red(QS[:, i * 10:i * 10 + 10], sq[:, i % 2, :].rearrange("p (h d) -> p h d", h=10), ALU.add, a)
                t_prev[i % 2] = r
                t_ss.append(r)
            t = ts(QS[:, :], QS[:, :], 1.0 / 64, EPS, ALU.mult, ALU.add, t_ss)
            t = af(QS[:, :], QS[:, :], ACT.Sqrt, t)
            t = rcp(QS[:, :], QS[:, :], t)
            t_n = []
            for i in range(NB):
                yield i % 2
                a = tt(qkn[:, i, :, :], qkn[:, i, :, :], bc(QS[:, i * 10:i * 10 + 10], 2, [128, 10, 64]), ALU.mult, t, t_q)
                t_n.append(tt(qkn[:, i, :, :], qkn[:, i, :, :], WQK[:, :, :], ALU.mult, a, t_c))
            yield 1
            R = [at(f"R{i}", 80 + 1.25 * i, [128, 4, 10, 8]) for i in range(4)]
            x1, x2 = qkn[:, :, :, 0:8], qkn[:, :, :, 8:16]
            cb = bc(COS[:, :, :], 2, [128, 4, 10, 8])
            sb_ = bc(SIN[:, :, :], 2, [128, 4, 10, 8])
            a1 = tt(R[0][:, :, :, :], x1, cb, ALU.mult, t_n, t_rope)
            a2 = tt(R[1][:, :, :, :], x2, sb_, ALU.mult, t_n, t_rope)
            a3 = tt(R[2][:, :, :, :], x2, cb, ALU.mult, t_n)
            a4 = tt(R[3][:, :, :, :], x1, sb_, ALU.mult, t_n)
            b1 = tt(x1, R[0][:, :, :, :], R[1][:, :, :, :], ALU.subtract, a1, a2, a4)
            b2 = tt(x2, R[2][:, :, :, :], R[3][:, :, :, :], ALU.add, a3, a4, a2)
            t_r = [b1, b2]
            t_kd = []
            for i in range(NB):
                for rep in range(2):
                    t_kd.append(cp(kd[:, i, :, rep * 64:rep * 64 + 64], qkn[:, i, 8:10, :], t_r))
            t_qT = []
            yield 3
            for j in range(4):
                b, fr = g.banks.take()
                for i in range(NB):
                    t = tr(PS[:, b, i * 128:i * 128 + 128], qkn[:, i, 2 * j:2 * j + 2, :].rearrange("p h d -> p (h d)"),
                           t_r, fr, inc=i == 3)
                a = acp(qT[:, j, :], PS[:, b, :], t)
                g.banks.give(b, a)
                t_qT.append(a)
            for j in range(2):
                b, fr = g.banks.take()
                for i in range(NB):
                    t = tr(PS[:, b, i * 128:i * 128 + 128], kd[:, i, j, :], t_kd, fr, inc=i == 3)
                a = acp(kT[:, j, :], PS[:, b, :], t, t_ss)
                g.banks.give(b, a)
                t_qT.append(a)
            yield 1
            t_sfree = [t_qT, t_qT]
            t_pT = [None, None]

            def scores(it):
                n, j = it // 2, it % 2
                W = 256 if n else 128
                k0 = (n - 1) * 128 if n else 0
                s = sA[it % 2][:, :, 0:W]
                c = SS[:, 20 * (it % 2):20 * (it % 2) + 20]
                mx, es, l, nm = c[:, 0:4], c[:, 4:8], c[:, 8:12], c[:, 12:16]
                b, fr = g.banks.take(2)
                for par in range(2):
                    for jj in range(2):
                        pr = 2 * j + jj
                        t = mm(PS[:, b + par, jj * 256:jj * 256 + W], qT[par * 64:par * 64 + 64, pr, n * 128:n * 128 + 128],
                               kT[par * 64:par * 64 + 64, j, k0:k0 + W], True, True, t_qT, fr, inc=jj == 1)
                pv = PS[:, b:b + 2, :].rearrange("p b (c w) -> p (b c) w", w=256)[:, :, 0:W]
                so = sink[:, 4 * j:4 * j + 4].rearrange("p (c e) -> p e c", e=2)
                t = stt(s, pv, 0.125, bc(amask[:, 256 - W:256], 1, [128, 4, W]), ALU.mult, ALU.add, t, t_c,
                        t_sfree[it % 2])
                g.banks.give(b, t, 2)
                t2 = red(mx, s, ALU.max, t)
                t2 = tt(mx.rearrange("p (e c) -> p e c", e=2), mx.rearrange("p (e c) -> p e c", e=2), so, ALU.max, t2)
                t4 = tt(es.rearrange("p (e c) -> p e c", e=2), so, mx.rearrange("p (e c) -> p e c", e=2), ALU.subtract, t2)
                t3 = ts(nm, mx, -1.0, None, ALU.mult, None, t2)
                te = [af(s[:, q, :], s[:, q, :], ACT.Exp, t3, t, bias=nm[:, q:q + 1], acc=l[:, q:q + 1]) for q in range(4)]
                te.append(af(es, es, ACT.Exp, t4))
                return n, j, W, s, c, te

            def weights(st_):
                n, j, W, s, c, te = st_
                it = 2 * n + j
                t5 = tt(c[:, 8:12], c[:, 8:12], c[:, 4:8], ALU.add, te)
                t5 = rcp(c[:, 16:20], c[:, 8:12], t5)
                return tt(s, s, bc(c[:, 16:20], 2, [128, 4, W]), ALU.mult, t5, te)

            def turned(st_, t6):
                n, j, W, s, c, te = st_
                it = 2 * n + j
                ev = []
                for kb in range(W // 128):
                    b, fr = g.banks.take()
                    for hh in range(4):
                        t = tr(PS[:, b, hh * 128:hh * 128 + 128], s[:, hh, kb * 128:kb * 128 + 128], t6, fr, inc=hh == 3)
                    a = acp(pTb[it % 2][:, kb, :, :].rearrange("p h q -> p (h q)"), PS[:, b, :], t, t_pT[it % 2])
                    g.banks.give(b, a)
                    ev.append(a)
                t_sfree[it % 2] = ev
                return ev

            def values(st_, ev):
                n, j, W, s, c, te = st_
                it, nkb = 2 * n + j, W // 128
                b, fr = g.banks.take()
                for par in range(2):
                    for kb in range(nkb):
                        t = mm(PS[par * 64:par * 64 + 64, b, 0:256], vn[:, n - nkb + 1 + kb, j * 64:j * 64 + 64],
                               pTb[it % 2][:, kb, 2 * par:2 * par + 2, :].rearrange("p h q -> p (h q)"), kb == 0,
                               kb == nkb - 1, ev, t_v, fr, inc=kb == nkb - 1)
                t_pT[it % 2] = t
                a = acp(attnT[:, 2 * j:2 * j + 2, n * 128:n * 128 + 128],
                        PS[:, b, 0:256].rearrange("p (c q) -> p c q", c=2), t)
                g.banks.give(b, a)
                t_at.extend([a, t])

            sc, ev = {}, {}
            for it in range(10):
                if 0 <= it - 1 < 8:
                    t6 = weights(sc[it - 1])
                if it < 8:
                    sc[it] = scores(it)
                    yield 1
                if 0 <= it - 1 < 8:
                    ev[it - 1] = turned(sc[it - 1], t6)
                if it >= 2:
                    values(sc[it - 2], ev[it - 2])
                yield 1

        qh, bb = at("qh", 64, [128, 4, T]), at("bb", 72, [128, 4, T])
        kh, vh = at("kh", 80, [128, 4, T]), at("vh", 88, [128, NB, 512])
        t_qh, t_fg, t_vh = {}, {}, []

        def ev_qh(i, b, t):
            t_qh[i] = af(qh[:, i, :], PS[:, b, :], ACT.Silu, t, t_xs_dead)
            return t_qh[i]

        def ev_fh(i, b, t):
            t_fg[i] = acp(bb[:, i, :], PS[:, b, :], t, t_xs_dead)
            return t_fg[i]

        def ev_vh(i, b, t):
            t_vh.append(acp(vh[:, i, :], PS[:, b, :], t))
            return t_vh[-1]


        gs = at("gs", 124, [128, NB, 512])
        t_gs = []

        def ev_gh(i, b, t):
            t_gs.append(acp(gs[:, i, :], PS[:, b, :], t, t_rope))
            return t_gs[-1]

        s_z = [slot("s_z0"), slot("s_z1")]
        t_z = [None, None]
        zi = [0]

        def ev_z(i, b, t):
            c = zi[0]
            zi[0] += 1
            sg = stg[c % 2]
            a = acp(sg[:, :], PS[:, b, :], t, t_z[c % 2])
            t_z[c % 2] = g.act.dma(lambda e: e.dma_start(zsp[c, :, :], sg[:, :]), s_z[c % 2], a)
            return a

        g.banks.span(4, 8)
        evs = {"qh": ev_qh, "fh": ev_fh, "ih": ev_vh, "gh": ev_gh}
        inproj = [dense_steps(st, n, 2, "a" if n in ("ih", "gh") else "b", xTh, xTl, t_xT, 4, evs.get(n, ev_z))
                  for n, _, _ in INP[2:]]
        t_attn = []

        def hgrn():
            E = [at("E0", 96, [128, T]), at("E1", 98, [128, T])]
            QE = [at("QE0", 100, [128, T]), at("QE1", 102, [128, T])]
            KE = [at("KE0", 104, [128, T]), at("KE1", 106, [128, T])]
            AT = [at("AT0", 108, [128, T]), at("AT1", 110, [128, T])]
            ho = at("ho", 112, [128, 4, NB, 128])
            St = at("St", 120, [128, 128])
            QB = at("QB", 120.5, [128, T])
            KN = at("KN", 122.5, [128, 3, 128])
            TK = nc.alloc_sbuf_tensor_at("TK", [128, T], F32, offset=spare)
            hss = at("hss", 31.5, [128, 16])
            eb = at("eb", 31.5625, [128, 4])
            z = [dve(lambda e, A=A: e.memset(A[:, :], 0.0), t_at) for A in AT]
            t_attn.extend(t_at)
            t_ho = []
            tE, tQ, tK, tA = [None, None], [None, None], [None, None], [z[0], z[1]]
            yield 1
            for i in range(NB):
                t_gs[i] = af(gs[:, i, :], gs[:, i, :], ACT.Silu, t_gs[i])
            tsg = [af(bb[:, h, :], bb[:, h, :], ACT.Sigmoid, t_fg[h]) for h in range(4)]
            for h in range(4):
                t_fg[h] = ts(bb[:, h, :], bb[:, h, :], oml[:, h:h + 1], lb[:, h:h + 1], ALU.mult, ALU.add, tsg[h], t_lb)
            yield 1
            lns = [af(kh[:, h, :], bb[:, h, :], ACT.Ln, t_fg[h], t_at) for h in range(4)]
            scans, kks = [], []
            for h in range(4):
                tk = af(E[h % 2][:, :], bb[:, h, :], ACT.Copy, t_fg[h], lns[h], t_attn, tE[h % 2], scale=-1.0, bias=1.0)
                t = dve(lambda e, h=h: e.tensor_tensor_scan(bb[:, h, :], M1[:, 256:768], kh[:, h, :], 0.0, ALU.mult, ALU.add),
                        lns[h], t_c, tk)
                tc_ = cp(kh[:, h, :], E[h % 2][:, :], tk, t)
                tE[h % 2] = tc_
                scans.append(t)
                kks.append(tc_)
                yield h % 2

            def decay(h, lv, p):
                e_ = E[p]
                hw = 64 >> lv
                nb = T // (2 * hw)
                bv = bb[:, h, :].rearrange("p (n w) -> p n w", w=2 * hw)
                t = tt(e_[:, :].rearrange("p (n w) -> p n w", w=2 * hw), bv,
                       bv[:, :, hw - 1:hw].broadcast_to([128, nb, 2 * hw]), ALU.subtract, scans[h], kks[h], tE[p])
                t = af(e_[:, :], e_[:, :], ACT.Abs, t)
                return af(e_[:, :], e_[:, :], ACT.Exp, t, scale=-1.0)

            def scaled(h, lv, p, td):
                if lv == 7:
                    return qh[:, h, :], kh[:, h, :], [t_qh[h], kks[h]]
                q_, k_ = QE[p], KE[p]
                tk = tt(k_[:, :], kh[:, h, :], E[p][:, :], ALU.mult, td, kks[h], tK[p], on=pool)
                tq = tt(q_[:, :], qh[:, h, :], E[p][:, :], ALU.mult, td, t_qh[h], tQ[p])
                tE[p] = [tq, tk]
                return q_[:, :], k_[:, :], [tq, tk]

            def products(h, lv, p, qs, ks, tq):
                b, fr = g.banks.take()
                for c in range(4):
                    t = mm(PS[:, b, c * 128:c * 128 + 128], ks[:, c * 128:c * 128 + 128], qs[:, c * 128:c * 128 + 128],
                           True, True, tq, fr, inc=c == 3)
                if lv < 7:
                    tQ[p] = tK[p] = t
                return b, t

            def place(h, lv, b, t):
                av = AT[h % 2][:, :].rearrange("p (c t) -> p c t", c=4)
                a = dve(lambda e: e.copy_predicated(
                    av, bc(MK[:, lv * 128:lv * 128 + 128], 1, [128, 4, 128]),
                    PS[:, b, :].rearrange("p (c t) -> p c t", c=4)), t, tA[h % 2], t_c)
                g.banks.give(b, a)
                tA[h % 2] = a

            s_free = [None, None, None, None]

            hTh, hTl = at("hTh", 64, [128, 4, T], F32R), at("hTl", 72, [128, 4, T], F32R)
            g.t_hT = []

            def tail(h):
                AH = AT[h % 2]
                b3 = bb[:, h, :]
                tb0 = [scans[h], kks[h]]
                t1 = af(QB[:, :], b3, ACT.Exp, tb0, s_free[0])
                bv = b3.rearrange("p (n w) -> p n w", w=128)
                t = tt(TK[:, :].rearrange("p (n w) -> p n w", w=128), bv, bv[:, :, 127:128].broadcast_to([128, 4, 128]),
                       ALU.subtract, tb0, s_free[1])
                t = af(TK[:, :], TK[:, :], ACT.Exp, t, scale=-1.0)
                te = af(eb[:, :], bv[:, :, 127], ACT.Exp, tb0, s_free[3])
                if h < 3:
                    yield 1
                t1 = tt(QB[:, :], QB[:, :], qh[:, h, :], ALU.mult, t1)
                t = tt(TK[:, :], TK[:, :], kh[:, h, :], ALU.mult, t, on=pool)
                if h == 3:
                    g.hgrn_levels = [tE, tQ, tK, t]
                    for c in range(4):
                        t_aT.append(hilo(aTh[:, c, :], aTl[:, c, :], attnT[:, c, :], t_attn, g.hgrn_levels))
                yield 1
                gv = gs[:, :, h * 128:h * 128 + 128]
                t_gs.append(tt(gv, gv, bc(HNW[:, :], 1, [128, NB, 128]), ALU.mult, t_gs, t_c, on=pool))
                b, fr = g.banks.take()
                for c in range(3):
                    t2 = tr(PS[:, b, c * 128:c * 128 + 128], TK[:, c * 128:c * 128 + 128], t, fr, inc=c == 2)
                a = acp(KN[:, :, :].rearrange("p c k -> p (c k)"), PS[:, b, 0:384], t2, s_free[2])
                g.banks.give(b, a)
                yield 1
                bo, fro = g.banks.take()
                tS = s_free[3]
                for c in range(4):
                    o = PS[:, bo, c * 128:c * 128 + 128]
                    v = vh[:, c, h * 128:h * 128 + 128]
                    if c < 3:
                        b, fr = g.banks.take()
                        t3 = mm(PS[:, b, 0:128], KN[:, c, :], v, True, True, a, t_vh, fr, inc=True)
                    t = mm(o, AH[:, c * 128:c * 128 + 128], v, True, c == 0, tA[h % 2], t_vh, fro, inc=c == 0)
                    if c:
                        t = mm(o, QB[:, c * 128:c * 128 + 128], St[:, :], False, True, t1, tS, inc=True)
                    if c < 3:
                        if c == 0:
                            tS = cp(St[:, :], PS[:, b, 0:128], t3, tS, t)
                        else:
                            tS = stt(St[:, :], St[:, :], eb[:, c:c + 1], PS[:, b, 0:128], ALU.mult, ALU.add, t3, tS, te, t)
                        g.banks.give(b, tS)
                    yield 1
                tA[h % 2] = [t, tA[h % 2]]
                hv = ho[:, h, :, :].rearrange("p c v -> p (c v)")
                a = cp(hv, PS[:, bo, :], t)
                g.banks.give(bo, a)
                t4 = tsq = af(TK[:, :], hv, ACT.Square, a, t2)
                yield 1
                hs = hss[:, 4 * h:4 * h + 4]
                t4 = red(hs, TK[:, :].rearrange("p (c v) -> p c v", c=4), ALU.add, t4)
                s_free[0], s_free[1], s_free[2], s_free[3] = t, t4, t3, [tS, t]
                t4 = ts(hs, hs, 1.0 / 128, EPS, ALU.mult, ALU.add, t4)
                t4 = af(hs, hs, ACT.Ln, t4)
                t4 = af(hs, hs, ACT.Exp, t4, scale=-0.5)
                a = tt(ho[:, h, :, :], ho[:, h, :, :], gs[:, :, h * 128:h * 128 + 128], ALU.mult, a, tsq, t_gs, on=pool)
                yield 1
                a = tt(ho[:, h, :, :], ho[:, h, :, :], bc(hs, 2, [128, NB, 128]), ALU.mult, a, t4)
                yield 1
                b, fr = g.banks.take()
                for c in range(4):
                    t2 = tr(PS[:, b, c * 128:c * 128 + 128], ho[:, h, c, :], a, fr, inc=c == 3)
                x = hilo(hTh[:, h, :], hTl[:, h, :], PS[:, b, :], t2, scans[h], kks[h], tE, tQ, tK, s_free)
                g.banks.give(b, x)
                g.t_hT.append(x)
                t_ho.append([a, t2])
                yield 1

            todo = [(h, lv) for h in range(4) for lv in range(8)]
            tails = []
            td, sc, pr = {}, {}, {}
            for i in range(len(todo) + 3):
                if 0 <= i - 1 < len(todo):
                    sc[i - 1] = scaled(*todo[i - 1], (i - 1) % 2, td.get(i - 1))
                if i < len(todo) and todo[i][1] < 7:
                    td[i] = decay(*todo[i], i % 2)
                if 0 <= i - 2 < len(todo):
                    pr[i - 2] = products(*todo[i - 2], (i - 2) % 2, *sc[i - 2])
                if i >= 3:
                    place(*todo[i - 3], *pr[i - 3])
                    if todo[i - 3][1] == 7:
                        tails.append(tail(todo[i - 3][0]))
                for q in list(tails):
                    next(q, None)
                yield 1
            for q in tails:
                yield from q
            g.hgrn_end = [t_ho, g.t_hT, tE, tQ, tK, tA, s_free, t_gs]
            g.hTh, g.hTl = hTh, hTl

        aTh, aTl = at("aTh", 96, [128, 4, T], F32R), at("aTl", 80, [128, 4, T], F32R)
        mTh, mTl = at("mTh", 32, [128, 8, T], F32R), at("mTl", 48, [128, 8, T], F32R)
        zr = [[at(f"zr{c}{i}", o[i // 4] + 2 * (i % 4), [128, 512]) for i in range(8)]
              for c, o in enumerate(((40, 56), (112, 120)))]
        s_zr = [[slot(f"s_zr{c}{i}") for i in range(8)] for c in range(2)]
        t_aT, t_mT, ta_, zl = [], [], {}, {}
        t_z0 = [[], []]

        def branch_loads(c):
            for i in range(4):
                for w in range(2):
                    q = 2 * i + w
                    t = g.pool.dma(lambda e, q=q, w=w, i=i: e.dma_start(zr[c][q][:, :], zsp[8 * w + 4 * c + i, :, :]),
                                   s_zr[c][q], t_z, t_z0[c])
                    zl[c, q] = t

        def ev_ba(c):
            def f(i, b, t):
                for q in (2 * i, 2 * i + 1):
                    zl[c, q] = af(zr[c][q][:, :], zr[c][q][:, :], ACT.Sigmoid, zl[c, q])
                z = zr[c][2 * i]
                ta_[c, i] = tt(z[:, :], z[:, :], PS[:, b, :], ALU.mult, t, zl[c, 2 * i])
                return ta_[c, i]
            return f

        def ev_bh(c):
            def f(i, b, t):
                z0, z1 = zr[c][2 * i][:, :], zr[c][2 * i + 1][:, :]
                a = tt(z1, z1, PS[:, b, :], ALU.mult, t, zl[c, 2 * i + 1])
                s = tt(z0, z0, z1, ALU.add, a, ta_[c, i])
                t_mT.append(hilo(mTh[:, 4 * c + i, :], mTl[:, 4 * c + i, :], z0, s, t_z0[0], t_mT if c else None))
                return a
            return f

        def branch_a():
            assert g.hgrn_levels
            t_z0[0].append(g.last)
            branch_loads(0)
            yield from dense_steps(st, ("ba", 0), 1, "b", aTh, aTl, t_aT, 4, ev_ba(0))

        inproj.append(branch_a())
        g.hgrn_levels = None
        st.spread = True
        interleave(inproj, chain(attention(), hgrn()))
        st.spread = False
        t_z0[1].append(g.hgrn_end)
        g.banks.span(0, 8)
        n2b = at("n2b", 128, [128, D])
        WR = at("WR", 29, [128, 8, 36])
        BR = at("BR", 30.25, [128, 36])
        s_r = slot("s_r")
        g.pool.dma(lambda e: e.dma_start(n2b[:, :], I["norm2_w"].partition_broadcast(128)[:, 0, :]), s_r, g.hgrn_end,
                   t_attn, t_gs)
        g.pool.dma(lambda e: e.dma_start(WR[:, :, :], I["w_router"]), s_r)
        g.pool.dma(lambda e: e.dma_start(BR[:, :], I["b_router"].partition_broadcast(128)[:, 0, :]), s_r)
        t_r = (s_r[0], s_r[1])

        for c in range(2):
            if c:
                branch_loads(c)
                dense(st, ("ba", c), 1, "b", aTh, aTl, t_aT, 4, ev_ba(c))
            dense(st, ("bh", c), 1, "b", g.hTh, g.hTl, g.t_hT, 4, ev_bh(c))
        t_x2 = [None] * NB

        def ev_add(c):
            def f(i, b, t):
                v = x_sb[:, i, c * 512:c * 512 + 512]
                a = tt(v, v, PS[:, b, :], ALU.add, t)
                t_x2[i] = a
                return a
            return f

        for c in range(2):
            t_wo = dense(st, ("wo", c), 2, "a", mTh, mTl, t_mT, 4, ev_add(c))

        hn = at("hn", 32, [128, NB, D])
        hnT = at("hnT", 48, [128, 8, T])
        hnh, hnl = at("hnh", 64, [128, NB, D], F32R), at("hnl", 80, [128, NB, D], F32R)
        Lg = at("Lg", 102, [128, 4, 36])
        moe_free = [t_wo, g.t_hT, t_aT, t_mT, g.hgrn_end]
        t_hn = [stt(hn[:, tb, :], x_sb[:, tb, :], rs4[:, tb:tb + 1], n2b[:, :], ALU.mult, ALU.mult, r, t_r)
                for tb, r in norm_steps(hn, t_x2, moe_free)]
        t_hT2 = []

        def ev_hnT(c, t):
            t_hT2.append((cp if c % 2 else acp)(hnT[:, c, :], PS[:, c, :], t, moe_free))
            return t_hT2[-1]

        transposed(hn, t_hn, ev_hnT)
        bl = [g.banks.take() for _ in range(NB)]
        t_lg = []
        for k in range(8):
            for tb in range(NB):
                b, fr = bl[tb]
                t = mm(PS[:, b, 0:36], hnT[:, k, tb * 128:tb * 128 + 128], WR[:, k, :], k == 0, k == 7, t_hT2[k], t_r, fr,
                       inc=k == 7)
                if k == 7:
                    t_lg.append(tt(Lg[:, tb, :], PS[:, b, 0:36], BR[:, :], ALU.add, t, t_r))
                    g.banks.give(b, t_lg[tb])
        t_hs = []
        for tb in range(NB):
            a = acp(hnh[:, tb, :], hn[:, tb, :], t_hn, moe_free)
            t_hs.append([a, tt(hnl[:, tb, :], hn[:, tb, :], hnh[:, tb, :].bitcast(F32), ALU.subtract, a, on=pool)])

        mraw = [raw[3], rawx, raw[0], raw[1], raw[2]]
        mhi, mlo = hi + [hix], lo + [lox]
        mst = Stream(g, wplan2, mslots, mraw, mhi, mlo, 0.4375,
                     [[g.hgrn_end, t_attn, t_z], [g.hgrn_end, t_attn, t_gs]] + [st.raw_end(i) for i in range(3)],
                     [st.hl_end(0), st.hl_end(1), [moe_free, t_hn, t_attn, t_z]])
        mst.split_to(3)

        OU = at("OU", 142.5, [128, 256], F32R)
        t_ou = [cp(OU[:, 0:128], ones, t_c), cp(OU[:, 128:256], cst("ustrict"), t_c)]
        RT = at("RT", 103, [128, 1600])
        ro = [0]

        def rt(n):
            o = ro[0]
            ro[0] += n
            assert ro[0] <= 1600
            return RT[:, o:o + n]

        lg, le = Lg[:, :, 0:4], Lg[:, :, 4:36].rearrange("p b (g j) -> p b g j", g=4)

        def first_max(v, n, t, dec):
            m = rt(4)
            eq, s = rt(4 * n).rearrange("p (b n) -> p b n", b=4), rt(4)
            t1 = red(m, v, ALU.max, t)
            t2 = tt(eq, v, bc(m, 2, [128, 4, n]), ALU.is_equal, t1)
            t2 = tt(eq, eq, bc(dec, 1, [128, 4, n]), ALU.mult, t2)
            t2 = red(s, eq, ALU.max, t2)
            t2 = tt(eq, eq, bc(s, 2, [128, 4, n]), ALU.is_equal, t2)
            return m, eq, t1, t2

        dec8 = cst("dec8")
        gm, g1h, tgm, tg = first_max(lg, 4, t_lg, dec8[:, 4:8])
        ls = rt(128).rearrange("p (b g j) -> p b g j", b=4, g=4)
        lsel = rt(32).rearrange("p (b j) -> p b j", b=4)
        t = tt(ls, le, bc(g1h, 3, [128, 4, 4, 8]), ALU.mult, tg)
        t = red(lsel, ls.rearrange("p b g j -> p b j g"), ALU.add, t)
        m1, o1, tm1, to1 = first_max(lsel, 8, t, dec8)
        l2 = rt(32).rearrange("p (b j) -> p b j", b=4)
        t = stt(l2, o1, -3e38, lsel, ALU.mult, ALU.add, to1)
        m2, o2, tm2, to2 = first_max(l2, 8, t, dec8)
        O = [rt(128).rearrange("p (b g j) -> p b g j", b=4, g=4) for _ in range(2)]
        t_o = [tt(O[k], bc(g1h, 3, [128, 4, 4, 8]), bc(o, 2, [128, 4, 4, 8]), ALU.mult, tg, tt_)
               for k, (o, tt_) in enumerate(((o1, to1), (o2, to2)))]
        Of = [o.rearrange("p b g j -> p b (g j)") for o in O]
        M = at("M", 31, [128, 4, 32], F32R)
        t_m = tt(M[:, :, :], Of[0], Of[1], ALU.add, t_o, moe_free)
        b, fr = g.banks.take()
        for tb in range(NB):
            for q in range(tb + 1):
                t = mm(PS[:, b, tb * 32:tb * 32 + 32], OU[:, 0:128] if q < tb else OU[:, 128:256], M[:, q, :], q == 0, q == tb,
                       t_m, t_ou, fr, inc=q == tb)
        for q in range(NB):
            t = mm(PS[:, b, 128:160], OU[:, 0:128], M[:, q, :], q == 0, q == 3, inc=q == 3)
        cnt = rt(32)
        WE = at("WE", 116, [128, 256])
        rkm = WE[:, 0:128].rearrange("p (b e) -> p b e", b=4)
        t_rkm = stt(rkm, PS[:, b, 0:128].rearrange("p (b e) -> p b e", b=4), 1.0, M[:, :, :].bitcast(F32), ALU.add, ALU.mult, t, t_m)
        S = [at(f"S{i}", 137.5 + 2 * i, [128, NB, 2, WIN], F32R) for i in range(2)]

        def choose(i, t_rkm, t_read):
            return tt(S[i % 2][:, :, :, :], bc(rkm[:, :, 2 * i:2 * i + 2], 3, [128, NB, 2, WIN]),
                      cst("iota").unsqueeze(1).unsqueeze(1).broadcast_to([128, NB, 2, WIN]), ALU.is_equal, t_rkm, t_read)

        t_S0 = choose(0, t_rkm, [moe_free, t_attn])
        t_n = cp(cnt, PS[:, b, 128:160], t)
        g.banks.give(b, [t_rkm, t_n])
        dlg, gsum = rt(16).rearrange("p (b n) -> p b n", b=4), rt(4)
        t = tt(dlg, lg, bc(gm, 2, [128, 4, 4]), ALU.subtract, tgm)
        t = af(dlg, dlg, ACT.Exp, t)
        t = red(gsum, dlg, ALU.add, t)
        t_pg = rcp(gsum, gsum, t)
        e2, den = rt(4), rt(4)
        t = tt(e2, m2, m1, ALU.subtract, tm1, tm2)
        t = af(e2, e2, ACT.Exp, t)
        t3 = ts(den, e2, 1.0, None, ALU.add, None, t)
        t3 = rcp(den, den, t3)
        gwv = gw.rearrange("p (b k) -> p b k", k=2)
        t3 = tt(gwv[:, :, 0], gsum, den, ALU.mult, t3, t_pg)
        t_gw = tt(gwv[:, :, 1], gwv[:, :, 0], e2, ALU.mult, t3, t)
        mxn, stp, pf = rt(1), rt(8), rt(1)
        t = red(mxn, cnt, ALU.max, t_n)
        t = ts(stp, cst("step8"), mxn, None, ALU.is_lt, None, t, t_c)
        t = red(pf, stp, ALU.add, t)
        t_P = cp(PI[:, 0:1], pf, t)
        we = WE[:, 128:256].rearrange("p (b e) -> p b e", b=4)
        t0_ = [tt(Of[k], Of[k], bc(gwv[:, :, k], 2, [128, 4, 32]), ALU.mult, t_gw, t_o, t_m, t3) for k in range(2)]
        t_we = tt(we, Of[0], Of[1], ALU.add, t0_)
        t_rt = [t_we, t_P, t_lg, t_rkm]
        XG = [at(f"XG{i}", 32 + 8 * i, [128, 8, 2, 2, WIN], F32R) for i in range(2)]
        GS = [at(f"GS{i}", 48 + 2 * i, [128, 512]) for i in range(2)]
        US = [at(f"US{i}", 52 + 2 * i, [128, 512]) for i in range(2)]
        HT = [at(f"HT{i}", 56 + 2 * i, [128, 4, 2, WIN], F32R) for i in range(2)]
        SG, HF = at("SG", 60, [128, 256]), at("HF", 61, [128, 256])
        GR = at("GR", 62, [128, 512])
        YT = at("YT", 133.5, [128, D])
        YH = [at(f"YH{i}", 96 + 4 * i, [128, D], F32R) for i in range(2)]
        YL = [at(f"YL{i}", 104 + 4 * i, [128, D], F32R) for i in range(2)]
        ST = [at(f"ST{i}", o, [128, NB, 128], F32R) for i, o in enumerate((112, 114, 29, 141.5))]
        NP = NE // 2

        def experts(st, t0, t_rkm, t_we, x_done, first=None):
            tS, tXG, tGS, tHT = [None] * 2, [None] * 2, [None] * 2, [None] * 2
            tST, tY, tYH, tws = [None] * 4, None, [None] * 2, [None] * 4
            tGR = tSG = None
            xg, xt = {}, {(tb, c): x_done[tb] for tb in range(NB) for c in range(2)}
            ready = {}

            def gather(i):
                nonlocal tGR
                p = i % 2
                if i >= NE // 2:
                    return
                t = first if first and i == 0 else choose(i, t_rkm, [tS[p], t0])
                xg[i] = ev = []
                yield
                for c4 in range(2):
                    b, fr = g.banks.take()
                    for tb in range(NB):
                        sv = S[p][:, tb, :, :].rearrange("p e s -> p (e s)")
                        for src in (hnh, hnl):
                            t2 = mm(PS[:, b, :], sv, src[:, tb, c4 * 512:c4 * 512 + 512], tb == 0 and src is hnh,
                                    tb == 3 and src is hnl, t, t_hs, fr, inc=tb == 3 and src is hnl)
                    a = acp(GR[:, :], PS[:, b, :], t2, tGR, t0)
                    g.banks.give(b, a)
                    yield
                    b, fr = g.banks.take()
                    for c in range(4):
                        t2 = tr(PS[:, b, c * 128:c * 128 + 128], GR[:, c * 128:c * 128 + 128], a, fr, inc=c == 3)
                    tGR = t2
                    xv = PS[:, b, :].rearrange("p (c e s) -> p c e s", c=4, e=2)
                    xh, xl = (XG[p][:, 4 * c4:4 * c4 + 4, :, hl, :] for hl in range(2))
                    h = acp(xh, xv, t2, tXG[p], t0)
                    l = tt(xl, xv, xh.bitcast(F32), ALU.subtract, h, t2, tXG[p], t0)
                    g.banks.give(b, [h, l])
                    ev.extend([h, l])
                    yield
                sv = [S[p][:, tb, :, :].rearrange("p e s -> p (e s)").bitcast(F32) for tb in range(NB)]
                b, fr = g.banks.take()
                for tb in range(NB):
                    t2 = tr(PS[:, b, tb * 128:tb * 128 + 128], sv[tb], t, fr, inc=tb == 3)
                a = acp(ST[i % 4][:, :, :].rearrange("p b t -> p (b t)"), PS[:, b, :], t2, tST[i % 4], t0)
                g.banks.give(b, a)
                b, fr = g.banks.take()
                for tb in range(NB):
                    t2 = mm(PS[:, b, 0:2], sv[tb], we[:, tb, 2 * i:2 * i + 2], tb == 0, tb == 3, t, t_we, fr, inc=tb == 3)
                tS[p] = t2
                w = [cp(ws[64 * e:64 * e + 64, i % 4:i % 4 + 1], PS[64 * e:64 * e + 64, b, e:e + 1], t2, tws[i % 4])
                     for e in range(2)]
                g.banks.give(b, w)
                marks[i] = [a, w]
                yield

            fold_in, marks = {}, {}

            def product(kind, e, dst, cpy):
                p, q = (e // 2) % 2, e % 2
                b, fr = g.banks.take()
                for ui in range(2):
                    u, h, l, tok = st.take((kind, e))
                    for kk in range(4):
                        k = 4 * ui + kk
                        xw = XG[p][:, k, q, :, :].rearrange("p a s -> p (a s)")
                        mm(PS[:, b, :], xw, h[:, kk, :], k == 0, False, tok, xg[e // 2], fr)
                        t = mm(PS[:, b, :], xw, l[:, kk, :], False, k == 7, inc=kk == 3)
                    st.done(u, t)
                    st.split_to(u + 1 + st.nh)
                a = cpy(dst[:, :], PS[:, b, :], t, tGS[q], t0)
                g.banks.give(b, a)
                tXG[p] = t
                return a

            def gate(e):
                fold_in[e] = [product("g", e, GS[e % 2], acp)]

            def up_(e):
                fold_in[e].append(product("u", e, US[e % 2], cp))

            def act_fold(e):
                nonlocal tSG
                q = e % 2
                b, fr = g.banks.take()
                for o, src in ((0, GS[q]), (256, US[q])):
                    for j in range(4):
                        t = mm(PS[:, b, o + j * 64:o + j * 64 + 64], src[:, j * 128:j * 128 + 128], fold, True, True,
                               fold_in[e], fr, t_c, inc=j == 3)
                tGS[q] = t
                a = af(SG[:, :], PS[:, b, 0:256], ACT.Silu, t, tSG, t0)
                tSG = m = tt(HF[:, :], SG[:, :], PS[:, b, 256:512], ALU.mult, a)
                g.banks.give(b, [a, m])
                hv = HF[:, :].rearrange("p (j s) -> p j s", j=4)
                a = cp(HT[q][:, :, 0, :], hv, m, tHT[q])
                l = tt(HT[q][:, :, 1, :], hv, HT[q][:, :, 0, :].bitcast(F32), ALU.subtract, a, tHT[q])
                return [a, l]

            def down(e, th):
                q, y = e % 2, YT
                r0, r1 = (0, 64) if q == 0 else (64, 0)
                outs = []
                for c in range(2):
                    b, fr = g.banks.take()
                    u, h, l, tok = st.take(("d", e))
                    for j in range(4):
                        hw = HT[q][:, j, :, :].rearrange("p a s -> p (a s)")
                        mm(PS[:, b, :], hw, h[:, j, :], j == 0, False, tok, th, fr)
                        t = mm(PS[:, b, :], hw, l[:, j, :], False, j == 3, inc=j == 3)
                    st.done(u, t)
                    yv = y[r0:r0 + 64, c * 512:c * 512 + 512]
                    a = acp(yv, PS[r0:r0 + 64, b, :], t, tY, t0)
                    m = tt(yv, PS[r1:r1 + 64, b, :], yv, ALU.add, a)
                    g.banks.give(b, [a, m])
                    outs.append(m)
                tHT[q] = t
                return outs

            def weighted(i, yo):
                nonlocal tY
                p, w = i % 2, ws[:, i % 4:i % 4 + 1]
                h = af(YH[p][:, :], YT[:, :], ACT.Copy, yo, marks[i], tYH[p], t0, scale=w)
                l = stt(YL[p][:, :], YT[:, :], w, YH[p][:, :].bitcast(F32), ALU.mult, ALU.subtract, h, yo, marks[i], tYH[p])
                tY = tws[i % 4] = [h, l]
                ready[i] = [h, l, marks[i]]

            def combine(pairs):
                for tb in range(NB):
                    for c in range(2):
                        b, fr = g.banks.take()
                        for i in pairs:
                            for y in (YH[i % 2], YL[i % 2]):
                                s0, s1 = i == pairs[0] and y is YH[i % 2], i == pairs[-1] and y is YL[i % 2]
                                t = mm(PS[:, b, :], ST[i % 4][:, tb, :], y[:, c * 512:c * 512 + 512], s0, s1, ready[i], fr,
                                       inc=s1)
                        v = x_sb[:, tb, c * 512:c * 512 + 512]
                        xt[tb, c] = tt(v, v, PS[:, b, :], ALU.add, t, xt[tb, c])
                        g.banks.give(b, xt[tb, c])
                        for i in pairs:
                            tYH[i % 2] = tST[i % 4] = t
                        yield

            for _ in gather(0):
                pass
            gate(0)
            up_(0)
            yo, co = [], iter(())
            ga = gather(1)
            next(ga)
            for e in range(NE):
                if e + 1 < NE:
                    gate(e + 1)
                next(co, None)
                if e % 2 == 0 and e:
                    next(ga, None)
                th = act_fold(e)
                next(co, None)
                if e + 1 < NE:
                    up_(e + 1)
                if e % 2 == 0:
                    next(ga, None)
                next(co, None)
                yo += down(e, th)
                next(ga, None)
                next(co, None)
                if e % 2 == 0:
                    for _ in ga:
                        pass
                    ga = gather(e // 2 + 2)
                    next(ga, None)
                else:
                    i = e // 2
                    assert next(co, 0) == 0
                    weighted(i, yo)
                    yo = []
                    if i >= NP - 2:
                        co = combine([i])
                    elif i % 2:
                        co = combine([i - 1, i])
            for _ in co:
                pass
            return [[xt[tb, 0], xt[tb, 1]] for tb in range(NB)], [tXG, tGS, tHT, tYH, tST, tS, tY]

        t_moe, t_exp = experts(mst, [t_rt, t_hs, t_hT2, t_hn], t_rkm, t_we, t_x2, t_S0)

        main, main_banks = (g.pe, g.act, g.dve, g.pool, g.sp), g.banks
        lsems = []

        def lsem(n):
            s = sem(n)
            lsems.append(s)
            return s

        loop = tuple(Eng(lsem("l_" + n)) for n in engs)
        g.pe, g.act, g.dve, g.pool, g.sp = loop
        g.banks = Banks()
        lw = [[lsem(f"l_w{i}"), 0] for i in range(5)]
        keep = (t_c, t_c0, t_hs)
        t_c = t_c0 = t_hs = None
        lst = Stream(g, make_plan_moe(I), lw, mraw, mhi, mlo, 0.4375)
        experts(lst, None, ts(rkm, rkm, -float(WIN), None, ALU.add, None), None, [None] * NB)
        t_c, t_c0, t_hs = keep
        bar = [sem(f"bar{i}") for i in range(4)]
        for q, lq, n in zip(main, loop, engs):
            q.items.append(("loop", q.waits([t_P]), lq.items, n))
        g.pe, g.act, g.dve, g.pool, g.sp = main
        g.banks = main_banks

        st = Stream(g, wplan3, wslots, raw, hi, lo, 0.0, [mst.raw_end(i) for i in (2, 3, 4, 0)],
                    [mst.hl_end(0), mst.hl_end(1)])
        st.load_to(4)
        s_small = [mst.raw_end(1), t_lg, t_r]
        s_b = slot("s_b")
        FNB = at("FNB", 128, [128, D])

        def ffn(st, pre, wcol, x_done, xs_at, xs_read, old, order):
            xs = at("xs_" + pre, xs_at, [128, NB, D])
            xh, xl = at("xh_" + pre, 48, [128, 8, T], F32R), at("xl_" + pre, 64, [128, 8, T], F32R)
            th, tl = at("th_" + pre, 80, [128, 11, T], F32R), at("tl_" + pre, 102, [128, 11, T], F32R)
            sg = [at(f"sg{i}_" + pre, 124 + 2 * i, [128, 512]) for i in range(4)]
            t_xT = norm_t(xs, wcol, xh, xl, x_done, xs_read, old, st, order)
            t_sg = [None] * 4
            t_dn = None
            xt = [None] * NB
            for half in range(2):
                t_h = {}
                for gi, (a0, b0) in enumerate(FCUTS):
                    nb = (b0 - a0) // 128
                    tg_ = {}

                    def ev_g(i, b, t):
                        tg_[i] = af(sg[i][:, :], PS[:, b, :], ACT.Silu, t, t_sg[i], old)
                        return tg_[i]

                    def ev_u(i, b, t):
                        m = tt(sg[i][:, :], sg[i][:, :], PS[:, b, :], ALU.mult, t, tg_[i])
                        f = a0 // 128 + i
                        x = hilo(th[:, f, :], tl[:, f, :], sg[i][:, :], m, t_dn, old)
                        t_sg[i] = x
                        t_h[f] = x
                        return m

                    dense(st, (pre, "g", half, gi), 2, "b", xh, xl, t_xT, nb, ev_g)
                    dense(st, (pre, "u", half, gi), 2, "b", xh, xl, t_xT, nb, ev_u)

                for c in range(2):
                    def ev_d(i, b, t):
                        v = x_sb[:, i, c * 512:c * 512 + 512]
                        a = stt(v, PS[:, b, :], 0.5, v, ALU.mult, ALU.add, t)
                        xt[i] = a
                        return a

                    t_dn = dense(st, (pre, "d", half, c), 3, "a", th, tl, t_h, 4, ev_d)
            return xt, [t_dn, t_sg]

        t_x4, t_f1 = ffn(st, "ffn1", f1c, t_moe, 32, t_exp, [t_exp, t_rkm, t_we], (0, 1, 2, 3))

        xs = at("xs2", 32, [128, NB, D])
        xh, xl = at("xh2", 48, [128, 8, T], F32R), at("xl2", 64, [128, 8, T], F32R)
        t_xT = norm_t(xs, mxc, xh, xl, t_x4, t_f1, t_f1, st)
        qn, kn, v2 = (at(n, 80 + 8 * i, [128, NB, 512]) for i, n in enumerate(("qn2", "kn2", "v2")))
        up = at("up", 104, [128, 4, 16 + T])
        q2T, k2T = at("q2T", 112.5, [128, 4, T]), at("k2T", 120.5, [128, 4, T])
        s2 = [at("s2a", 128.5, [128, 4, T]), at("s2b", 40, [128, 4, T])]
        P2 = [[at(f"P2{i}{k}", o, [128, 4, 128]) for k, o in enumerate(os)]
              for i, os in enumerate(((136.5, 138.5, 140.5, 24), (26, 28, 30, 92.25)))]
        Bt = at("Bt", 32, [128, 8, 256])
        QW = at("QW", 21, [128, 2, 64])
        QS2 = at("QS2", 21.5, [128, 64])
        S4 = at("S4", 21.75, [128, 32])
        PW = at("PW", 22, [128, 4, 128])
        g.pool.dma(lambda e: e.dma_start(QW[:, 0, :], I["q_norm_2"].partition_broadcast(128)[:, 0, :]), s_b, s_small)
        g.pool.dma(lambda e: e.dma_start(QW[:, 1, :], I["k_norm_2"].partition_broadcast(128)[:, 0, :]), s_b)
        g.pool.dma(lambda e: e.dma_start(PW[:, :, :], I["pool_w_2"][0].rearrange("g c d -> c g d")), s_b)
        t_b = (s_b[0], s_b[1])
        s_bt = slot("s_bt")
        t_bt = g.pool.dma(lambda e: e.dma_start(Bt[:, :, :], I["rel_tile"]), s_bt, t_xT)
        t_bt = tt(Bt[:, :, 128:256], Bt[:, :, 128:256], bc(cst("cmask"), 1, [128, 8, 128]), ALU.add, t_bt, on=pool)
        t_p = pool(lambda e: e.memset(up[:, :, 0:16], 0.0), t_f1)
        t_q2, t_k2, t_v2, t_u2 = [], [], [], []

        def ev_nat(dst, toks, f):
            def ev(i, b, t):
                a = f(dst[:, i, :], PS[:, b, :], t, t_f1)
                toks.append(a)
                return a
            return ev

        def ev_up(i, b, t):
            a = acp(up[:, i, 16:16 + T], PS[:, b, :], t, t_f1)
            t_u2.append(a)
            return a

        rawr = [nc.alloc_sbuf_tensor_at(f"rawr{i}", [128, 2048], F32R, offset=ring + i * 8 * KB) for i in range(4)]
        wst = None
        pTh, pTl = at("pTh", 48, [128, 4, T], F32R), at("pTl", 56, [128, 4, T], F32R)
        a2h, a2l = at("a2h", 64, [128, 4, T], F32R), at("a2l", 72, [128, 4, T], F32R)
        W0 = [at(f"PP{i}", 80 + 2.0625 * i, [128, 16 + T]) for i in range(2)]
        dd = [at(f"dd{i}", 84.25 + 2 * i, [128, T]) for i in range(4)]
        t_x3 = [[] for _ in range(NB)]
        t_a2 = [[] for _ in range(NB)]
        t_pool, t_at2 = [], []

        def wo_steps(tb):
            for c in range(2):
                fr = g.banks.hold(c)[1]
                for half in range(2):
                    u = 2 * c + half
                    for kk in range(4):
                        xa, xb = ((a2h, a2l), (pTh, pTl))[half]
                        xa, xb = xa[:, kk, tb * 128:tb * 128 + 128], xb[:, kk, tb * 128:tb * 128 + 128]
                        h, l = (w[u][:, kk * 512:kk * 512 + 512] for w in (whi, rawr))
                        s0, s1 = half + kk == 0, half == 1 and kk == 3
                        mm(PS[:, c, :], xa, h, s0, False, wst.sp[u], fr if s0 else None, t_pool if half else t_a2[tb])
                        mm(PS[:, c, :], xa, l, False, False)
                        t = mm(PS[:, c, :], xb, h, False, s1, inc=kk == 3)
                    wst.done(u, t)
                    if half:
                        v = x_sb[:, tb, c * 512:c * 512 + 512]
                        a = tt(v, v, PS[:, c, :], ALU.add, t)
                        t_x3[tb].append(a)
                        g.banks.give(c, a)
                    g.last = t
                    yield 1

        def qk_norm(w, src, tk):
            t_ss, qs = [], QS2[:, 32 * w:32 * w + 32]
            for i in range(NB):
                sv = s2[0][:, i, :]
                a = af(sv, src[:, i, :], ACT.Square, tk[i], t_sq[i], t_f1)
                t_sq[i] = red(qs[:, 8 * i:8 * i + 8], sv.rearrange("p (h d) -> p h d", h=8), ALU.add, a, t_b)
                t_ss.append(t_sq[i])
            t = ts(qs, qs, 1.0 / 64, EPS, ALU.mult, ALU.add, t_ss)
            t = af(qs, qs, ACT.Sqrt, t)
            t = rcp(qs, qs, t)
            t_n = []
            for i in range(NB):
                v = src[:, i, :].rearrange("p (h d) -> p h d", h=8)
                a = tt(v, v, bc(qs[:, 8 * i:8 * i + 8], 2, [128, 8, 64]), ALU.mult, t, tk)
                t_n.append(tt(v, v, bc(QW[:, w, :], 1, [128, 8, 64]), ALU.mult, a, t_b, on=pool if i % 2 else dve))
            return t_n

        def qk_turn(src, dst, t_n):
            for j in range(4):
                b, fr = g.banks.take()
                for i in range(NB):
                    t = tr(PS[:, b, i * 128:i * 128 + 128], src[:, i, j * 128:j * 128 + 128], t_n[i], fr, inc=i == 3)
                a = acp(dst[:, j, :], PS[:, b, :], t, t_f1)
                g.banks.give(b, a)
                t_qk.append(a)

        t_sq, t_qk = [None] * 4, []

        def mixer2():
            t_n = qk_norm(0, qn, t_q2)
            yield 6
            qk_turn(qn, q2T, t_n)
            yield 2
            t_n = qk_norm(1, kn, t_k2)
            yield 6
            qk_turn(kn, k2T, t_n)
            t_sf, t_pf = [[t_qk, t_sq], t_xT], [t_qk, t_qk]

            def scores(n):
                qb, j = 3 - n // 2, n % 2
                W = (qb + 1) * 128
                Wn = min(W, 256)
                Wf = W - Wn
                b, fr = g.banks.hold(4, 4)
                for hh in range(4):
                    h = 4 * j + hh
                    p0 = (h % 2) * 64
                    t = mm(PS[:, b + hh, 0:W], q2T[p0:p0 + 64, h // 2, qb * 128:qb * 128 + 128], k2T[p0:p0 + 64, h // 2, 0:W],
                           True, True, t_qk, fr, inc=hh == 3)
                s = s2[n % 2][:, :, 0:W]
                t1 = stt(s[:, :, Wf:W], PS[:, b:b + 4, Wf:W], 0.125, Bt[:, 4 * j:4 * j + 4, 256 - Wn:256], ALU.mult, ALU.add,
                         t, t_bt, t_sf[n % 2])
                t2 = None
                if Wf:
                    t2 = stt(s[:, :, 0:Wf], PS[:, b:b + 4, 0:Wf], 0.125, bc(bfar[:, 4 * j:4 * j + 4], 2, [128, 4, Wf]),
                             ALU.mult, ALU.add, t, t_sf[n % 2])
                g.banks.give(b, [t1, t2], 4)
                c = S4[:, 16 * (n % 2):16 * (n % 2) + 16]
                t3 = red(c[:, 0:4], s, ALU.max, t1, t2, t_b, t_sf[n % 2])
                t3 = ts(c[:, 4:8], c[:, 0:4], -1.0, None, ALU.mult, None, t3)
                te = [af(s[:, q, :], s[:, q, :], ACT.Exp, t3, t1, t2, bias=c[:, 4 + q:5 + q], acc=c[:, 8 + q:9 + q])
                      for q in range(4)]
                return n, qb, j, s, c, te, t

            def weights(sc):
                n, qb, j, s, c, te, _ = sc
                W = (qb + 1) * 128
                t = rcp(c[:, 12:16], c[:, 8:12], te)
                return [tt(s[:, q, :], s[:, q, :], c[:, 12 + q:13 + q].broadcast_to([128, W]), ALU.mult, t, te)
                        for q in range(4)]

            def turned(sc, t):
                n, qb, j, s, c, te, _ = sc
                ev = []
                for kb in range(qb + 1):
                    b, fr = g.banks.take()
                    for hh in range(4):
                        t2 = tr(PS[:, b, hh * 128:hh * 128 + 128], s[:, hh, kb * 128:kb * 128 + 128], t[hh], fr, inc=hh == 3)
                    a = acp(P2[n % 2][kb][:, :, :].rearrange("p h q -> p (h q)"), PS[:, b, :], t2, t_pf[n % 2])
                    g.banks.give(b, a)
                    ev.append(a)
                t_sf[n % 2] = ev
                return ev

            def values(sc, ev):
                n, qb, j, s, c, te, _ = sc
                b, fr = g.banks.take()
                for hh in range(4):
                    h = 4 * j + hh
                    o = PS[(h % 2) * 64:(h % 2) * 64 + 64, b, (hh // 2) * 128:(hh // 2) * 128 + 128]
                    for kb in range(qb + 1):
                        t = mm(o, v2[:, kb, h * 64:h * 64 + 64], P2[n % 2][kb][:, hh, :], kb == 0, kb == qb, ev, t_v2, fr,
                               inc=kb == qb)
                t_pf[n % 2] = t
                q = slice(qb * 128, qb * 128 + 128)
                a = hilo(a2h[:, 2 * j:2 * j + 2, q], a2l[:, 2 * j:2 * j + 2, q],
                         PS[:, b, 0:256].rearrange("p (c q) -> p c q", c=2), t, g.in2_end)
                g.banks.give(b, a)
                t_a2[qb].append(a)
                t_at2.extend([t, ev])

            sc, ev = {}, {}
            sc[0] = scores(0)
            yield 2
            z = [pool(lambda e, w=w: e.memset(w[:, 0:16], 0.0), t_qk) for w in W0]
            td, tc2 = [], None
            for gi in range(4):
                cur, t = up[:, gi, :], [t_u2, t_p]
                for k in range(gi + 1):
                    d = 1 << k
                    nx = W0[k % 2]
                    t = tt(nx[:, 16:16 + T], cur[:, 16:16 + T], cur[:, 16 - d:16 - d + T], ALU.add, t, z, tc2, on=pool)
                    cur = nx
                t2 = ts(dd[gi][:, :], cur[:, 16:16 + T], 1.0 / (2 << gi), None, ALU.mult, None, t, t_qk, on=pool)
                t2 = tt(dd[gi][:, 0:16], cur[:, 16:32], cst("rc16")[:, gi * 16:gi * 16 + 16], ALU.mult, t, t2, on=pool)
                tc2 = tt(dd[gi][:, :], dd[gi][:, :], up[:, gi, 16:16 + T], ALU.subtract, t2, on=pool)
                td.append(tc2)
            yield 2
            tw = weights(sc[0])
            sc[1] = scores(1)
            yield 2
            ev[0] = turned(sc[0], tw)
            tw = weights(sc[1])
            sc[2] = scores(2)
            yield 2
            ev[1] = turned(sc[1], tw)
            yield 100
            g.in2_end = g.last
            g.banks.span(2, 4)
            def pooled(gi):
                b, fr = g.banks.take()
                t = mm(PS[:, b, :], PW[:, gi, :], dd[gi][:, :], True, True, td[gi], t_b, fr, inc=True)
                h = af(pTh[:, gi, :], PS[:, b, :], ACT.Copy, t, g.in2_end, scale=psc[:, gi:gi + 1])
                l = stt(pTl[:, gi, :], PS[:, b, :], psc[:, gi:gi + 1], pTh[:, gi, :].bitcast(F32), ALU.mult, ALU.subtract, h,
                        g.in2_end)
                g.banks.give(b, [h, l])
                t_pool.append([h, l])

            pooled(0)
            pooled(1)
            tw = weights(sc[2])
            sc[3] = scores(3)
            values(sc[0], ev[0])
            values(sc[1], ev[1])
            pooled(2)
            pooled(3)
            split_out()
            wst.split_to(2)
            ev[2] = turned(sc[2], tw)
            wst.split_to(4)
            main2.append(wo_steps(3))
            yield 1
            for n in range(4, 10):
                if n - 1 < 8:
                    tw = weights(sc[n - 1])
                if n < 8:
                    sc[n] = scores(n)
                values(sc[n - 2], ev[n - 2])
                if n % 2:
                    main2.append(wo_steps(3 - (n - 2) // 2))
                yield 1
                if n - 1 < 8:
                    ev[n - 1] = turned(sc[n - 1], tw)
                yield 1
            g.sc_end = sc[7][6]

        def split_out():
            nonlocal wst
            wst = Stream(g, wplan4, wslots, raw, whi, rawr, 0.5, [st.raw_end(i) for i in range(4)],
                         [st.hl_end(i % 2) for i in range(4)])

        whi = hi + lo
        dense(st, ("in2", 0), 2, "a", xh, xl, t_xT, 4, ev_nat(qn, t_q2, cp))
        g.banks.span(4, 8)
        main2 = [dense_steps(st, ("in2", 1), 2, "a", xh, xl, t_xT, 4, ev_nat(kn, t_k2, acp)),
                 dense_steps(st, ("in2", 3), 2, "b", xh, xl, t_xT, 4, ev_up),
                 dense_steps(st, ("in2", 2), 2, "a", xh, xl, t_xT, 4, ev_nat(v2, t_v2, acp))]
        st.spread = True
        interleave(main2, mixer2())
        g.banks.span(0, 8)
        t_m2 = [t_at2, t_a2, t_pool, g.last, g.sc_end]
        st = Stream(g, wplan5, wslots, raw, hi, lo, 0.0, [wst.hl_end(i) for i in range(4)],
                    [[wst.hl_end(0), wst.hl_end(2)], [wst.hl_end(1), wst.hl_end(3)]])
        st.load_to(4)

        t_x5, t_f2 = ffn(st, "ffn2", f2c, t_x3, 112.5, g.sc_end, t_m2, (3, 2, 1, 0))

        t_fn = g.sp.dma(lambda e: e.dma_start(FNB[:, :], I["final_norm_2"].partition_broadcast(128)[:, 0, :]), s_late, t_f2)
        ot = at("ot", 32, [128, NB, D])
        s_o = slot("s_o")
        for tb, r in norm_steps(ot, t_x5, t_f2):
            t = stt(ot[:, tb, :], x_sb[:, tb, :], rs4[:, tb:tb + 1], FNB[:, :], ALU.mult, ALU.mult, r, t_fn)
            t = g.sp.dma(lambda e, tb=tb: e.dma_start(out[0, tb * 128:tb * 128 + 128, :], ot[:, tb, :]), s_o, t)
        g.sp.items.append(("wait", [t, (s_z[0][0], s_z[0][1]), (s_z[1][0], s_z[1][1])]))

        def play(e, items):
            for it in items:
                if it[0] == "op":
                    _, waits, fn, inc = it
                    for s, v in waits:
                        e.wait_ge(s, v)
                    ins = fn(e)
                    if inc:
                        ins.then_inc(*inc)
                elif it[0] == "wait":
                    for s, v in it[1]:
                        e.wait_ge(s, v)
                else:
                    _, waits, body, name = it
                    for s, v in waits:
                        e.wait_ge(s, v)
                    r = e.value_load(PI[0:1, 0:1], min_val=0, max_val=T // WIN)
                    with e.If(r > 1):
                        meet(e, name)
                        with e.Fori(1, r):
                            play(e, body)
                            meet(e, name)

        def meet(e, name):
            e.drain().then_inc(bar[0], 1)
            if name == "sp":
                e.wait_ge(bar[0], 5)
                for q in lsems:
                    e.sem_clear(q)
                e.sem_clear(bar[0])
                e.sem_inc(bar[1], 1)
                e.wait_ge(bar[2], 4)
                e.sem_clear(bar[1])
                e.sem_clear(bar[2])
            else:
                e.wait_ge(bar[1], 1)
                e.sem_inc(bar[2], 1)

        blk = ctx.enter_context(nc.Block())

        @blk.sync
        def _(e):
            play(e, g.sp.items)

        @blk.scalar
        def _(e):
            play(e, g.act.items)

        @blk.vector
        def _(e):
            play(e, g.dve.items)

        @blk.gpsimd
        def _(e):
            play(e, g.pool.items)

        @blk.tensor
        def _(e):
            play(e, g.pe.items)


def constants():
    import numpy as np
    p = np.arange(128)
    c = np.zeros((128, NC1), np.float32)

    def put(n, v):
        o, w = CW[n]
        c[:, o:o + w] = v

    put("ident", np.eye(128))
    put("ustrict", p[:, None] < p[None, :])
    put("ones", 1.0)
    put("fold", (p[:, None] % 64) == np.arange(64)[None, :])
    put("iota", 1 + np.arange(WIN)[None, :])
    put("cmask", np.where((p[:, None] < 64) & (p[None, :] >= 64), NEG, 0.0))
    put("rc16", np.concatenate([1.0 / np.minimum(np.arange(16) + 1, 2 << i) for i in range(4)])[None, :])
    put("e64", WIN * np.arange(32)[None, :])
    put("step8", (WIN * np.arange(8))[None, :])
    put("dec8", (8 - np.arange(8))[None, :])
    put("invf", (np.float32(500000.0) ** (-np.arange(0, 16, 2, dtype=np.float32) / np.float32(16)))[None, :])
    m1 = np.zeros((128, NC2), np.float32)
    k = np.arange(256)[None, :]
    m1[:, 0:256] = np.where((k <= p[:, None] + 128) & (p[:, None] + 128 - k < 128), 0.0, NEG)
    m1[:, 256:768] = (np.arange(512) % 128 != 0)[None, :]
    mk = np.zeros((128, 8, 128), np.uint32)
    s, t = p[:, None], p[None, :]
    for lv in range(7):
        h = 64 >> lv
        mk[:, lv, :] = (s // (2 * h) == t // (2 * h)) & (s // h % 2 == 0) & (t // h % 2 == 1)
    mk[:, 7, :] = s == t
    return c, m1, mk.reshape(128, NMASK)


NAMES = ["x", "w_in", "hgrn_norm_w", "w_branch_attn", "w_branch_hgrn", "w_out", "norm2_w", "w_gate_experts",
         "w_up_experts", "w_down_experts", "ffn1_w_gate_2", "ffn1_w_up_2", "ffn1_w_down_2", "w_in_2", "q_norm_2", "k_norm_2",
         "pool_w_2", "w_out_2", "ffn2_w_gate_2", "ffn2_w_up_2", "ffn2_w_down_2", "final_norm_2"]


def kernel(**inputs):
    import numpy as np
    import concourse.bacc as bacc
    from concourse.bass_utils import run_bass_kernel_spmd as run

    arrays = {n: np.ascontiguousarray(inputs[n]) for n in NAMES}
    rb = np.ascontiguousarray(inputs["rel_bias_2"])[0]
    rev = np.concatenate([np.repeat(rb[:, 256:257], 127, axis=1), rb[:, 256:0:-1]], axis=1)
    arrays["rel_tile"] = np.ascontiguousarray(np.stack([rev[:, 127 - q:383 - q] for q in range(128)]))
    def cols(n):
        a = np.ascontiguousarray(inputs[n])
        return a.reshape(a.shape[0], -1, 128).transpose(2, 0, 1).reshape(128, -1)

    def rows(a):
        return np.broadcast_to(a.reshape(1, -1), (128, a.size))

    arrays["c_par"] = np.ascontiguousarray(np.concatenate(
        [cols(n) for n in ("norm1_w", "norm2_w", "ffn1_norm_2", "mix_norm_2", "ffn2_norm_2", "pool_scale_2",
                           "hgrn_lower_bounds")]
        + [rows(np.ascontiguousarray(inputs["attn_sinks"])), rows(rb[:, 256])], axis=1))
    arrays["positions"] = np.ascontiguousarray(np.ascontiguousarray(inputs["positions"]).reshape(NB, 128).T)
    arrays["qk_norm"] = np.concatenate([np.ascontiguousarray(inputs["q_norm_w"])] * 8
                                       + [np.ascontiguousarray(inputs["k_norm_w"])] * 2, axis=1)
    wr = np.concatenate([np.ascontiguousarray(inputs["w_router_group"])[0],
                         np.ascontiguousarray(inputs["w_router_expert"])[0]], axis=1)
    arrays["w_router"] = np.ascontiguousarray(wr.reshape(8, 128, 36).transpose(1, 0, 2))
    arrays["b_router"] = np.concatenate([np.ascontiguousarray(inputs["b_router_group"]),
                                         np.ascontiguousarray(inputs["b_router_expert"])], axis=1)
    arrays["c_f32"], arrays["c_m1"], arrays["c_mask"] = constants()
    nc = bacc.Bacc("TRN2", target_bir_lowering=False, num_devices=1)
    I = {n: nc.dram_tensor("in_" + n, a.shape, mybir.dt.from_np(a.dtype), kind="ExternalInput").ap()
         for n, a in arrays.items()}
    out = nc.dram_tensor("out_0", (1, T, D), F32, kind="ExternalOutput").ap()
    program(nc, I, out)
    r = run(nc, [{"in_" + n: a for n, a in arrays.items()}], core_ids=[0])
    return r.results[0]["out_0"]
```
